# Optimizing a Trainium2 kernel written in Bass

```python
import math
import jax, jax.numpy as jnp
from jax import lax
import numpy as np
import jax
import jax.numpy as jnp

D_MODEL = 1024
BATCH = 1
SEQ = 256
DEPTH = 1

MEM_LEN = 256
MLA_NOPE = 128
MLA_ROPE = 64
MLA_V = 128
MLA_HEADS = D_MODEL // MLA_V
MLA_KV_RANK = 256
GLA_HEADS = 4
GLA_DK = D_MODEL // 2 // GLA_HEADS
GLA_DV = D_MODEL // GLA_HEADS
GLA_GATE_RANK = 16
GLA_GATE_NORMALIZER = 16.0
GLA_CHUNK = 64
MEM_HEADS = 4
MEM_DQK = 64
MEM_DV = D_MODEL // MEM_HEADS
N_BRANCHES = 3
D_FF = 4 * D_MODEL
ATTN_BLOCK = 128
ROPE_THETA = 10000.0
EPS = 1e-6

IN_SPLITS = (
    MLA_HEADS * (MLA_NOPE + MLA_ROPE),
    MLA_KV_RANK,
    MLA_ROPE,
    GLA_HEADS * GLA_DK,
    GLA_HEADS * GLA_DK,
    GLA_HEADS * GLA_DV,
    GLA_GATE_RANK,
    GLA_HEADS * GLA_DV,
    MEM_HEADS * MEM_DQK,
    N_BRANCHES * D_MODEL,
)
D_IN = sum(IN_SPLITS)


def rms_norm(t, g):
    tf = t.astype(jnp.float32)
    y = tf * lax.rsqrt(jnp.mean(tf * tf, axis=-1, keepdims=True) + EPS)
    return (y * g.astype(jnp.float32)).astype(t.dtype)

def rope_tables(positions):
    inv = 1.0 / (ROPE_THETA ** (jnp.arange(0, MLA_ROPE, 2, dtype=jnp.float32) / MLA_ROPE))
    ang = positions.astype(jnp.float32)[..., None] * inv
    return jnp.cos(ang), jnp.sin(ang)

def apply_rope(t, cos, sin):
    tf = t.astype(jnp.float32)
    t1, t2 = jnp.split(tf, 2, axis=-1)
    c = cos[:, :, None, :]
    s = sin[:, :, None, :]
    return jnp.concatenate([t1 * c - t2 * s, t1 * s + t2 * c], axis=-1).astype(t.dtype)

def causal_block_attention(q, k, v, scale):
    B, S, H, D = q.shape
    Dv = v.shape[-1]
    nb = S // ATTN_BLOCK
    qb = q.reshape(B, nb, ATTN_BLOCK, H, D).transpose(1, 0, 3, 2, 4)
    kh = k.transpose(0, 2, 1, 3)
    vh = v.transpose(0, 2, 1, 3)
    kpos = jnp.arange(S)

    def one_block(args):
        qi, i = args
        s = jnp.einsum('bhqd,bhkd->bhqk', qi, kh).astype(jnp.float32) * scale
        qpos = i * ATTN_BLOCK + jnp.arange(ATTN_BLOCK)
        s = jnp.where(kpos[None, :] <= qpos[:, None], s, -1e30)
        p = jax.nn.softmax(s, axis=-1).astype(vh.dtype)
        return jnp.einsum('bhqk,bhkd->bhqd', p, vh)

    o = lax.map(one_block, (qb, jnp.arange(nb)))
    return o.transpose(1, 0, 3, 2, 4).reshape(B, S, H, Dv)

def gla_chunked(q, k, v, log_a):
    B, S, H, DK = q.shape
    DV = v.shape[-1]
    C = GLA_CHUNK
    nc = S // C

    def to_chunks(t):
        return t.astype(jnp.float32).reshape(B, nc, C, H, t.shape[-1]).transpose(1, 0, 3, 2, 4)

    qc, kc, vc = to_chunks(q), to_chunks(k), to_chunks(v)
    bc = jnp.cumsum(to_chunks(log_a), axis=3)
    mask = jnp.tril(jnp.ones((C, C), dtype=bool))[None, None, :, :, None]

    def step(state, inp):
        qi, ki, vi, bi = inp
        diff = bi[:, :, :, None, :] - bi[:, :, None, :, :]
        decay = jnp.where(mask, jnp.exp(jnp.where(mask, diff, 0.0)), 0.0)
        a = jnp.einsum('bhid,bhjd,bhijd->bhij', qi, ki, decay)
        o_intra = jnp.einsum('bhij,bhje->bhie', a, vi)
        o_inter = jnp.einsum('bhid,bhde->bhie', qi * jnp.exp(bi), state)
        b_last = bi[:, :, -1, :]
        k_dec = ki * jnp.exp(b_last[:, :, None, :] - bi)
        new_state = jnp.exp(b_last)[..., None] * state + jnp.einsum('bhjd,bhje->bhde', k_dec, vi)
        return new_state, o_intra + o_inter

    state0 = jnp.zeros((B, H, DK, DV), jnp.float32)
    _, o = lax.scan(step, state0, (qc, kc, vc, bc))
    return o.transpose(1, 0, 3, 2, 4).reshape(B, S, H, DV).astype(q.dtype)

def hybrid_layer(x, mem, cos, sin, g_mix, w_in, b_gate, g_ckv, w_ukv, g_q_nope, g_k_nope,
                 g_q_rope, g_k_rope, w_gla_gate, b_gla_gate, g_gla_out, g_mem, w_mem_kv,
                 g_q_mem, g_k_mem, w_o, g_ffn, w_up, w_down):
    B, S, _ = x.shape
    M = mem.shape[1]
    h = rms_norm(x, g_mix)
    proj = h @ w_in
    offsets = []
    acc = 0
    for n in IN_SPLITS[:-1]:
        acc += n
        offsets.append(acc)
    (q_mla, c_kv, k_rope, q_gla, k_gla, v_gla, a_gla, r_gla, q_mem,
     gate_logits) = jnp.split(proj, offsets, axis=-1)

    q_mla = q_mla.reshape(B, S, MLA_HEADS, MLA_NOPE + MLA_ROPE)
    q_nope = rms_norm(q_mla[..., :MLA_NOPE], g_q_nope)
    q_pe = apply_rope(rms_norm(q_mla[..., MLA_NOPE:], g_q_rope), cos, sin)
    kv = (rms_norm(c_kv, g_ckv) @ w_ukv).reshape(B, S, MLA_HEADS, MLA_NOPE + MLA_V)
    k_nope = rms_norm(kv[..., :MLA_NOPE], g_k_nope)
    v_mla = kv[..., MLA_NOPE:]
    k_pe = apply_rope(rms_norm(k_rope, g_k_rope)[:, :, None, :], cos, sin)
    q_full = jnp.concatenate([q_nope, q_pe], axis=-1)
    k_full = jnp.concatenate([k_nope, jnp.broadcast_to(k_pe, (B, S, MLA_HEADS, MLA_ROPE))], axis=-1)
    o_mla = causal_block_attention(q_full, k_full, v_mla,
                                   (MLA_NOPE + MLA_ROPE) ** -0.5).reshape(B, S, MLA_HEADS * MLA_V)

    qg = q_gla.reshape(B, S, GLA_HEADS, GLA_DK) * (GLA_DK ** -0.5)
    kg = k_gla.reshape(B, S, GLA_HEADS, GLA_DK)
    vg = v_gla.reshape(B, S, GLA_HEADS, GLA_DV)
    log_a = jax.nn.log_sigmoid((a_gla @ w_gla_gate + b_gla_gate).astype(jnp.float32)) / GLA_GATE_NORMALIZER
    log_a = log_a.reshape(B, S, GLA_HEADS, GLA_DK)
    og = gla_chunked(qg, kg, vg, log_a)
    o_gla = rms_norm(og, g_gla_out).reshape(B, S, GLA_HEADS * GLA_DV) * jax.nn.silu(r_gla)

    kv_m = rms_norm(mem, g_mem) @ w_mem_kv
    k_m = rms_norm(kv_m[..., :MEM_HEADS * MEM_DQK].reshape(B, M, MEM_HEADS, MEM_DQK), g_k_mem)
    v_m = kv_m[..., MEM_HEADS * MEM_DQK:].reshape(B, M, MEM_HEADS, MEM_DV)
    q_m = rms_norm(q_mem.reshape(B, S, MEM_HEADS, MEM_DQK), g_q_mem)
    s_m = jnp.einsum('bshd,bmhd->bhsm', q_m, k_m).astype(jnp.float32) * (MEM_DQK ** -0.5)
    p_m = jax.nn.softmax(s_m, axis=-1).astype(v_m.dtype)
    o_mem = jnp.einsum('bhsm,bmhd->bshd', p_m, v_m).reshape(B, S, MEM_HEADS * MEM_DV)

    gates = jax.nn.sigmoid(gate_logits + b_gate).reshape(B, S, N_BRANCHES, D_MODEL)
    y = gates[..., 0, :] * o_mla + gates[..., 1, :] * o_gla + gates[..., 2, :] * o_mem
    x = x + y @ w_o

    h2 = rms_norm(x, g_ffn)
    return x + jnp.square(jax.nn.relu(h2 @ w_up)) @ w_down

def first_inputs(seed: int = 0) -> dict:
    key = jax.random.key(seed)
    ks = jax.random.split(key, 24)
    L = DEPTH

    def w(k, shape, fan_in):
        return jax.random.normal(k, (L,) + shape, jnp.float32) * (fan_in ** -0.5)

    def gain(k, n):
        return 1.0 + 0.02 * jax.random.normal(k, (L, n), jnp.float32)

    def bias(k, n):
        return 0.01 * jax.random.normal(k, (L, n), jnp.float32)

    x = jax.random.normal(ks[0], (BATCH, SEQ, D_MODEL), jnp.float32)
    mem = jax.random.normal(ks[1], (BATCH, MEM_LEN, D_MODEL), jnp.float32)
    positions = (jax.random.randint(ks[2], (BATCH, 1), 0, 4096, dtype=jnp.int32)
                 + jnp.arange(SEQ, dtype=jnp.int32)[None, :])
    return {
        'x': x,
        'mem': mem,
        'positions': positions,
        'g_mix': gain(ks[3], D_MODEL),
        'w_in': w(ks[4], (D_MODEL, D_IN), D_MODEL),
        'b_gate': bias(ks[5], N_BRANCHES * D_MODEL),
        'g_ckv': gain(ks[6], MLA_KV_RANK),
        'w_ukv': w(ks[7], (MLA_KV_RANK, MLA_HEADS * (MLA_NOPE + MLA_V)), MLA_KV_RANK),
        'g_q_nope': gain(ks[8], MLA_NOPE),
        'g_k_nope': gain(ks[9], MLA_NOPE),
        'g_q_rope': gain(ks[10], MLA_ROPE),
        'g_k_rope': gain(ks[11], MLA_ROPE),
        'w_gla_gate': w(ks[12], (GLA_GATE_RANK, GLA_HEADS * GLA_DK), GLA_GATE_RANK),
        'b_gla_gate': bias(ks[13], GLA_HEADS * GLA_DK),
        'g_gla_out': gain(ks[14], GLA_DV),
        'g_mem': gain(ks[15], D_MODEL),
        'w_mem_kv': w(ks[16], (D_MODEL, MEM_HEADS * (MEM_DQK + MEM_DV)), D_MODEL),
        'g_q_mem': gain(ks[17], MEM_DQK),
        'g_k_mem': gain(ks[18], MEM_DQK),
        'w_o': w(ks[19], (D_MODEL, D_MODEL), D_MODEL),
        'g_ffn': gain(ks[20], D_MODEL),
        'w_up': w(ks[21], (D_MODEL, D_FF), D_MODEL),
        'w_down': w(ks[22], (D_FF, D_MODEL), D_FF),
    }

def first_block(x, mem, positions, g_mix, w_in, b_gate, g_ckv, w_ukv, g_q_nope, g_k_nope,
              g_q_rope, g_k_rope, w_gla_gate, b_gla_gate, g_gla_out, g_mem, w_mem_kv,
              g_q_mem, g_k_mem, w_o, g_ffn, w_up, w_down):
    cos, sin = rope_tables(positions)
    for l in range(DEPTH):
        x = hybrid_layer(x, mem, cos, sin, g_mix[l], w_in[l], b_gate[l], g_ckv[l], w_ukv[l],
                         g_q_nope[l], g_k_nope[l], g_q_rope[l], g_k_rope[l], w_gla_gate[l],
                         b_gla_gate[l], g_gla_out[l], g_mem[l], w_mem_kv[l], g_q_mem[l],
                         g_k_mem[l], w_o[l], g_ffn[l], w_up[l], w_down[l])
    return x


GRID_W = 64
CTX_LEN = 256
HEAD_DIM = 64
A_HEADS = 8
A_KV_HEADS = 2
A_GROUPS = A_HEADS // A_KV_HEADS
B_HEADS = 8
B_KV_HEADS = 2
B_GROUPS = B_HEADS // B_KV_HEADS
WINDOW = 128
BLOCK = 128
D_FF_2 = 2816
CONV_WIDTH = 3
LN_EPS = 1e-5
QK_EPS = 1e-6
N_MOD = 6
DEEPNORM_ALPHA = (2.0 * DEPTH) ** 0.25
DEEPNORM_BETA = (8.0 * DEPTH) ** -0.25

OFF_QA = 0
OFF_KA = OFF_QA + A_HEADS * HEAD_DIM
OFF_VA = OFF_KA + A_KV_HEADS * HEAD_DIM
OFF_QB = OFF_VA + A_KV_HEADS * HEAD_DIM
OFF_KB = OFF_QB + B_HEADS * HEAD_DIM
OFF_VB = OFF_KB + B_KV_HEADS * HEAD_DIM
OFF_GA = OFF_VB + B_KV_HEADS * HEAD_DIM
OFF_GB = OFF_GA + D_MODEL
IN_COLS = OFF_GB + D_MODEL


def _layer_norm(x, g, b):
    xf = x.astype(jnp.float32)
    mu = jnp.mean(xf, axis=-1, keepdims=True)
    var = jnp.mean(jnp.square(xf - mu), axis=-1, keepdims=True)
    return ((xf - mu) * lax.rsqrt(var + LN_EPS) * g + b).astype(x.dtype)

def _qk_rms(t, g):
    tf = t.astype(jnp.float32)
    return (tf * lax.rsqrt(jnp.mean(tf * tf, axis=-1, keepdims=True) + QK_EPS) * g).astype(t.dtype)

def _axial_rope_tables(n_tok, dtype):
    pos = jnp.arange(n_tok, dtype=jnp.int32)
    rows = (pos // GRID_W).astype(jnp.float32)
    cols = (pos % GRID_W).astype(jnp.float32)
    n_freq = HEAD_DIM // 4
    inv_freq = ROPE_THETA ** (-jnp.arange(n_freq, dtype=jnp.float32) / n_freq)
    ang_r = rows[:, None, None] * inv_freq
    ang_c = cols[:, None, None] * inv_freq
    return (jnp.cos(ang_r).astype(dtype), jnp.sin(ang_r).astype(dtype),
            jnp.cos(ang_c).astype(dtype), jnp.sin(ang_c).astype(dtype))

def _rotate_half(t, cos, sin):
    t1, t2 = jnp.split(t, 2, axis=-1)
    return jnp.concatenate([t1 * cos - t2 * sin, t2 * cos + t1 * sin], axis=-1)

def _rope_2d(t, tables):
    cos_r, sin_r, cos_c, sin_c = tables
    t_row, t_col = jnp.split(t, 2, axis=-1)
    return jnp.concatenate([_rotate_half(t_row, cos_r, sin_r), _rotate_half(t_col, cos_c, sin_c)], axis=-1)

def _gqa_scores(q, k):
    return jnp.einsum("bqhgd,bkhd->bhgqk", q, k).astype(jnp.float32) * (HEAD_DIM ** -0.5)

def _gqa_values(p, v):
    return jnp.einsum("bhgqk,bkhd->bqhgd", p.astype(v.dtype), v)

def _sink_softmax(scores, sink):
    sink = sink.astype(jnp.float32)[:, :, None, None]
    m = jnp.maximum(jnp.max(scores, axis=-1, keepdims=True), sink)
    e = jnp.exp(scores - m)
    return e / (jnp.sum(e, axis=-1, keepdims=True) + jnp.exp(sink - m))

def _windowed_attention(q, k, v, k_ctx, v_ctx, sink):
    bsz, n_tok = q.shape[:2]
    pad = ((0, 0), (BLOCK, BLOCK), (0, 0), (0, 0))
    k_pad = jnp.pad(k, pad)
    v_pad = jnp.pad(v, pad)
    ctx_mask = jnp.ones((BLOCK, k_ctx.shape[1]), dtype=bool)

    def one_block(i):
        start = i * BLOCK
        q_blk = lax.dynamic_slice_in_dim(q, start, BLOCK, axis=1)
        k_blk = jnp.concatenate([lax.dynamic_slice_in_dim(k_pad, start, 3 * BLOCK, axis=1), k_ctx], axis=1)
        v_blk = jnp.concatenate([lax.dynamic_slice_in_dim(v_pad, start, 3 * BLOCK, axis=1), v_ctx], axis=1)
        q_pos = start + jnp.arange(BLOCK)
        k_pos = start - BLOCK + jnp.arange(3 * BLOCK)
        band = ((jnp.abs(q_pos[:, None] - k_pos[None, :]) <= WINDOW)
                & (k_pos[None, :] >= 0) & (k_pos[None, :] < n_tok))
        mask = jnp.concatenate([band, ctx_mask], axis=1)
        scores = jnp.where(mask, _gqa_scores(q_blk, k_blk), -jnp.inf)
        return _gqa_values(_sink_softmax(scores, sink), v_blk)

    out = lax.map(one_block, jnp.arange(n_tok // BLOCK))
    return jnp.moveaxis(out, 0, 1).reshape(bsz, n_tok, -1)

def _global_attention(q, k_all, v_all):
    bsz, n_tok = q.shape[:2]

    def one_block(i):
        q_blk = lax.dynamic_slice_in_dim(q, i * BLOCK, BLOCK, axis=1)
        p = jax.nn.softmax(_gqa_scores(q_blk, k_all), axis=-1)
        return _gqa_values(p, v_all)

    out = lax.map(one_block, jnp.arange(n_tok // BLOCK))
    return jnp.moveaxis(out, 0, 1).reshape(bsz, n_tok, -1)

def _merge_branches(o_a, o_b, gate_logits, w_branch_a, w_branch_b, w_out):
    g_a, g_b = jnp.split(jax.nn.sigmoid(gate_logits), 2, axis=-1)
    return (g_a * (o_a @ w_branch_a) + g_b * (o_b @ w_branch_b)) @ w_out

def _context_kv(h_c, w_in, b_in, k_norm_g):
    bsz, n_ctx, _ = h_c.shape
    kv_a = (h_c @ w_in[:, OFF_KA:OFF_QB] + b_in[OFF_KA:OFF_QB]).reshape(bsz, n_ctx, 2 * A_KV_HEADS, HEAD_DIM)
    kv_b = (h_c @ w_in[:, OFF_KB:OFF_GA] + b_in[OFF_KB:OFF_GA]).reshape(bsz, n_ctx, 2 * B_KV_HEADS, HEAD_DIM)
    k_a, v_a = jnp.split(kv_a, 2, axis=2)
    k_b, v_b = jnp.split(kv_b, 2, axis=2)
    return (k_a, v_a, _qk_rms(k_b, k_norm_g), v_b)

def _latent_token_mixer(h, kv_ctx, w_in, b_in, sink, q_norm_g, k_norm_g,
                        w_branch_a, w_branch_b, w_out, rope):
    bsz, n_tok, _ = h.shape
    k_a_c, v_a_c, k_b_c, v_b_c = kv_ctx
    proj = h @ w_in + b_in

    def heads(lo, hi, n):
        return proj[..., lo:hi].reshape(bsz, n_tok, n, HEAD_DIM)

    q_a = _rope_2d(heads(OFF_QA, OFF_KA, A_HEADS), rope).reshape(bsz, n_tok, A_KV_HEADS, A_GROUPS, HEAD_DIM)
    k_a = _rope_2d(heads(OFF_KA, OFF_VA, A_KV_HEADS), rope)
    v_a = heads(OFF_VA, OFF_QB, A_KV_HEADS)
    q_b = _rope_2d(_qk_rms(heads(OFF_QB, OFF_KB, B_HEADS), q_norm_g), rope).reshape(
        bsz, n_tok, B_KV_HEADS, B_GROUPS, HEAD_DIM)
    k_b = _rope_2d(_qk_rms(heads(OFF_KB, OFF_VB, B_KV_HEADS), k_norm_g), rope)
    v_b = heads(OFF_VB, OFF_GA, B_KV_HEADS)
    o_a = _windowed_attention(q_a, k_a, v_a, k_a_c, v_a_c, sink.reshape(A_KV_HEADS, A_GROUPS))
    o_b = _global_attention(q_b, jnp.concatenate([k_b, k_b_c], axis=1), jnp.concatenate([v_b, v_b_c], axis=1))
    return _merge_branches(o_a, o_b, proj[..., OFF_GA:], w_branch_a, w_branch_b, w_out)

def _context_token_mixer(h_c, kv_ctx, w_in, b_in, sink, q_norm_g, w_branch_a, w_branch_b, w_out):
    bsz, n_ctx, _ = h_c.shape
    k_a_c, v_a_c, k_b_c, v_b_c = kv_ctx
    q_a = (h_c @ w_in[:, OFF_QA:OFF_KA] + b_in[OFF_QA:OFF_KA]).reshape(bsz, n_ctx, A_KV_HEADS, A_GROUPS, HEAD_DIM)
    q_b = _qk_rms((h_c @ w_in[:, OFF_QB:OFF_KB] + b_in[OFF_QB:OFF_KB]).reshape(bsz, n_ctx, B_HEADS, HEAD_DIM),
                  q_norm_g).reshape(bsz, n_ctx, B_KV_HEADS, B_GROUPS, HEAD_DIM)
    gate_logits = h_c @ w_in[:, OFF_GA:] + b_in[OFF_GA:]
    o_a = _gqa_values(_sink_softmax(_gqa_scores(q_a, k_a_c), sink.reshape(A_KV_HEADS, A_GROUPS)), v_a_c)
    o_b = _gqa_values(jax.nn.softmax(_gqa_scores(q_b, k_b_c), axis=-1), v_b_c)
    return _merge_branches(o_a.reshape(bsz, n_ctx, -1), o_b.reshape(bsz, n_ctx, -1), gate_logits,
                           w_branch_a, w_branch_b, w_out)

def _conv_ffn(h, w_up, conv_w, conv_b, w_down):
    u = h @ w_up
    half = CONV_WIDTH // 2
    u = lax.conv_general_dilated(u, conv_w[:, None, :], window_strides=(1,), padding=((half, half),),
                                 dimension_numbers=("NWC", "WIO", "NWC"),
                                 feature_group_count=u.shape[-1]) + conv_b
    gate, val = jnp.split(u, 2, axis=-1)
    return (jax.nn.silu(gate) * val) @ w_down

def second_inputs(seed: int = 0) -> dict:
    key = jax.random.key(seed)
    ks = jax.random.split(key, 24)
    f32 = jnp.float32

    def normal(k, shape, scale):
        return jax.random.normal(k, shape, f32) * scale

    L = DEPTH
    return {
        "x": normal(ks[0], (BATCH, SEQ, D_MODEL), 1.0),
        "c": normal(ks[1], (BATCH, D_MODEL), 1.0),
        "ctx": normal(ks[2], (BATCH, CTX_LEN, D_MODEL), 1.0),
        "c_ctx": normal(ks[3], (D_MODEL,), 1.0),
        "w_mod": normal(ks[4], (L, D_MODEL, N_MOD * D_MODEL), 0.5 * D_MODEL ** -0.5),
        "b_mod": normal(ks[5], (L, N_MOD * D_MODEL), 0.02),
        "w_in": normal(ks[6], (L, D_MODEL, IN_COLS), D_MODEL ** -0.5),
        "b_in": normal(ks[7], (L, IN_COLS), 0.02),
        "attn_sink": normal(ks[8], (L, A_HEADS), 0.5),
        "q_norm_g": 1.0 + normal(ks[9], (L, HEAD_DIM), 0.05),
        "k_norm_g": 1.0 + normal(ks[10], (L, HEAD_DIM), 0.05),
        "w_branch_a": normal(ks[11], (L, A_HEADS * HEAD_DIM, D_MODEL), (A_HEADS * HEAD_DIM) ** -0.5),
        "w_branch_b": normal(ks[12], (L, B_HEADS * HEAD_DIM, D_MODEL), (B_HEADS * HEAD_DIM) ** -0.5),
        "w_out": normal(ks[13], (L, D_MODEL, D_MODEL), DEEPNORM_BETA * D_MODEL ** -0.5),
        "ln1_g": 1.0 + normal(ks[14], (L, D_MODEL), 0.05),
        "ln1_b": normal(ks[15], (L, D_MODEL), 0.02),
        "w_up": normal(ks[16], (L, D_MODEL, 2 * D_FF_2), D_MODEL ** -0.5),
        "conv_w": normal(ks[17], (L, CONV_WIDTH, 2 * D_FF_2), CONV_WIDTH ** -0.5),
        "conv_b": normal(ks[18], (L, 2 * D_FF_2), 0.02),
        "w_down": normal(ks[19], (L, D_FF_2, D_MODEL), DEEPNORM_BETA * D_FF_2 ** -0.5),
        "ln2_g": 1.0 + normal(ks[20], (L, D_MODEL), 0.05),
        "ln2_b": normal(ks[21], (L, D_MODEL), 0.02),
    }

def second_block(x, c, ctx, c_ctx, w_mod, b_mod, w_in, b_in, attn_sink, q_norm_g, k_norm_g,
              w_branch_a, w_branch_b, w_out, ln1_g, ln1_b, w_up, conv_w, conv_b, w_down,
              ln2_g, ln2_b):
    n_tok = x.shape[1]
    rope = _axial_rope_tables(n_tok, x.dtype)
    for l in range(DEPTH):
        last = l == DEPTH - 1
        mod = jax.nn.silu(c) @ w_mod[l] + b_mod[l]
        shift1, scale1, gate1, shift2, scale2, gate2 = jnp.split(mod[:, None, :], N_MOD, axis=-1)
        n_mod_c = 2 if last else N_MOD
        mod_c = jax.nn.silu(c_ctx) @ w_mod[l, :, :n_mod_c * D_MODEL] + b_mod[l, :n_mod_c * D_MODEL]
        mods_c = jnp.split(mod_c, n_mod_c)
        h_c = ctx * (1.0 + mods_c[1]) + mods_c[0]
        kv_ctx = _context_kv(h_c, w_in[l], b_in[l], k_norm_g[l])

        h = x * (1.0 + scale1) + shift1
        y = _latent_token_mixer(h, kv_ctx, w_in[l], b_in[l], attn_sink[l], q_norm_g[l], k_norm_g[l],
                                w_branch_a[l], w_branch_b[l], w_out[l], rope)
        x = _layer_norm(DEEPNORM_ALPHA * x + gate1 * y, ln1_g[l], ln1_b[l])

        h = x * (1.0 + scale2) + shift2
        y = _conv_ffn(h, w_up[l], conv_w[l], conv_b[l], w_down[l])
        x = _layer_norm(DEEPNORM_ALPHA * x + gate2 * y, ln2_g[l], ln2_b[l])

        if not last:
            y_c = _context_token_mixer(h_c, kv_ctx, w_in[l], b_in[l], attn_sink[l], q_norm_g[l],
                                       w_branch_a[l], w_branch_b[l], w_out[l])
            ctx = _layer_norm(DEEPNORM_ALPHA * ctx + mods_c[2] * y_c, ln1_g[l], ln1_b[l])
            h_c = ctx * (1.0 + mods_c[4]) + mods_c[3]
            y_c = _conv_ffn(h_c, w_up[l], conv_w[l], conv_b[l], w_down[l])
            ctx = _layer_norm(DEEPNORM_ALPHA * ctx + mods_c[5] * y_c, ln2_g[l], ln2_b[l])
    return x


def setup_inputs(seed=0):
    out = dict(first_inputs(seed))
    for name, value in second_inputs(seed + 1).items():
        if name != "x":
            out[name + "_2"] = value
    return out


def reference(
    x, mem, positions, g_mix, w_in, b_gate, g_ckv, w_ukv, g_q_nope, g_k_nope, g_q_rope,
    g_k_rope, w_gla_gate, b_gla_gate, g_gla_out, g_mem, w_mem_kv, g_q_mem, g_k_mem, w_o, g_ffn,
    w_up, w_down, c_2, ctx_2, c_ctx_2, w_mod_2, b_mod_2, w_in_2, b_in_2, attn_sink_2,
    q_norm_g_2, k_norm_g_2, w_branch_a_2, w_branch_b_2, w_out_2, ln1_g_2, ln1_b_2, w_up_2,
    conv_w_2, conv_b_2, w_down_2, ln2_g_2, ln2_b_2,
):
    x = first_block(
        x, mem, positions, g_mix, w_in, b_gate, g_ckv, w_ukv, g_q_nope, g_k_nope, g_q_rope,
        g_k_rope, w_gla_gate, b_gla_gate, g_gla_out, g_mem, w_mem_kv, g_q_mem, g_k_mem, w_o,
        g_ffn, w_up, w_down,
    )
    return second_block(
        x, c_2, ctx_2, c_ctx_2, w_mod_2, b_mod_2, w_in_2, b_in_2, attn_sink_2, q_norm_g_2,
        k_norm_g_2, w_branch_a_2, w_branch_b_2, w_out_2, ln1_g_2, ln1_b_2, w_up_2, conv_w_2,
        conv_b_2, w_down_2, ln2_g_2, ln2_b_2,
    )


_drawn_inputs = setup_inputs


def setup_inputs(seed=0):
    import zlib

    import numpy as np

    out = dict(_drawn_inputs(seed))
    spreads = {}
    factors = {'g_mix': 4.041,
     'b_gate': 8.0,
     'g_ckv': 8.0,
     'g_q_nope': 8.0,
     'g_k_nope': 8.0,
     'g_q_rope': 8.0,
     'g_k_rope': 8.0,
     'b_gla_gate': 8.0,
     'g_gla_out': 8.0,
     'g_mem': 8.0,
     'g_q_mem': 8.0,
     'g_k_mem': 8.0,
     'g_ffn': 3.334,
     'ctx_2': 8.0,
     'c_ctx_2': 6.141,
     'b_mod_2': 5.738,
     'b_in_2': 8.0,
     'attn_sink_2': 8.0,
     'q_norm_g_2': 8.0,
     'k_norm_g_2': 8.0,
     'w_branch_b_2': 2.958,
     'ln1_b_2': 2.876,
     'conv_b_2': 8.0,
     'ln2_b_2': 2.85}
    for name, (base, spread) in spreads.items():
        noise = np.random.default_rng([zlib.crc32(name.encode()), seed]).standard_normal(out[name].shape)
        drawn = base * np.exp(spread * noise) if base else spread * noise
        out[name] = jnp.asarray(drawn.astype(out[name].dtype))
    for name, factor in factors.items():
        out[name] = (out[name] * factor).astype(out[name].dtype)
    return out
```

```python
from contextlib import ExitStack

import numpy as np

import concourse.bass as bass
import concourse.mybir as mybir

F32 = mybir.dt.float32
F32R = mybir.dt.float32r
I32 = mybir.dt.int32
I8 = mybir.dt.int8
ALU = mybir.AluOpType
ACT = mybir.ActivationFunctionType
AX = mybir.AxisListType

P = 128
D = 1024
SEQ = 256
T = SEQ // P
KT = D // P
NEG = -1e30
EPS = 1e-6

H_MLA, NOPE, ROPE, V_MLA, KV_RANK = 8, 128, 64, 128, 256
H_GLA, DK_GLA, DV_GLA, GATE_RANK = 4, 128, 256, 16
H_MEM, DQ_MEM, DV_MEM = 4, 64, 256
D_FF = 4 * D
WIDTHS = dict(q=H_MLA * (NOPE + ROPE), ck=KV_RANK + ROPE, gq=H_GLA * DK_GLA, gk=H_GLA * DK_GLA,
              gv=H_GLA * DV_GLA, a=GATE_RANK, r=H_GLA * DV_GLA, qm=H_MEM * DQ_MEM, gates=3 * D)
COL = {}
for _name, _w in WIDTHS.items():
    COL[_name] = sum(WIDTHS[n] for n in list(WIDTHS)[:list(WIDTHS).index(_name)])
HEADS, KVH, HD = 8, 2, 64
GROUP = HEADS // KVH
FF2 = 2816
FT2 = FF2 // P
GRID_W = 64
ALPHA = 2.0 ** 0.25
LN_EPS = 1e-5

RING = 4
UNIT = 2
COLS = 512
AHEAD = 3


class Order:

    def __init__(self, eng, sem):
        self.eng, self.sem, self.n, self.i, self.per = eng, sem, 0, None, 0

    def done(self, ins):
        self.n += 1
        ins.then_inc(self.sem, 1)
        self.eng.wait_ge(self.sem, self.n if self.i is None else self.n + self.per * self.i)

    def enter(self, i, per):
        self.i, self.per, self.n0 = i, per, self.n

    def leave(self, times):
        assert self.n - self.n0 == self.per, (self.n - self.n0, self.per)
        self.n += self.per * (times - 1)
        self.i = None


def panels():
    out = [(f"MK{c}", KT, 1) for c in range(3)]
    out += [("AQ", KT, 2)]
    out += [(n, KT, 1) for n in ("GQ", "GK", "V0", "V1", "R0", "R1", "CK", "Q0", "Q1", "Q2")]
    out += [(f"UKV{c}", KV_RANK // P, 1) for c in range(4)]
    out += [(f"G{b}{c}", KT, 1) for b in (1, 2, 0) for c in range(2)]
    out += [("WO0", KT, 1), ("WO1", KT, 1), ("CX", KT, 2)]
    out += [(f"WU{c}", KT, 1) for c in range(D_FF // COLS)]
    out += [("WD0", D_FF // P, 1), ("WD1", D_FF // P, 1)]
    out += [(f"IN{c}", KT, 1) for c in range(7)]
    out += [("BA0", KT // 2, 1), ("BA1", KT // 2, 1), ("BB0", KT // 2, 1), ("BB1", KT // 2, 1)]
    out += [("OUT0", KT, 1), ("OUT1", KT, 1)]
    out += [(f"UP{c}", KT, 2) for c in range(FF2 // (COLS // 2))]
    out += [("DN0", FT2, 2), ("DN1", FT2, 2)]
    return out


NARROW = dict(MK0=H_MEM * DQ_MEM, AQ=GATE_RANK + H_MEM * DQ_MEM, CK=KV_RANK + ROPE)


class Plan:

    def __init__(self):
        self.no, self.unit, self.landed, self.cols = {}, {}, [], []
        loads = [0] * RING
        for i, (name, kts, per_unit) in enumerate(panels()):
            self.no[name], self.unit[name] = i, len(self.landed)
            for u in range(len(self.landed), len(self.landed) + kts // UNIT):
                loads[u % RING] += 16 * per_unit
                self.landed.append(loads[u % RING])
                self.cols.append(NARROW.get(name, COLS))
        self.units = len(self.landed)

    def bank(self, name):
        return self.no[name] % 2, self.no[name] // 2


PLAN = Plan()


def uses(names, banks=2):
    return {n: (i % banks, i // banks) for i, n in enumerate(names)}


def t_names():
    g = lambda n, k: [f"{n}.{i}" for i in range(k)]
    out = g("vec", 3) + g("me", 4) + ["mod.0"] + g("h", 4) + ["mod.1", "aT", "z.0", "z.1", "mod.2", "mod.3"]
    out += ["mqT", "mkT"] + attention_t("MEM", H_MEM, [f"mod.{4 + n}" for n in range(H_MEM)])
    out += g("gqT", 2) + g("gkT", 2) + [f"mod.{8 + n}" for n in range(4)] + g("go", 4)
    out += ["ck", "qn.0", "qn.1", "qn.2", "qn.3", "qr.0", "qr.1", "kp"] + g("kn", 4)
    out += attention_t("MLA", H_MLA)
    out += g("y", 4) + g("hc", 4) + g("h2", 4)
    out += [f"WU{c}.{i}" for c in range(8) for i in range(2)]
    out += g("x2", 4) + g("kA", 2) + g("qA", 2) + g("kB", 2) + g("qB", 2)
    out += attention_t("AB", 2 * HEADS * T)
    out += g("oab", 4) + g("ym", 4) + g("gate1", 2) + g("x3", 4)
    out += [f"UP{c}.{i}" for c in range(11) for i in range(2)]
    out += g("gate2", 2)
    return out


def attention_t(name, n, extra=()):
    out = []
    for i in range(n + 1):
        if i < n:
            out.append(f"{name}.PT{i}")
        if i >= 1:
            out.append(f"{name}.O{i - 1}")
        out += extra[i:i + 1]
    return out


T_USE = uses(t_names())
S_USE = uses([f"MEM.{i}" for i in range(H_MEM)] + ["gla.0.0", "gla.0.1", "gla.off"]
             + [f"gla.{s}.{t}" for s in range(1, 8) for t in range(T)]
             + [f"MLA.{i}" for i in range(H_MLA)] + [f"AB.{i}" for i in range(2 * HEADS * T)])
LT_ORDER = ["me", "h", "y", "hc", "h2", "x2", "oab", "ym", "x3"]


def hybrid_kernel(nc, a, out):
    ctx = ExitStack()
    with ctx:
        def sem(name):
            return ctx.enter_context(nc.semaphore(name))

        def sb(name, shape, dt=F32, scope=ctx):
            return scope.enter_context(nc.sbuf_tensor(name, shape, dt))

        acc = [ctx.enter_context(nc.psum_tensor(f"acc{i}", [P, T, COLS], F32)) for i in range(2)]
        tb = [ctx.enter_context(nc.psum_tensor(f"turned{i}", [P, COLS], F32)) for i in range(2)]
        sc = [ctx.enter_context(nc.psum_tensor(f"scores{i}", [P, COLS], F32)) for i in range(2)]

        raw = sb("raw", [P, RING, UNIT, COLS])
        whi = sb("whi", [P, RING, UNIT, COLS], F32R)
        wlo = sb("wlo", [P, RING, UNIT, COLS], F32R)
        x = sb("x_res", [P, T, D])
        lta = [sb(f"lta_{n}", [P, KT, SEQ], F32R) for n in ("hi", "lo")]
        ident = sb("ident", [P, P])
        ones = sb("ones", [P, P])
        keep_past = sb("keep_past", [P, P])
        keep_next = sb("keep_next", [P, P])
        vcol = sb("vcol", [P, 96])
        ccol = sb("ccol", [P, 4, 2 * FT2])
        modc = sb("modc", [P, 48])
        modx = sb("modx", [P, 16])
        sic = sb("sic", [P, 16])
        rot = sb("rot", [P, 3, T, 64])
        bias = sb("bias", [P, 2, COLS])
        turn = sb("turn", [P, 2, COLS])
        prob = sb("prob", [P, 2, COLS])
        probT = sb("probT", [P, 2, COLS])
        work = sb("work", [P, T, D])
        stat = sb("stat", [P, 8, 16])
        soft = sb("soft", [P, 2, 10])
        gains = sb("gains", [P, 6 * 64 + DV_GLA + HEADS])

        ROWS, at = {}, 0
        for name, n in (("g_mix", 8), ("g_mem", 8), ("g_ffn", 8), ("g_ckv", 2), ("c_2", 8), ("c_ctx_2", 8),
                        ("g_q_nope", 1), ("g_k_nope", 1), ("b_gla_gate", 4), ("b_mod_2", 48)):
            ROWS[name] = (at, n)
            at += n
        assert at == 96

        def col(name, k=0, n=1):
            return vcol[:, ROWS[name][0] + k:ROWS[name][0] + k + n]

        GAIN, at = {}, 0
        for name, n in (("g_q_rope", 64), ("g_k_rope", 64), ("g_q_mem", 64), ("g_k_mem", 64), ("q_norm_g_2", 64),
                        ("k_norm_g_2", 64), ("g_gla_out", DV_GLA), ("attn_sink_2", HEADS)):
            GAIN[name] = gains[:, at:at + n]
            at += n

        one = ExitStack()
        arena = sb("arena", [P, 20736], F32, one)
        wm = sb("wm", [P, 2, UNIT, COLS], F32, one)
        macc = sb("macc", [P, 2, COLS], F32, one)
        ckT = [sb(f"ckT_{n}", [P, 2, SEQ], F32R, one) for n in ("hi", "lo")]
        gmask = sb("gmask", [P, 7, P], I8, one)
        one.close()

        def ar(at, *shape):
            v = arena[:, at:at + int(np.prod(shape))]
            if len(shape) == 1:
                return v
            names = "abcd"[:len(shape)]
            return v.rearrange(f"p ({' '.join(names)}) -> p {' '.join(names)}", **dict(zip(names, shape)))

        o_mem = ar(0, T, D)
        r_gla = ar(2048, T, D)
        o_mla = ar(4096, T, D)
        gqT, gkT = ar(4096, H_GLA, SEQ), ar(5120, H_GLA, SEQ)
        mqT, mkT = ar(4096, 2, SEQ), ar(4608, 2, SEQ)
        stage = ar(6144, 2, T, COLS)
        decay = ar(6144, H_GLA, SEQ)
        eq, ek = ar(7168, 512), ar(7680, 512)
        rsig = ar(5120, T, COLS)
        angle, turns = ar(15360, T, 64), ar(15488, T, 64)
        q = ar(8192, T, 1536)
        kvm = ar(8192, T, 1280)
        kv = ar(11264, T, 2048)
        memx = ar(11264, T, D)
        attn = ar(11264, 3, H_GLA, P)
        og = ar(6144, T, H_GLA, DV_GLA)
        zb, ze = ar(11264, H_GLA, SEQ), ar(12288, H_GLA, SEQ)
        zflag = ar(13312, H_GLA * T, P)
        wg, aT = ar(14336, 512), ar(14848, SEQ)
        ck = ar(15360, T, 320)
        aq = ar(16000, T, 272)
        gv = ar(16544, T, D)
        gq, gk = ar(18592, T, 512), ar(19616, T, 512)
        gqd, gkd = ar(18592, H_GLA, SEQ), ar(19616, H_GLA, SEQ)
        qnT, knT = ar(15360, H_MLA, SEQ), ar(17408, H_MLA, SEQ)
        qrT, kpT = ar(19456, H_MLA // 2, SEQ), ar(20480, SEQ)
        kpe = work[:, 0, 512:768].rearrange("p (t c) -> p t c", t=T)
        vrow = [ar(4096 + 128 * i, 128) for i in range(3)]

        ltb = [sb(f"ltb_{n}", [P, KT, SEQ], F32R) for n in ("hi", "lo")]
        kvx = sb("kvx", [P, T, COLS])
        two = ExitStack()
        ff = [sb(f"ff_{n}", [P, D_FF // P, SEQ], F32R, two) for n in ("hi", "lo")]
        up = sb("up", [P, 2, T, COLS], F32, two)
        two.close()
        three = ExitStack()
        qkv = sb("qkv", [P, T, 1536], F32, three)
        qT = [sb(f"qT_{b}", [P, HEADS // 2, SEQ], F32, three) for b in "ab"]
        kT = [sb(f"kT_{b}", [P, KVH, 2 * SEQ], F32, three) for b in "ab"]
        kdup = sb("kdup", [P, 4, T, KVH * 2 * HD], F32, three)
        gate2 = sb("gate2", [P, T, 2 * D], F32, three)
        oab = sb("oab", [P, T, D], F32, three)
        ym = sb("ym", [P, T, D], F32, three)
        three.close()
        four = ExitStack()
        diag = sb("diag", [P, 4, P], F32, four)
        lnrow = sb("lnrow", [P, 2, D], F32, four)
        actT = [sb(f"act_{n}", [P, FT2, SEQ], F32R, four) for n in ("hi", "lo")]
        upv = sb("upv", [P, 2, T, COLS], F32, four)
        conv = sb("conv", [P, 4, SEQ], F32, four)
        sig = sb("sig", [P, 2, SEQ], F32, four)
        tap = sb("tap", [P, 4, 4], F32, four)
        four.close()

        landed = [sem(f"weights_landed{i}") for i in range(RING)]
        hi_ready, split_ready, unit_used = sem("hi_ready"), sem("split_ready"), sem("unit_used")
        panel_out = [sem(f"panel_out{i}") for i in range(2)]
        t_full = [sem(f"turned_full{i}") for i in range(2)]
        t_free = [sem(f"turned_free{i}") for i in range(2)]
        s_full = [sem(f"scores_full{i}") for i in range(2)]
        s_free = [sem(f"scores_free{i}") for i in range(2)]
        lt_hi, lt_ready = sem("stationary_hi"), sem("stationary_ready")
        soft_ready = sem("maxima_ready")
        mod_landed = [sem(f"mod_landed{i}") for i in range(2)]
        mod_free, mod_sum = sem("mod_free"), sem("mod_sum")
        bias_landed = [sem(f"bias_landed{i}") for i in range(2)]
        bias_used = sem("bias_used")
        gate_sig, gate_used = sem("gate_sigmoid"), sem("gate_used")
        up_done, up_hi = sem("up_done"), sem("up_hi")
        conv_lin, conv_sig, conv_mul = sem("conv_lin"), sem("conv_sig"), sem("conv_mul")
        gla_exp, gla_in = sem("gla_exp"), sem("gla_in")
        act_order, dve_order, pool_order = sem("act_order"), sem("dve_order"), sem("pool_order")
        stored = sem("stored")
        once = {}

        def ev(name):
            if name not in once:
                once[name] = sem(name)
            return once[name]

        BIASED = ["G10", "G11", "G20", "G21", "G00", "G01", "CX"] + [f"IN{c}" for c in range(7)]
        STEPS = {"MEM": (0, H_MEM), "MLA": (H_MEM, H_MLA), "AB": (H_MEM + H_MLA, 2 * HEADS * T)}
        n_gate = {n: i for i, n in enumerate(BIASED)}

        def lt_done(name, g=3):
            return 4 * LT_ORDER.index(name) + g + 1

        block = ctx.enter_context(nc.Block())

        def rows(w, k):
            return w[k * UNIT * P:(k + 1) * UNIT * P, :].rearrange("(k p) n -> p k n", p=P)

        def loads_of(name, k):
            w, w2 = a["w_in"], a["w_in_2"]
            kind, c = name.rstrip("0123456789"), int("".join(ch for ch in name if ch.isdigit()) or 0)
            if kind == "MK":
                first, n = [(0, 256), (256, COLS), (256 + COLS, COLS)][c]
                return [(0, rows(a["w_mem_kv"], k)[:, :, first:first + n])]
            if kind == "AQ":
                return [(0, rows(w, k)[:, :, COL["a"]:COL["a"] + GATE_RANK]),
                        (GATE_RANK, rows(w, k)[:, :, COL["qm"]:COL["qm"] + 256])]
            if kind == "CX":
                return [(0, rows(w2, k)[:, :, 512:768]), (256, rows(w2, k)[:, :, 1280:1536])]
            if kind == "CK":
                return [(0, rows(w, k)[:, :, COL["ck"]:COL["ck"] + 320])]
            if kind == "G":
                first = COL["gates"] + (c // 10) * D + (c % 10) * COLS
                return [(0, rows(w, k)[:, :, first:first + COLS])]
            where = {"GQ": (w, COL["gq"]), "GK": (w, COL["gk"]), "V": (w, COL["gv"]), "R": (w, COL["r"]),
                     "Q": (w, COL["q"]), "UKV": (a["w_ukv"], 0), "WO": (a["w_o"], 0), "WU": (a["w_up"], 0),
                     "WD": (a["w_down"], 0), "IN": (w2, 0), "BA": (a["w_branch_a_2"], 0),
                     "BB": (a["w_branch_b_2"], 0), "OUT": (a["w_out_2"], 0)}
            src, first = where[kind]
            return [(0, rows(src, k)[:, :, first + c * COLS:first + (c + 1) * COLS])]

        def units_of(name):
            names = list(PLAN.unit)
            i = names.index(name)
            return (PLAN.unit[names[i + 1]] if i + 1 < len(names) else PLAN.units) - PLAN.unit[name]

        @block.sync
        def _(sp):
            sp.dma_start(memx, a["mem"].rearrange("(t p) d -> p t d", p=P)).then_inc(ev("mem_landed"), 16)
            sp.dma_start(x[:], a["x"].rearrange("(t p) d -> p t d", p=P)).then_inc(ev("x_landed"), 16)

            def panel(name):
                for k in range(units_of(name)):
                    u = PLAN.unit[name] + k
                    sp.wait_ge(split_ready, u + 1)
                    if name.startswith("DN"):
                        for kk in range(UNIT):
                            r = (UNIT * k + kk) * P
                            sp.dma_start(raw[:, u % RING, kk], a["w_down_2"][r:r + P, COLS * int(name[2]):][:, 0:COLS])\
                              .then_inc(landed[u % RING], 16)
                        continue
                    for first, src in loads_of(name, k):
                        sp.dma_start(raw[:, u % RING, :, first:first + src.shape[2]], src)\
                          .then_inc(landed[u % RING], 16)

            for name in PLAN.no:
                if name.startswith("WU"):
                    if name == "WU0":
                        u0 = PLAN.unit[name]
                        with sp.Fori(0, D_FF // COLS) as c:
                            for k in range(KT // UNIT):
                                sp.wait_ge(split_ready, u0 + k + 1 + 4 * c)
                                sp.dma_start(raw[:, (u0 + k) % RING],
                                             rows(a["w_up"], k)[:, :, bass.ds(COLS * c, COLS)])\
                                  .then_inc(landed[(u0 + k) % RING], 16)
                elif name.startswith("UP"):
                    if name == "UP0":
                        u0 = PLAN.unit[name]
                        with sp.Fori(0, FF2 // 256) as c:
                            for k in range(KT // UNIT):
                                sp.wait_ge(split_ready, u0 + k + 1 + 4 * c)
                                for e in range(2):
                                    sp.dma_start(raw[:, (u0 + k) % RING, :, 256 * e:256 * e + 256],
                                                 rows(a["w_up_2"], k)[:, :, bass.ds(FF2 * e + 256 * c, 256)])\
                                      .then_inc(landed[(u0 + k) % RING], 16)
                else:
                    panel(name)

            for t in range(T):
                sp.wait_ge(ev("y_ready"), t + 1)
                sp.dma_start(out[t * P:(t + 1) * P, :], x[:, t, :]).then_inc(stored, 16)
            sp.wait_ge(stored, 16 * T)

        @block.gpsimd
        def _(pool):
            order = Order(pool, pool_order)
            pool.memset(ones[:], 1.0).then_inc(ev("ones_ready"), 1)
            for m, fill in ((ident, 0.0), (keep_past, 0.0), (keep_next, 0.0), (gmask, 0)):
                ins = pool.memset(m[:], fill)
            order.done(ins)
            pool.affine_select(out=ident[:], in_=ident[:], compare_op=ALU.not_equal, fill=1.0, base=0,
                               pattern=[[-1, P]], channel_multiplier=1).then_inc(ev("ident_ready"), 1)
            pool.affine_select(out=keep_past[:], in_=keep_past[:], compare_op=ALU.is_ge, fill=NEG, base=0,
                               pattern=[[-1, P]], channel_multiplier=1)
            pool.affine_select(out=keep_next[:], in_=keep_next[:], compare_op=ALU.is_ge, fill=NEG, base=0,
                               pattern=[[1, P]], channel_multiplier=-1).then_inc(ev("keeps_ready"), 1)
            freq = rot[:, 2, 0, :]
            for i in range(32):
                f = np.float32(1.0) / (np.float32(10000.0) ** np.float32(2 * i / np.float32(ROPE)))
                pool.memset(freq[:, i:i + 1], float(np.float32(f)))
            for i in range(16):
                f = np.float32(10000.0) ** (-np.float32(i) / np.float32(16))
                ins = pool.memset(freq[:, 32 + i:64:16], float(np.float32(f)))
            order.done(ins)
            for half in range(2):
                lane = slice(64 * half, 64 * half + 64)
                for t in range(T):
                    order.done(pool.memset(stat[lane, 7, t:t + 1], float(2 * t + half)))
                order.done(pool.iota(stat[lane, 7, 2:3].bitcast(I32), pattern=[[0, 1]], base=0, channel_multiplier=1))
            pool.sem_inc(ev("grid_ready"), 1)
            for n, s in enumerate((64, 32, 16, 8, 4, 2, 1)):
                odd = gmask[:, n, :].rearrange("p (m e w) -> p m e w", e=2, w=s)[:, :, 1, :]
                order.done(pool.memset(odd, 1))
                order.done(pool.affine_select(out=odd, in_=odd, compare_op=ALU.is_ge, fill=0.0, base=0,
                                              pattern=[[-2 * s, P // (2 * s)], [0, s]], channel_multiplier=1))
                ins = pool.affine_select(out=odd, in_=odd, compare_op=ALU.is_ge, fill=0.0, base=s - 1,
                                         pattern=[[2 * s, P // (2 * s)], [0, s]], channel_multiplier=-1)
                if n < 6:
                    order.done(ins)
            ins.then_inc(ev("gmask_ready"), 1)
            with pool.Fori(0, 12) as c:
                for k in range(KT // UNIT):
                    pool.wait_ge(mod_free, 4 * c + k + 1)
                    pool.dma_start(wm[:, k % 2], rows(a["w_mod_2"], k)[:, :, bass.ds(COLS * c, COLS)])\
                        .then_inc(mod_landed[k % 2], 16)
            for n, name in enumerate(BIASED):
                pool.wait_ge(bias_used, n + 1)
                if name == "CX":
                    for j, first in enumerate((512, 1280)):
                        pool.dma_start(bias[:, n % 2, 256 * j:256 * j + 256],
                                       a["b_in_2"][first:first + 256].partition_broadcast(P))\
                            .then_inc(bias_landed[n % 2], 16)
                    continue
                src = a["b_in_2"][int(name[2:]) * COLS:][:COLS] if name.startswith("IN") else \
                    a["b_gate"][int(name[1]) * D + int(name[2]) * COLS:][:COLS]
                pool.dma_start(bias[:, n % 2], src.partition_broadcast(P)).then_inc(bias_landed[n % 2], 16)
                if name == "G00":
                    b, k = T_USE["qr.1"]
                    pool.wait_ge(t_full[b], k + 1)
                    pool.dma_start(ar(8192, T, D), a["ctx_2"].rearrange("(t p) d -> p t d", p=P))\
                        .then_inc(ev("ctx_landed"), 16)
            b, k = T_USE["ym.3"]
            pool.wait_ge(t_full[b], k + 1)
            for i, name in enumerate(("ln1_g_2", "ln1_b_2")):
                pool.dma_start(lnrow[:, i], a[name].partition_broadcast(P)).then_inc(ev("ln1_landed"), 16)
            pool.wait_ge(ev("ln1_done"), 1)
            for i, name in enumerate(("ln2_g_2", "ln2_b_2")):
                pool.dma_start(lnrow[:, i], a[name].partition_broadcast(P)).then_inc(ev("ln2_landed"), 16)

        @block.tensor
        def _(pe):
            pe.sem_inc(unit_used, RING)

            def unit(name, k, lhs, n=COLS, first_kt=None, i=None, per=0):
                u, (s, cnt) = PLAN.unit[name] + k, PLAN.bank(name)
                du, dc = (per * i, per // 8 * i) if i is not None else (0, 0)
                kt0 = UNIT * k if first_kt is None else first_kt
                last = k == units_of(name) - 1
                if k == 0:
                    pe.wait_ge(panel_out[s], cnt + 1 + dc)
                pe.wait_ge(split_ready, RING + u + 1 + du)
                for t in range(T):
                    for kk in range(UNIT):
                        tok = slice(t * P, (t + 1) * P)
                        pairs = [(1, whi), (0, whi), (0, wlo)]
                        for j, (part, w) in enumerate(pairs):
                            ins = pe.matmul(acc[s][:, t, 0:n], lhs[part][:, kt0 + kk, tok], w[:, u % RING, kk, 0:n],
                                            start=(k == 0 and kk == 0 and j == 0),
                                            stop=(last and kk == UNIT - 1 and j == 2))
                ins.then_inc(unit_used, 1)

            def panel(name, lhs, n=COLS, **kw):
                for k in range(units_of(name)):
                    unit(name, k, lhs, n, **kw)

            def t_begin(name):
                b, k = T_USE[name]
                pe.wait_ge(t_free[b], k + 1)
                return tb[b], t_full[b]

            def turn_tokens(name, src, kts=KT):
                for g in range(kts // 2):
                    bank, full = t_begin(f"{name}.{g}" if kts > 2 else name)
                    for kk in range(2):
                        for t in range(T):
                            c = P * (2 * g + kk)
                            ins = pe.transpose(bank[:, 256 * kk + P * t:256 * kk + P * t + P],
                                               src[:, t, c:c + P], ident[:])
                    ins.then_inc(full, 1)

            def s_begin(name):
                b, k = S_USE[name]
                pe.wait_ge(s_free[b], k + 1)
                return sc[b], s_full[b]

            def attend(name, n, scores, blocks, values, fill_a=None, fill_b=None, after=None):
                def score(i):
                    bank, full = s_begin(f"{name}.{i}")
                    scores(i, bank).then_inc(full, 1)

                score(0)
                for i in range(n + 1):
                    if i + 1 < n:
                        score(i + 1)
                    if i < n:
                        if fill_a:
                            fill_a(i)
                        b, k = S_USE[f"{name}.{i}"]
                        pe.wait_ge(s_free[b], k + 2)
                        bank, full = t_begin(f"{name}.PT{i}")
                        for j in range(blocks):
                            ins = pe.transpose(bank[:, P * j:P * j + P],
                                               prob[:, (STEPS[name][0] + i) % 2, P * j:P * j + P], ident[:])
                        ins.then_inc(full, 1)
                        if fill_b:
                            fill_b(i)
                    if i >= 1:
                        b, k = T_USE[f"{name}.PT{i - 1}"]
                        pe.wait_ge(t_free[b], k + 2)
                        bank, full = t_begin(f"{name}.O{i - 1}")
                        values(i - 1, bank, probT[:, (STEPS[name][0] + i - 1) % 2, :]).then_inc(full, 1)
                    if after:
                        after(i)

            def mod_columns(c):
                bank, full = t_begin(f"mod.{c}")
                pe.wait_ge(mod_sum, c + 1)
                for part in range(2 if c < 4 else 1):
                    for j in range(4):
                        ins = pe.matmul(bank[:, 4 * part + j:4 * part + j + 1], macc[:, part, P * j:P * j + P],
                                        ones[:, 0:1], start=True, stop=True)
                ins.then_inc(full, 1)

            def lt_wait(name, g=3):
                pe.wait_ge(lt_ready, lt_done(name, g))

            pe.wait_ge(ev("ident_ready"), 1)
            pe.wait_ge(ev("rows_landed"), 16 * 14)
            for g, n in enumerate((96, 4 * FT2, 4 * FT2)):
                bank, full = t_begin(f"vec.{g}")
                pe.transpose(bank[:, 0:n], vrow[g][0:n, :], ident[0:n, 0:n]).then_inc(full, 1)

            pe.wait_ge(ev("me_scaled"), T)
            turn_tokens("me", work)
            lt_wait("me")
            panel("MK0", lta, 256)
            pe.wait_ge(ev("ones_ready"), 1)
            mod_columns(0)
            panel("MK1", lta)
            panel("MK2", lta)
            pe.wait_ge(ev("h_scaled"), T)
            turn_tokens("h", work)
            lt_wait("h")

            panel("AQ", lta, 272)
            mod_columns(1)
            s, k = PLAN.bank("AQ")
            pe.wait_ge(panel_out[s], k + 2)
            bank, full = t_begin("aT")
            for t in range(T):
                ins = pe.transpose(bank[:, P * t:P * t + P], aq[:, t, 0:P], ident[:])
            ins.then_inc(full, 1)
            panel("GQ", lta)
            b, k = T_USE["aT"]
            pe.wait_ge(t_free[b], k + 2)
            pe.wait_ge(ev("wg_landed"), 16)
            for g in range(2):
                bank, full = t_begin(f"z.{g}")
                for j in range(2):
                    h = 2 * g + j
                    ins = pe.matmul(bank[:, 256 * j:256 * j + 256], wg[0:GATE_RANK, P * h:P * h + P],
                                    aT[0:GATE_RANK, :], start=True, stop=True)
                ins.then_inc(full, 1)
            mod_columns(2)
            panel("GK", lta)
            mod_columns(3)

            for name, src in (("mqT", aq[:, :, GATE_RANK:272]), ("mkT", kvm[:, :, 0:256])):
                pe.wait_ge(ev(f"{name}_normed"), 1)
                turn_tokens(name, src, 2)
            for name in ("mqT", "mkT"):
                b, k = T_USE[name]
                pe.wait_ge(t_free[b], k + 2)

            def mem_scores(h, bank):
                lane = slice(64 * (h % 2), 64 * (h % 2) + 64)
                for t in range(T):
                    ins = pe.matmul(bank[:, 256 * t:256 * t + 256], mqT[lane, h // 2, P * t:P * t + P],
                                    mkT[lane, h // 2, :], start=True, stop=True)
                return ins

            def mem_values(h, bank, pT):
                for t in range(T):
                    for kt in range(T):
                        ins = pe.matmul(bank[:, 256 * t:256 * t + 256], pT[:, 256 * t + P * kt:256 * t + P * kt + P],
                                        kvm[:, kt, 256 + 256 * h:512 + 256 * h], start=(kt == 0), stop=(kt == T - 1))
                return ins

            def fill(names, first, n):
                for j in range(first, first + n):
                    unit(names[j // 4], j % 4, lta)

            vr = ["V0", "V1", "R0", "R1"]
            attend("MEM", H_MEM, mem_scores, 4, mem_values, lambda i: fill(vr, 4 * i, 2),
                   lambda i: fill(vr, 4 * i + 2, 2), lambda i: mod_columns(4 + i) if i < 4 else None)

            for name, src in (("gqT", gq), ("gkT", gk)):
                turn_tokens(name, src, 4)
            for g in ("gqT.0", "gqT.1", "gkT.0", "gkT.1"):
                b, k = T_USE[g]
                pe.wait_ge(t_free[b], k + 2)
            cq = ["CK", "Q0", "Q1", "Q2"]
            for s in range(9):
                lhs, rhs = (gkT, gqT) if s == 0 else (gkd, gqd)
                if s >= 1:
                    pe.wait_ge(gla_in, s)
                if s == 1:
                    bank, full = s_begin("gla.off")
                    for h in range(H_GLA):
                        ins = pe.matmul(bank[:, P * h:P * h + P], lhs[:, h, 0:P], rhs[:, h, P:2 * P],
                                        start=True, stop=True)
                    ins.then_inc(full, 1)
                else:
                    for t in range(T):
                        bank, full = s_begin(f"gla.{max(s - 1, 0)}.{t}")
                        for h in range(H_GLA):
                            tok = slice(P * t, P * t + P)
                            ins = pe.matmul(bank[:, P * h:P * h + P], lhs[:, h, tok], rhs[:, h, tok],
                                            start=True, stop=True)
                        ins.then_inc(full, 1)
                if s < 8:
                    for j in (2 * s, 2 * s + 1):
                        unit(cq[j // 4], j % 4, lta, 320 if j < 4 else COLS)
                if s % 2 == 1:
                    mod_columns(8 + s // 2)
            for name in ("gla.off", "gla.7.0", "gla.7.1"):
                b, k = S_USE[name]
                pe.wait_ge(s_free[b], k + 2)
            for t in range(T):
                for g in range(2):
                    bank, full = t_begin(f"go.{2 * t + g}")
                    for j in range(2):
                        h = 2 * g + j
                        o = bank[:, 256 * j:256 * j + 256]
                        if t == 1:
                            pe.matmul(o, attn[:, 2, h, :], gv[:, 0, 256 * h:256 * h + 256], start=True, stop=False)
                        ins = pe.matmul(o, attn[:, t, h, :], gv[:, t, 256 * h:256 * h + 256],
                                        start=(t == 0), stop=True)
                    ins.then_inc(full, 1)

            pe.wait_ge(ev("ck_normed"), 1)
            turn_tokens("ck", ck, 2)
            pe.wait_ge(ev("ckT_ready"), 1)
            for c in range(4):
                unit(f"UKV{c}", 0, ckT)
            pe.wait_ge(ev("q_normed"), 1)
            for g in range(4):
                bank, full = t_begin(f"qn.{g}")
                for j in range(2):
                    for t in range(T):
                        c = 192 * (2 * g + j)
                        ins = pe.transpose(bank[:, 256 * j + P * t:256 * j + P * t + P], q[:, t, c:c + P], ident[:])
                ins.then_inc(full, 1)
            for g in range(2):
                bank, full = t_begin(f"qr.{g}")
                for j in range(2):
                    for t in range(T):
                        ins = pe.transpose(bank[:, 256 * j + P * t:256 * j + P * t + P],
                                           work[:, t, 0:512][:, P * (2 * g + j):P * (2 * g + j) + P], ident[:])
                ins.then_inc(full, 1)
            bank, full = t_begin("kp")
            for t in range(T):
                ins = pe.transpose(bank[:, P * t:P * t + P], kpe[:, t, :], ident[:])
            ins.then_inc(full, 1)
            pe.wait_ge(ev("k_normed"), 1)
            for g in range(4):
                bank, full = t_begin(f"kn.{g}")
                for j in range(2):
                    for t in range(T):
                        c = 256 * (2 * g + j)
                        ins = pe.transpose(bank[:, 256 * j + P * t:256 * j + P * t + P], kv[:, t, c:c + P], ident[:])
                ins.then_inc(full, 1)
            for g in ("kn.2", "kn.3"):
                b, k = T_USE[g]
                pe.wait_ge(t_free[b], k + 2)

            def mla_scores(h, bank):
                lane = slice(64 * (h % 2), 64 * (h % 2) + 64)
                for t in range(T):
                    o = bank[:, P * t:P * t + P * (t + 1)]
                    pe.matmul(o, qnT[:, h, P * t:P * t + P], knT[:, h, 0:P * (t + 1)], start=True, stop=False)
                    ins = pe.matmul(o, qrT[lane, h // 2, P * t:P * t + P], kpT[lane, 0:P * (t + 1)],
                                    start=False, stop=True)
                return ins

            def mla_values(h, bank, pT):
                for t in range(T):
                    for kt in range(t + 1):
                        ins = pe.matmul(bank[:, P * t:P * t + P], pT[:, P * (t + kt):P * (t + kt) + P],
                                        kv[:, kt, 256 * h + P:256 * h + 2 * P], start=(kt == 0), stop=(kt == t))
                return ins

            gates = ["G10", "G11", "G20", "G21", "G00", "G01"]
            attend("MLA", H_MLA, mla_scores, 3, mla_values, lambda i: fill(gates, 3 * i, 2),
                   lambda i: fill(gates, 3 * i + 2, 1))

            pe.wait_ge(ev("branches_mixed"), 1)
            turn_tokens("y", r_gla)
            lt_wait("y")
            panel("WO0", lta)
            panel("WO1", lta)
            pe.wait_ge(ev("ctx_landed"), 16)
            turn_tokens("hc", ar(8192, T, D))
            lt_wait("hc")
            panel("CX", lta)

            pe.wait_ge(ev("h2_scaled"), T)
            turn_tokens("h2", work)
            lt_wait("h2")

            def up_turn(c, i=None):
                pe.wait_ge(up_done, c + 1 + (2 * i if i is not None else 0))
                for g in range(2):
                    b, k = T_USE[f"WU{c}.{g}"]
                    pe.wait_ge(t_free[b], k + 1 + (2 * i if i is not None else 0))
                    for kk in range(2):
                        for t in range(T):
                            ins = pe.transpose(tb[b][:, 256 * kk + P * t:256 * kk + P * t + P],
                                               up[:, c % 2, t, P * (2 * g + kk):P * (2 * g + kk) + P], ident[:])
                    ins.then_inc(t_full[b], 1)

            panel("WU0", ltb)
            with pe.Fori(0, 3) as i:
                for c in (1, 2):
                    for k in range(4):
                        unit(f"WU{c}", k, ltb, i=i, per=8)
                        if k == 1:
                            up_turn(c - 1, i)
            for k in range(4):
                unit("WU7", k, ltb)
                if k == 1:
                    up_turn(6)
            for c in range(2):
                for k in range(D_FF // P // UNIT):
                    if c == 0 and k == 2:
                        up_turn(7)
                    if c == 0 and k % 2 == 0:
                        for g in range(2):
                            b, n = T_USE[f"WU{k // 2}.{g}"]
                            pe.wait_ge(t_free[b], n + 2)
                    unit(f"WD{c}", k, ff)

            for s in range(2):
                p, k = PLAN.bank(f"WD{s}")
                pe.wait_ge(panel_out[p], k + 2)
            turn_tokens("x2", x)
            lt_wait("x2")
            for c in range(3):
                panel(f"IN{c}", lta)
            for br, (kn, qn) in enumerate((("kA", "qA"), ("kB", "qB"))):
                pe.wait_ge(ev(f"{kn}_normed"), 1)
                for g in range(KVH):
                    bank, full = t_begin(f"{kn}.{g}")
                    for j in range(2):
                        for t in range(T):
                            ins = pe.transpose(bank[:, 256 * j + P * t:256 * j + P * t + P],
                                               kdup[:, 2 * br + j, t, P * g:P * g + P], ident[:])
                    ins.then_inc(full, 1)
                pe.wait_ge(ev(f"{qn}_normed"), 1)
                for g in range(2):
                    bank, full = t_begin(f"{qn}.{g}")
                    for j in range(2):
                        for t in range(T):
                            c = 768 * br + P * (2 * g + j)
                            ins = pe.transpose(bank[:, 256 * j + P * t:256 * j + P * t + P],
                                               qkv[:, t, c:c + P], ident[:])
                    ins.then_inc(full, 1)
            for g in ("kA.0", "kA.1", "qA.0", "qA.1", "kB.0", "kB.1", "qB.0", "qB.1"):
                b, k = T_USE[g]
                pe.wait_ge(t_free[b], k + 2)

            def ab_step(i):
                return i // (HEADS * T), i % (HEADS * T) // T, i % T

            def ab_scores(i, bank):
                br, h, t = ab_step(i)
                lane = slice(64 * (h % 2), 64 * (h % 2) + 64)
                return pe.matmul(bank[:, :], qT[br][lane, h // 2, P * t:P * t + P], kT[br][lane, h // GROUP, :],
                                 start=True, stop=True)

            def ab_values(i, bank, pT):
                br, h, t = ab_step(i)
                for kt in range(4):
                    v = qkv[:, kt, 768 * br + 640:768 * br + 768] if kt < 2 else \
                        kvx[:, kt - 2, 256 * br + 128:256 * br + 256]
                    ins = pe.matmul(bank[:, 0:HD], pT[:, P * kt:P * kt + P], v[:, HD * (h // GROUP):][:, 0:HD],
                                    start=(kt == 0), stop=(kt == 3))
                return ins

            in2 = ["IN3", "IN4", "IN5", "IN6"]
            attend("AB", 2 * HEADS * T, ab_scores, 4, ab_values,
                   lambda i: fill(in2, i // 2, 1) if i % 2 == 0 else None)

            b, k = T_USE[f"AB.O{2 * HEADS * T - 1}"]
            pe.wait_ge(t_free[b], k + 2)
            b, k = T_USE[f"AB.O{2 * HEADS * T - 2}"]
            pe.wait_ge(t_free[b], k + 2)
            turn_tokens("oab", oab)
            lt_wait("oab", 1)
            for name in ("BA0", "BA1", "BB0", "BB1"):
                if name == "BB0":
                    lt_wait("oab")
                for k in range(2):
                    unit(name, k, ltb, first_kt=2 * k + (4 if name[1] == "B" else 0))
            pe.wait_ge(ev("ym_ready"), 1)
            turn_tokens("ym", ym)
            lt_wait("ym")
            panel("OUT0", lta)
            panel("OUT1", lta)

            def gate_rows(name):
                for g in range(2):
                    bank, full = t_begin(f"{name}.{g}")
                    pe.wait_ge(ev(f"{name}_diag"), g + 1)
                    for j in range(4):
                        ins = pe.matmul(bank[:, P * j:P * j + P], ones[:], diag[:, j, :], start=True, stop=True)
                    ins.then_inc(full, 1)

            gate_rows("gate1")

            pe.wait_ge(ev("x3_ready"), T)
            turn_tokens("x3", x)
            lt_wait("x3")

            def conv_turn(c, i=None):
                s, k = PLAN.bank(f"UP{c}")
                pe.wait_ge(panel_out[s], k + 2 + (i if i is not None else 0))
                for g in range(2):
                    b, k = T_USE[f"UP{c}.{g}"]
                    pe.wait_ge(t_free[b], k + 1 + (2 * i if i is not None else 0))
                    for kk in range(2):
                        for t in range(T):
                            ins = pe.transpose(tb[b][:, 256 * kk + P * t:256 * kk + P * t + P],
                                               upv[:, c % 2, t, P * (2 * g + kk):P * (2 * g + kk) + P], ident[:])
                    ins.then_inc(t_full[b], 1)

            panel("UP0", ltb)
            with pe.Fori(0, 5) as i:
                for c in (1, 2):
                    for k in range(4):
                        unit(f"UP{c}", k, ltb, i=i, per=8)
                        if k == 1:
                            conv_turn(c - 1, i)
            for c in range(2):
                for k in range(FT2 // UNIT):
                    if c == 0 and k == 2:
                        conv_turn(10)
                    if c == 0:
                        pe.wait_ge(conv_mul, k + 1)
                    unit(f"DN{c}", k, actT)
            gate_rows("gate2")

        def last_unit(name):
            return PLAN.unit[name] + units_of(name) - 1

        @block.scalar
        def _(act):
            order = Order(act, act_order)

            def split(u, i=None, per=0, landings=0):
                s = u % RING
                du = per * i if i is not None else 0
                act.wait_ge(landed[s], PLAN.landed[u] + (landings * i if i is not None else 0))
                act.wait_ge(unit_used, u + 1 + du)
                n = PLAN.cols[u]
                act.copy(whi[:, s, :, 0:n], raw[:, s, :, 0:n]).then_inc(hi_ready, 1)

            cursor = [0]

            def ahead(pos):
                while cursor[0] < min(pos + AHEAD, PLAN.units):
                    split(cursor[0])
                    cursor[0] += 1

            def panel_wait(name, du=0):
                act.wait_ge(unit_used, RING + last_unit(name) + 1 + du)

            def evac(name, dst, n=COLS, func=ACT.Copy):
                ahead(last_unit(name) + 1)
                panel_wait(name)
                s, _ = PLAN.bank(name)
                act.activation(dst, acc[s][:, :, 0:n], func).then_inc(panel_out[s], 1)

            def lt_act(name, lt):
                for g in range(4):
                    b, k = T_USE[f"{name}.{g}"]
                    act.wait_ge(t_free[b], k + 2)
                    act.copy(lt[0][:, 2 * g:2 * g + 2, :].rearrange("p a b -> p (a b)"), turn[:, g % 2])\
                        .then_inc(lt_hi, 1)

            def sqrt(name, view):
                act.wait_ge(ev(f"{name}_var"), 1)
                act.activation(view, view, ACT.Sqrt).then_inc(ev(f"{name}_std"), 1)

            def t_out(name, dst, n=COLS, scale=1.0, parts=None):
                b, k = T_USE[name]
                act.wait_ge(t_full[b], k + 1)
                act.activation(dst, tb[b][0:(parts or P), 0:n], ACT.Copy, scale=scale).then_inc(t_free[b], 1)

            def attend(name, n, exps, at_scores, at_turn, blocks, after=None):
                def exp(i):
                    ahead(at_scores(i))
                    g = STEPS[name][0] + i
                    b, _ = S_USE[f"{name}.{i}"]
                    act.wait_ge(soft_ready, g + 1)
                    exps(i, g % 2, sc[b]).then_inc(s_free[b], 1)

                exp(0)
                for i in range(n):
                    if i + 1 < n:
                        exp(i + 1)
                    ahead(at_turn(i))
                    if i >= 2:
                        b, k = T_USE[f"{name}.O{i - 2}"]
                        act.wait_ge(t_full[b], k + 1)
                    t_out(f"{name}.PT{i}", probT[:, (STEPS[name][0] + i) % 2, 0:P * blocks], P * blocks)
                    if after:
                        after(i)

            for name, (first, n) in ROWS.items():
                act.dma_start(vrow[0][first:first + n, :], a[name].rearrange("(r c) -> r c", c=P))\
                    .then_inc(ev("rows_landed"), 16)
            for k, src in enumerate((a["conv_w_2"][0], a["conv_w_2"][1], a["conv_w_2"][2], a["conv_b_2"])):
                act.dma_start(vrow[1 + k // 2][44 * (k % 2):44 * (k % 2) + 44, :],
                              src.rearrange("(r c) -> r c", c=P)).then_inc(ev("rows_landed"), 16)
            act.dma_start(stat[:, 7, 4:6].bitcast(I32), a["positions"].rearrange("(t p) -> p t", p=P),
                          allow_slow_non_contiguous=True)\
                .then_inc(ev("pos_landed"), 16)
            for name, view in GAIN.items():
                act.dma_start(view, a[name].partition_broadcast(P)).then_inc(ev("gains_landed"), 16)
            for name, src, s in (("me", memx, 0), ("h", x[:], 1)):
                act.wait_ge(ev("mem_landed" if name == "me" else "x_landed"), 16)
                for t in range(T):
                    act.activation(prob[:].rearrange("p a b -> p (a b)"), src[:, t, :], ACT.Square,
                                   accum_out=stat[:, s, t:t + 1]).then_inc(ev(f"{name}_sum"), 1)
                    act.wait_ge(ev(f"{name}_sum"), t + 1)
            sqrt("me", stat[:, 0, 2:4])
            sqrt("h", stat[:, 1, 2:4])
            act.wait_ge(ev("vec_ready"), 1)
            act.activation(sic[:], vcol[:, ROWS["c_2"][0]:ROWS["c_2"][0] + 16], ACT.Sigmoid).then_inc(ev("c_sig"), 1)
            ahead(0)
            lt_act("me", lta)
            act.wait_ge(ev("rot_arg"), 1)
            act.activation(rot[:, 0:2], rot[:, 0:2], ACT.Sin).then_inc(ev("rot_ready"), 1)
            evac("MK0", kvm[:, :, 0:256], 256)
            evac("MK1", kvm[:, :, 256:768])
            evac("MK2", kvm[:, :, 768:1280])
            lt_act("h", lta)
            act.wait_ge(ev("memx_free"), 1)
            act.dma_start(wg[0:GATE_RANK, :], a["w_gla_gate"]).then_inc(ev("wg_landed"), 16)
            evac("AQ", aq[:], 272)
            t_out("aT", aT[0:GATE_RANK, :], 256, parts=GATE_RANK)
            evac("GQ", gq)
            act.wait_ge(ev("zb_ready"), 1)
            order.done(act.activation(ze, zb, ACT.Abs))
            order.done(act.activation(ze, ze, ACT.Exp, scale=-1.0))
            act.activation(ze, ze, ACT.Ln, bias=1.0).then_inc(ev("zln_ready"), 1)
            evac("GK", gk)
            sqrt("mm", stat[:, 2, 0:16])
            for name, dst in (("mqT", mqT), ("mkT", mkT)):
                t_out(name, dst.rearrange("p a b -> p (a b)"))

            def mem_exps(i, slot, bank):
                for t in range(T):
                    ins = act.activation(prob[:, slot, 256 * t:256 * t + 256], bank[:, 256 * t:256 * t + 256], ACT.Exp,
                                         bias=soft[:, slot, 2 + t:3 + t], scale=DQ_MEM ** -0.5,
                                         accum_out=soft[:, slot, 4 + t:5 + t])
                return ins

            def mem_after(i):
                if i < 2:
                    evac(f"V{i}", gv[:, :, COLS * i:COLS * i + COLS])
                else:
                    name = f"R{i - 2}"
                    ahead(last_unit(name) + 1)
                    panel_wait(name)
                    if i == 3:
                        b, k = PLAN.bank("R0")
                        act.wait_ge(panel_out[b], k + 2)
                    act.activation(rsig, acc[PLAN.bank(name)[0]][:], ACT.Sigmoid).then_inc(ev("r_sig"), 1)

            u0 = PLAN.unit["V0"]
            attend("MEM", H_MEM, mem_exps, lambda i: u0 + 4 * max(i - 1, 0), lambda i: u0 + 4 * i + 2, 4, mem_after)

            for name, dst, f in (("gqT", gqT, DK_GLA ** -0.5), ("gkT", gkT, 1.0)):
                for g in range(2):
                    t_out(f"{name}.{g}", dst[:, 2 * g:2 * g + 2, :].rearrange("p a b -> p (a b)"), scale=f)
            u0 = PLAN.unit["CK"]
            for s in range(1, 9):
                ahead(u0 + 2 * s)
                act.wait_ge(gla_exp, s)
                e = arena[:, 7168:8192]
                act.activation(e, e, ACT.Exp).then_inc(ev("gla_expd"), 1)
                if s == 2:
                    evac("CK", ck, 320)
                if s in (4, 6, 8):
                    c = s // 2 - 2
                    evac(f"Q{c}", q[:, :, COLS * c:COLS * c + COLS])
            sqrt("ck", stat[:, 3, 0:4])
            for t in range(T):
                for g in range(2):
                    t_out(f"go.{2 * t + g}", og[:, t, 2 * g:2 * g + 2, :].rearrange("p a b -> p (a b)"))
            act.wait_ge(ev("ck_turned"), 1)
            act.copy(ckT[0][:].rearrange("p a b -> p (a b)"), turn[:, 0]).then_inc(ev("ckT_hi"), 1)
            sqrt("qq", stat[:, 4:6, :])
            sqrt("og", stat[:, 6, 0:8])
            for c in range(4):
                evac(f"UKV{c}", kv[:, :, COLS * c:COLS * c + COLS])
            for g in range(4):
                t_out(f"qn.{g}", qnT[:, 2 * g:2 * g + 2, :].rearrange("p a b -> p (a b)"), scale=col("g_q_nope"))
            for g in range(2):
                t_out(f"qr.{g}", qrT[:, 2 * g:2 * g + 2, :].rearrange("p a b -> p (a b)"))
            t_out("kp", kpT, 256)
            sqrt("kk", stat[:, 2, 0:16])
            for g in range(4):
                t_out(f"kn.{g}", knT[:, 2 * g:2 * g + 2, :].rearrange("p a b -> p (a b)"), scale=col("g_k_nope"))

            def mla_exps(i, slot, bank):
                for t, (first, n) in enumerate(((0, P), (P, 2 * P))):
                    ins = act.activation(prob[:, slot, first:first + n], bank[:, first:first + n], ACT.Exp,
                                         bias=soft[:, slot, 2 + t:3 + t], scale=(NOPE + ROPE) ** -0.5,
                                         accum_out=soft[:, slot, 4 + t:5 + t])
                return ins

            gates = ["G10", "G11", "G20", "G21", "G00", "G01"]
            gate_at = {}
            for c in range(6):
                gate_at[(4 * c + 3) // 3] = c

            def mla_after(i):
                if i in gate_at:
                    c = gate_at[i]
                    s, k = PLAN.bank(gates[c])
                    ahead(last_unit(gates[c]) + 1)
                    act.wait_ge(panel_out[s], k + 2)
                    act.activation(stage[:, c % 2], stage[:, c % 2], ACT.Sigmoid).then_inc(gate_sig, 1)

            u0 = PLAN.unit["G10"]
            attend("MLA", H_MLA, mla_exps, lambda i: u0 + 3 * max(i - 1, 0), lambda i: u0 + 3 * i + 2, 3, mla_after)

            lt_act("y", lta)
            ahead(PLAN.unit["CX"])
            for t in range(T):
                act.wait_ge(ev("x1_ready"), 2)
                act.activation(prob[:].rearrange("p a b -> p (a b)"), x[:, t, :], ACT.Square,
                               accum_out=stat[:, 1, t:t + 1]).then_inc(ev("h2_sum"), 1)
                act.wait_ge(ev("h2_sum"), t + 1)
            sqrt("h2", stat[:, 1, 2:4])
            lt_act("hc", lta)
            ahead(PLAN.unit["WU0"])
            lt_act("h2", ltb)

            def up_hi_of(c, i=None):
                d = 2 * i if i is not None else 0
                for g in range(2):
                    b, k = T_USE[f"WU{c}.{g}"]
                    act.wait_ge(t_full[b], k + 1 + d)
                    ft = 4 * c + 2 * g
                    dst = ff[0][:, ft:ft + 2, :] if i is None else ff[0][:, bass.ds(8 * i + ft, 2), :]
                    act.copy(dst.rearrange("p a b -> p (a b)"), tb[b][:]).then_inc(up_hi, 1)

            def up_relu(c, i=None):
                s, _ = PLAN.bank(f"WU{c}")
                panel_wait(f"WU{c}", 8 * i if i is not None else 0)
                act.activation(up[:, c % 2], acc[s][:], ACT.Relu).then_inc(panel_out[s], 1)

            evac("WU0", up[:, 0], func=ACT.Relu)
            u0 = PLAN.unit["WU1"]
            assert cursor[0] == u0 + AHEAD
            with act.Fori(0, 3) as i:
                for c in (1, 2):
                    for k in range(4):
                        split(u0 + 4 * (c - 1) + k + AHEAD, i, 8, 32)
                        if k == 1:
                            up_hi_of(c - 1, i)
                    up_relu(c, i)
            cursor[0] += 24
            ahead(PLAN.unit["WU7"] + 2)
            up_hi_of(6)
            ahead(PLAN.unit["WU7"] + 4)
            up_relu(7)
            ahead(PLAN.unit["WD0"] + 2)
            up_hi_of(7)
            ahead(PLAN.unit["IN0"])

            lt_act("x2", lta)
            ahead(PLAN.unit["IN3"])
            sqrt("ab", stat[:, 2:4, :])
            for br, names in enumerate((("kA", "qA"), ("kB", "qB"))):
                for g in range(2):
                    t_out(f"{names[0]}.{g}", kT[br][:, g, :])
                for g in range(2):
                    t_out(f"{names[1]}.{g}", qT[br][:, 2 * g:2 * g + 2, :].rearrange("p a b -> p (a b)"))

            def ab_exps(i, slot, bank):
                br, h = i // (HEADS * T), i % (HEADS * T) // T
                if br == 0:
                    act.activation(soft[:, slot, 6:7], GAIN["attn_sink_2"][:, h:h + 1], ACT.Exp,
                                   bias=soft[:, slot, 2:3])
                return act.activation(prob[:, slot, :], bank[:], ACT.Exp, bias=soft[:, slot, 2:3],
                                      scale=HD ** -0.5, accum_out=soft[:, slot, 4:5])

            def ab_after(i):
                if i % 8 == 7:
                    name = f"IN{3 + i // 8}"
                    s, k = PLAN.bank(name)
                    c = COLS * (i // 8)
                    ahead(last_unit(name) + 1)
                    act.wait_ge(panel_out[s], k + 2)
                    act.activation(gate2[:, :, c:c + COLS], gate2[:, :, c:c + COLS], ACT.Sigmoid).then_inc(gate_sig, 1)

            u0 = PLAN.unit["IN3"]
            attend("AB", 2 * HEADS * T, ab_exps, lambda i: u0 + max(i, 0) // 2, lambda i: u0 + i // 2 + 1, 4, ab_after)
            lt_act("oab", ltb)
            ahead(PLAN.unit["OUT0"])
            lt_act("ym", lta)
            for c in range(2):
                evac(f"OUT{c}", work[:, :, COLS * c:COLS * c + COLS])
            sqrt("ln1", stat[:, 1, 4:6])
            ahead(PLAN.unit["UP0"])
            lt_act("x3", ltb)

            def conv_of(c, i=None):
                d = i if i is not None else 0
                act.wait_ge(ev("tap_ready"), c + 1 + 2 * d)
                for j in range(4):
                    b, k = T_USE[f"UP{c}.{j // 2}"]
                    act.wait_ge(t_full[b], k + 1 + 2 * d)
                    act.activation(conv[:, j], tb[b][:, 256 * (j % 2):256 * (j % 2) + 256], ACT.Identity,
                                   bias=tap[:, 3, j:j + 1], scale=tap[:, 1, j:j + 1]).then_inc(conv_lin, 1)
                b, k = T_USE[f"UP{c}.0"]
                act.wait_ge(t_free[b], k + 2 + 2 * d)
                act.activation(sig[:], conv[:, 0:2], ACT.Sigmoid).then_inc(conv_sig, 1)

            def conv_hi(c, i=None):
                d = i if i is not None else 0
                act.wait_ge(ev("conv_prod"), c + 1 + 2 * d)
                dst = actT[0][:, 2 * c:2 * c + 2, :] if i is None else actT[0][:, bass.ds(4 * i + 2 * c, 2), :]
                act.copy(dst, conv[:, 2:4]).then_inc(ev("conv_hi"), 1)

            def upv_out(c, i=None):
                s, _ = PLAN.bank(f"UP{c}")
                panel_wait(f"UP{c}", 8 * i if i is not None else 0)
                act.copy(upv[:, c % 2], acc[s][:]).then_inc(panel_out[s], 1)

            evac("UP0", upv[:, 0])
            u0 = PLAN.unit["UP1"]
            assert cursor[0] == u0 + AHEAD
            with act.Fori(0, 5) as i:
                for c in (1, 2):
                    for k in range(4):
                        split(u0 + 4 * (c - 1) + k + AHEAD, i, 8, 64)
                        if k == 1:
                            conv_of(c - 1, i)
                        if k == 2:
                            conv_hi(c - 1, i)
                    upv_out(c, i)
            cursor[0] += 40
            ahead(PLAN.unit["DN0"] + 2)
            conv_of(10)
            conv_hi(10)
            ahead(PLAN.units)
            for c in range(2):
                evac(f"DN{c}", work[:, :, COLS * c:COLS * c + COLS])
            sqrt("ln2", stat[:, 1, 4:6])

        @block.vector
        def _(dve):
            order = Order(dve, dve_order)
            done = order.done
            for s in panel_out + t_free + s_free:
                dve.sem_inc(s, 1)
            dve.sem_inc(split_ready, RING)
            dve.sem_inc(mod_free, 2)
            dve.sem_inc(bias_used, 2)

            def split(u, i=None, per=0):
                s = u % RING
                dve.wait_ge(hi_ready, u + 1 + (per * i if i is not None else 0))
                n = PLAN.cols[u]
                dve.tensor_tensor(wlo[:, s, :, 0:n], raw[:, s, :, 0:n], whi[:, s, :, 0:n].bitcast(F32), ALU.subtract)\
                   .then_inc(split_ready, 1)

            cursor = [0]

            def ahead(pos):
                while cursor[0] < min(pos + AHEAD, PLAN.units):
                    split(cursor[0])
                    cursor[0] += 1

            def panel_wait(name):
                ahead(last_unit(name) + 1)
                dve.wait_ge(unit_used, RING + last_unit(name) + 1)
                return acc[PLAN.bank(name)[0]]

            def evacuated(name):
                s, k = PLAN.bank(name)
                dve.wait_ge(panel_out[s], k + 2)

            def frees(name, ins):
                s, k = PLAN.bank(name)
                ins.then_inc(panel_out[s], 1)
                dve.wait_ge(panel_out[s], k + 2)

            def biased(name, dst):
                p, n = panel_wait(name), n_gate[name]
                twice = (n // 2 + 1) + (1 if n % 2 == 0 and n >= n_gate["CX"] else 0)
                dve.wait_ge(bias_landed[n % 2], 16 * twice)
                frees(name, dve.tensor_tensor(dst, p[:], bias[:, n % 2].unsqueeze(1).broadcast_to([P, T, COLS]),
                                              ALU.add))
                dve.sem_inc(bias_used, 1)

            def lt_dve(name, lt, scale=None, shift=None):
                def low(g):
                    dve.wait_ge(lt_hi, lt_done(name, g))
                    dve.tensor_tensor(lt[1][:, 2 * g:2 * g + 2, :].rearrange("p a b -> p (a b)"), turn[:, g % 2],
                                      lt[0][:, 2 * g:2 * g + 2, :].bitcast(F32).rearrange("p a b -> p (a b)"),
                                      ALU.subtract).then_inc(lt_ready, 1)

                for g in range(4):
                    b, k = T_USE[f"{name}.{g}"]
                    if lt_done(name, g) > 2:
                        dve.wait_ge(lt_ready, lt_done(name, g) - 2)
                    dve.wait_ge(t_full[b], k + 1)
                    if scale is None:
                        ins = dve.tensor_copy(turn[:, g % 2], tb[b][:])
                    else:
                        for kk in range(2):
                            half, c = slice(256 * kk, 256 * kk + 256), 2 * g + kk
                            if shift is None:
                                ins = dve.tensor_scalar(turn[:, g % 2, half], tb[b][:, half], scale[:, c:c + 1], None,
                                                        ALU.mult)
                            else:
                                ins = dve.tensor_scalar(turn[:, g % 2, half], tb[b][:, half], scale[:, c:c + 1],
                                                        shift[:, c:c + 1], ALU.mult, ALU.add)
                    ins.then_inc(t_free[b], 1)
                    if g >= 1:
                        low(g - 1)
                low(3)

            def spread(v, n):
                return v.unsqueeze(2).broadcast_to([P, v.shape[1], n])

            def squares(src, scratch, dst):
                done(dve.tensor_tensor(scratch, src, src, ALU.mult))
                done(dve.tensor_reduce(dst, scratch, AX.X, ALU.add))

            def var(view, n, eps=EPS):
                return dve.tensor_scalar(view, view, 1.0 / n, eps, ALU.mult, ALU.add)

            def inverse(name, view):
                dve.wait_ge(ev(f"{name}_std"), 1)
                done(dve.reciprocal(view, view))

            def rope(y1, y2, x1, x2, cos, sin, tmp):
                done(dve.tensor_tensor(y1, x1, cos, ALU.mult))
                done(dve.tensor_tensor(tmp, x2, sin, ALU.mult))
                done(dve.tensor_tensor(y1, y1, tmp, ALU.subtract))
                done(dve.tensor_tensor(y2, x2, cos, ALU.mult))
                done(dve.tensor_tensor(tmp, x1, sin, ALU.mult))
                done(dve.tensor_tensor(y2, y2, tmp, ALU.add))

            def mod_panel(c, pos, step=0):
                if c >= 1:
                    b, k = T_USE[f"mod.{c - 1}"]
                    dve.wait_ge(t_full[b], k + 1)
                for k in range(KT // UNIT):
                    ahead(pos + step * k)
                    dve.wait_ge(mod_landed[k % 2], 16 * (2 * c + k // 2 + 1))
                    for kk in range(UNIT):
                        for part in range(2 if c < 4 else 1):
                            f = sic[:, 8 * part + UNIT * k + kk:8 * part + UNIT * k + kk + 1]
                            w, s = wm[:, k % 2, kk], macc[:, part]
                            if k == 0 and kk == 0:
                                done(dve.tensor_scalar(s, w, f, None, ALU.mult))
                            else:
                                done(dve.scalar_tensor_tensor(s, w, f, s, ALU.mult, ALU.add))
                    dve.sem_inc(mod_free, 1)
                dve.sem_inc(mod_sum, 1)

            def mod_out(c):
                b, k = T_USE[f"mod.{c}"]
                dve.wait_ge(t_full[b], k + 1)
                if c < 4:
                    done(dve.tensor_tensor(modx[:, 4 * c:4 * c + 4], tb[b][:, 4:8], col("b_mod_2", 4 * c, 4), ALU.add))
                dve.tensor_tensor(modc[:, 4 * c:4 * c + 4], tb[b][:, 0:4], col("b_mod_2", 4 * c, 4), ALU.add)\
                    .then_inc(t_free[b], 1)

            def attend(name, n, maxima, sums, weigh, at_scores, at_turn, after=None):
                def softmax(i):
                    ahead(at_scores(i))
                    g = STEPS[name][0] + i
                    b, k = S_USE[f"{name}.{i}"]
                    dve.wait_ge(s_full[b], k + 1)
                    maxima(i, soft[:, g % 2], sc[b]).then_inc(soft_ready, 1)

                softmax(0)
                for i in range(n + 1):
                    if i >= 1:
                        b, k = S_USE[f"{name}.{i - 1}"]
                        dve.wait_ge(s_free[b], k + 2)
                        sums(i - 1, soft[:, (STEPS[name][0] + i - 1) % 2])
                    if i + 1 < n:
                        softmax(i + 1)
                    ahead(at_turn(i))
                    if i >= 1:
                        b, k = T_USE[f"{name}.O{i - 1}"]
                        dve.wait_ge(t_full[b], k + 1)
                        weigh(i - 1, soft[:, (STEPS[name][0] + i - 1) % 2, 8:10], tb[b]).then_inc(t_free[b], 1)
                    if after:
                        after(i)

            dve.wait_ge(ev("grid_ready"), 1)
            dve.wait_ge(ev("pos_landed"), 16)
            done(dve.tensor_copy(stat[:, 7, 6:8], stat[:, 7, 4:6].bitcast(I32)))
            done(dve.tensor_copy(stat[:, 7, 8:9], stat[:, 7, 2:3].bitcast(I32)))
            freq = rot[:, 2, 0, :]
            for t in range(T):
                for first, n, p in ((0, 32, stat[:, 7, 6 + t:7 + t]), (32, 16, stat[:, 7, t:t + 1]),
                                    (48, 16, stat[:, 7, 8:9])):
                    done(dve.tensor_scalar(angle[:, t, first:first + n], freq[:, first:first + n], p, None, ALU.mult))
            magic = 1.5 * 2.0 ** 23
            done(dve.tensor_scalar(turns, angle, float(1 / (2 * np.pi)), magic, ALU.mult, ALU.add))
            done(dve.tensor_scalar(turns, turns, magic, None, ALU.subtract))
            rest = 2 * np.pi
            for bits in (5, 14, 23, 60):
                part = float(np.float32(np.floor(rest * 2.0 ** bits) / 2.0 ** bits)) if bits < 60 else \
                    float(np.float32(rest))
                rest -= part
                done(dve.scalar_tensor_tensor(angle, turns, -part, angle, ALU.mult, ALU.add))
            pi = float(np.nextafter(np.float32(np.pi), np.float32(0)))
            done(dve.tensor_scalar(rot[:, 0], angle, pi, -pi, ALU.min, ALU.max))
            done(dve.scalar_tensor_tensor(turns, rot[:, 0], -1.0, rot[:, 0], ALU.mult, ALU.max))
            dve.tensor_scalar(rot[:, 1], turns, -1.0, float(np.pi / 2), ALU.mult, ALU.add)\
                .then_inc(ev("rot_arg"), 1)

            for s, name in ((0, "me"), (1, "h")):
                dve.wait_ge(ev(f"{name}_sum"), T)
                dve.tensor_scalar(stat[:, s, 2:4], stat[:, s, 0:2], 1.0 / D, EPS, ALU.mult, ALU.add)\
                    .then_inc(ev(f"{name}_var"), 1)
            inverse("me", stat[:, 0, 2:4])
            for t in range(T):
                dve.tensor_scalar(work[:, t], memx[:, t], stat[:, 0, 2 + t:3 + t], None, ALU.mult)\
                   .then_inc(ev("me_scaled"), 1)
            dve.wait_ge(ev("me_scaled"), T)
            dve.sem_inc(ev("memx_free"), 1)
            for g, dst in enumerate((vcol[:], ccol[:, 0:2], ccol[:, 2:4])):
                b, k = T_USE[f"vec.{g}"]
                dve.wait_ge(t_full[b], k + 1)
                n = (96, 88, 88)[g]
                src = tb[b][:, 0:n] if g == 0 else tb[b][:, 0:n].rearrange("p (a c) -> p a c", a=2)
                dve.tensor_copy(dst, src).then_inc(t_free[b], 1)
                dve.wait_ge(t_free[b], k + 2)
            dve.sem_inc(ev("vec_ready"), 1)
            ahead(0)
            lt_dve("me", lta, col("g_mem", 0, 8))
            inverse("h", stat[:, 1, 2:4])
            for t in range(T):
                dve.tensor_scalar(work[:, t], x[:, t], stat[:, 1, 2 + t:3 + t], None, ALU.mult)\
                   .then_inc(ev("h_scaled"), 1)
            dve.wait_ge(ev("c_sig"), 1)
            done(dve.tensor_tensor(sic[:], sic[:], vcol[:, ROWS["c_2"][0]:ROWS["c_2"][0] + 16], ALU.mult))
            mod_panel(0, 0, 1)
            ahead(PLAN.unit["MK1"])
            mod_out(0)
            ahead(PLAN.unit["AQ"])
            lt_dve("h", lta, col("g_mix", 0, 8))
            mod_panel(1, PLAN.unit["AQ"], 1)
            ahead(PLAN.unit["GQ"])
            mod_out(1)
            mod_panel(2, PLAN.unit["GQ"], 1)

            done(dve.memset(zflag, 1.0))
            done(dve.memset(zflag[:, :, 0:1], 0.0))
            ahead(PLAN.unit["GK"])
            for g in range(2):
                b, k = T_USE[f"z.{g}"]
                dve.wait_ge(t_full[b], k + 1)
                for j in range(2):
                    ins = dve.tensor_scalar(zb[:, 2 * g + j, :], tb[b][:, 256 * j:256 * j + 256],
                                            col("b_gla_gate", 2 * g + j), None, ALU.add)
                ins.then_inc(t_free[b], 1)
                dve.wait_ge(t_free[b], k + 2)
            dve.sem_inc(ev("zb_ready"), 1)
            mod_out(2)
            evacuated("AQ")
            evacuated("MK0")
            views = []
            for t in range(T):
                views.append((aq[:, t, GATE_RANK:272].rearrange("p (h c) -> p h c", c=DQ_MEM), stat[:, 2, 4 * t:4 * t + 4],
                              "g_q_mem"))
            for t in range(T):
                views.append((kvm[:, t, 0:256].rearrange("p (h c) -> p h c", c=DQ_MEM),
                              stat[:, 2, 8 + 4 * t:12 + 4 * t], "g_k_mem"))
            b, k = T_USE["h.3"]
            dve.wait_ge(t_full[b], k + 1)
            scratch = work[:, 0, 0:256].rearrange("p (h c) -> p h c", c=DQ_MEM)
            for v, s, _ in views:
                squares(v, scratch, s)
            var(stat[:, 2, :], DQ_MEM).then_inc(ev("mm_var"), 1)
            mod_panel(3, PLAN.unit["GK"], 1)
            dve.wait_ge(ev("zln_ready"), 1)
            done(dve.scalar_tensor_tensor(zb, zb, 0.0, ze, ALU.min, ALU.subtract))
            done(dve.tensor_scalar(zb, zb, 1.0 / 16.0, None, ALU.mult))
            done(dve.tensor_tensor_scan(arena[:, 6144:7168], arena[:, 13312:14336], arena[:, 11264:12288], 0.0,
                                        ALU.mult, ALU.add))
            inverse("mm", stat[:, 2, :])
            dve.wait_ge(ev("gains_landed"), 16 * len(GAIN))
            for i, (v, s, gain) in enumerate(views):
                done(dve.tensor_tensor(v, v, spread(s, DQ_MEM), ALU.mult))
                ins = dve.tensor_tensor(v, v, GAIN[gain].unsqueeze(1).broadcast_to([P, H_MEM, DQ_MEM]), ALU.mult)
                done(ins)
                if i % 2 == 1:
                    dve.sem_inc(ev(("mqT_normed", "mkT_normed")[i // 2]), 1)
            ahead(PLAN.unit["V0"])
            mod_out(3)

            def neg(s, n, scale):
                return dve.tensor_scalar(s[:, 2:2 + n], s[:, 0:n], -scale, None, ALU.mult)

            def mem_maxima(i, s, bank):
                done(dve.tensor_reduce(s[:, 0:2], bank[:].rearrange("p (t k) -> p t k", t=T), AX.X, ALU.max))
                return neg(s, 2, DQ_MEM ** -0.5)

            def sums2(i, s):
                done(dve.reciprocal(s[:, 8:10], s[:, 4:6]))

            def weigh2(dst, bank, r, n):
                return dve.tensor_tensor(dst, bank[:, 0:T * n].rearrange("p (t c) -> p t c", t=T), spread(r, n), ALU.mult)

            def mem_after(i):
                if 2 <= i < 4:
                    name, c = f"R{i - 2}", COLS * (i - 2)
                    p = panel_wait(name)
                    dve.wait_ge(ev("r_sig"), i - 1)
                    frees(name, dve.tensor_tensor(r_gla[:, :, c:c + COLS], p[:], rsig, ALU.mult))
                if i < 4:
                    mod_panel(4 + i, u0 + 4 * i + 4)
                    mod_out(4 + i)

            u0 = PLAN.unit["V0"]
            attend("MEM", H_MEM, mem_maxima, sums2,
                   lambda i, r, bank: weigh2(o_mem[:, :, DV_MEM * i:DV_MEM * i + DV_MEM], bank, r, DV_MEM),
                   lambda i: u0 + 4 * max(i - 1, 0), lambda i: u0 + min(4 * i + 2, 16), mem_after)

            u0 = PLAN.unit["CK"]
            for g in ("gqT.0", "gqT.1", "gkT.0", "gkT.1"):
                b, k = T_USE[g]
                dve.wait_ge(t_free[b], k + 2)
            done(dve.memset(attn, 0.0))
            done(dve.memset(arena[:, 18592:20640], 0.0))
            dve.wait_ge(ev("gmask_ready"), 1)

            def halves(v, w):
                return v.rearrange("p h (m e w) -> p (h m) e w", e=2, w=w)

            def exponents(s):
                if s == 1:
                    e = eq.rearrange("p (h c) -> p h c", h=H_GLA), ek.rearrange("p (h c) -> p h c", h=H_GLA)
                    done(dve.tensor_copy(e[0], decay[:, :, P:2 * P]))
                    ins = dve.tensor_tensor(e[1], decay[:, :, P - 1:P].broadcast_to([P, H_GLA, P]), decay[:, :, 0:P],
                                            ALU.subtract)
                else:
                    w = P >> (s - 1)
                    d = halves(decay, w)
                    ref = d[:, :, 0, w - 1:w].broadcast_to([P, d.shape[1], w])
                    done(dve.tensor_tensor(eq.rearrange("p (m w) -> p m w", w=w), d[:, :, 1, :], ref, ALU.subtract))
                    ins = dve.tensor_tensor(ek.rearrange("p (m w) -> p m w", w=w), ref, d[:, :, 0, :], ALU.subtract)
                ins.then_inc(gla_exp, 1)

            def decayed(s):
                if s >= 2:
                    b, k = S_USE["gla.off" if s == 2 else f"gla.{s - 2}.1"]
                    dve.wait_ge(s_full[b], k + 1)
                dve.wait_ge(ev("gla_expd"), s)
                if s == 1:
                    done(dve.tensor_tensor(gqd[:, :, P:2 * P], gqT[:, :, P:2 * P],
                                           eq.rearrange("p (h c) -> p h c", h=H_GLA), ALU.mult))
                    ins = dve.tensor_tensor(gkd[:, :, 0:P], gkT[:, :, 0:P],
                                            ek.rearrange("p (h c) -> p h c", h=H_GLA), ALU.mult)
                else:
                    w = P >> (s - 1)
                    done(dve.tensor_tensor(halves(gqd, w)[:, :, 1, :], halves(gqT, w)[:, :, 1, :],
                                           eq.rearrange("p (m w) -> p m w", w=w), ALU.mult))
                    ins = dve.tensor_tensor(halves(gkd, w)[:, :, 0, :], halves(gkT, w)[:, :, 0, :],
                                            ek.rearrange("p (m w) -> p m w", w=w), ALU.mult)
                ins.then_inc(gla_in, 1)
                dve.wait_ge(gla_in, s)

            def weights(s):
                if s == 1:
                    b, k = S_USE["gla.off"]
                    dve.wait_ge(s_full[b], k + 1)
                    dve.tensor_copy(attn[:, 2], sc[b][:].rearrange("p (h c) -> p h c", h=H_GLA)).then_inc(s_free[b], 1)
                    return
                mask = ident[:].bitcast(I32) if s == 0 else gmask[:, s - 2, :]
                for t in range(T):
                    b, k = S_USE[f"gla.{max(s - 1, 0)}.{t}"]
                    dve.wait_ge(s_full[b], k + 1)
                    dve.copy_predicated(attn[:, t], mask.unsqueeze(1).broadcast_to([P, H_GLA, P]),
                                        sc[b][:].rearrange("p (h c) -> p h c", h=H_GLA)).then_inc(s_free[b], 1)
                    dve.wait_ge(s_free[b], k + 2)

            exponents(1)
            for s in range(1, 9):
                ahead(u0 + 2 * s)
                decayed(s)
                if s < 8:
                    exponents(s + 1)
                weights(s - 1)
                if s % 2 == 1:
                    mod_panel(8 + s // 2, u0 + 2 * s + 2)
                    mod_out(8 + s // 2)
            weights(8)
            for v in (modc[:, 8:16], modc[:, 32:40], modx[:, 8:16]):
                done(dve.tensor_scalar(v, v, 1.0, None, ALU.add))

            ahead(PLAN.unit["UKV0"])
            evacuated("CK")
            for t in range(T):
                squares(ck[:, t:t + 1, 0:256], work[:, t:t + 1, 0:256], stat[:, 3, t:t + 1])
                squares(ck[:, t:t + 1, 256:320], work[:, t:t + 1, 0:64], stat[:, 3, 2 + t:3 + t])
            done(var(stat[:, 3, 0:2], KV_RANK))
            var(stat[:, 3, 2:4], ROPE).then_inc(ev("ck_var"), 1)
            inverse("ck", stat[:, 3, 0:4])
            for t in range(T):
                done(dve.tensor_scalar(ck[:, t, 0:256], ck[:, t, 0:256], stat[:, 3, t:t + 1], None, ALU.mult))
            dve.sem_inc(ev("ck_normed"), 1)
            for t in range(T):
                done(dve.scalar_tensor_tensor(ck[:, t, 256:320], ck[:, t, 256:320], stat[:, 3, 2 + t:3 + t],
                                              GAIN["g_k_rope"], ALU.mult, ALU.mult))
            dve.wait_ge(ev("rot_ready"), 1)
            x1, x2 = ck[:, :, 256:288], ck[:, :, 288:320]
            rope(kpe[:, :, 0:32], kpe[:, :, 32:64], x1, x2, rot[:, 1, :, 0:32], rot[:, 0, :, 0:32], work[:, :, 768:800])
            done(dve.tensor_copy(kpe[:, :, 64:128], kpe[:, :, 0:64]))
            b, k = T_USE["ck"]
            dve.wait_ge(t_full[b], k + 1)
            for kk in range(2):
                ins = dve.tensor_scalar(turn[:, 0, 256 * kk:256 * kk + 256], tb[b][:, 256 * kk:256 * kk + 256],
                                        col("g_ckv", kk), None, ALU.mult)
            ins.then_inc(t_free[b], 1)
            dve.wait_ge(t_free[b], k + 2)
            dve.sem_inc(ev("ck_turned"), 1)
            dve.wait_ge(ev("ckT_hi"), 1)
            dve.tensor_tensor(ckT[1][:].rearrange("p a b -> p (a b)"), turn[:, 0],
                              ckT[0][:].bitcast(F32).rearrange("p a b -> p (a b)"), ALU.subtract)\
                .then_inc(ev("ckT_ready"), 1)
            dve.wait_ge(ev("ckT_ready"), 1)

            for name in ("Q0", "Q1", "Q2"):
                evacuated(name)
            qh = [q[:, t, :].rearrange("p (h c) -> p h c", c=NOPE + ROPE) for t in range(T)]
            room = [o_mla[:, t, :].rearrange("p (h c) -> p h c", c=NOPE) for t in range(T)]
            for t in range(T):
                squares(qh[t][:, :, 0:NOPE], room[t], stat[:, 4, 8 * t:8 * t + 8])
                squares(qh[t][:, :, NOPE:], room[t][:, :, 0:ROPE], stat[:, 5, 8 * t:8 * t + 8])
            done(var(stat[:, 4, :], NOPE))
            var(stat[:, 5, :], ROPE).then_inc(ev("qq_var"), 1)
            for t in range(T):
                for g in range(2):
                    b, k = T_USE[f"go.{2 * t + g}"]
                    dve.wait_ge(t_free[b], k + 2)
            for t in range(T):
                squares(og[:, t], o_mla[:, t, :].rearrange("p (h c) -> p h c", c=DV_GLA), stat[:, 6, 4 * t:4 * t + 4])
            var(stat[:, 6, 0:8], DV_GLA).then_inc(ev("og_var"), 1)
            ahead(PLAN.unit["UKV0"] + 1)
            inverse("qq", stat[:, 4:6, :])
            for t in range(T):
                done(dve.tensor_tensor(qh[t][:, :, 0:NOPE], qh[t][:, :, 0:NOPE], spread(stat[:, 4, 8 * t:8 * t + 8], NOPE),
                                       ALU.mult))
                done(dve.tensor_tensor(qh[t][:, :, NOPE:], qh[t][:, :, NOPE:], spread(stat[:, 5, 8 * t:8 * t + 8], ROPE),
                                       ALU.mult))
                done(dve.tensor_tensor(qh[t][:, :, NOPE:], qh[t][:, :, NOPE:],
                                       GAIN["g_q_rope"].unsqueeze(1).broadcast_to([P, H_MLA, ROPE]), ALU.mult))
                y = work[:, t, 0:512].rearrange("p (h c) -> p h c", c=ROPE)
                ang = [rot[:, f, t, 0:32].unsqueeze(1).broadcast_to([P, H_MLA, 32]) for f in (1, 0)]
                rope(y[:, :, 0:32], y[:, :, 32:64], qh[t][:, :, NOPE:NOPE + 32], qh[t][:, :, NOPE + 32:], *ang,
                     work[:, t, 768:1024].rearrange("p (h c) -> p h c", c=32))
            dve.sem_inc(ev("q_normed"), 1)
            ahead(PLAN.unit["G10"])
            for c in range(4):
                evacuated(f"UKV{c}")
            kh = [kv[:, t, :].rearrange("p (h c) -> p h c", c=NOPE + V_MLA)[:, :, 0:NOPE] for t in range(T)]
            for t in range(T):
                squares(kh[t], room[t], stat[:, 2, 8 * t:8 * t + 8])
            var(stat[:, 2, :], NOPE).then_inc(ev("kk_var"), 1)
            inverse("kk", stat[:, 2, :])
            for t in range(T):
                done(dve.tensor_tensor(kh[t], kh[t], spread(stat[:, 2, 8 * t:8 * t + 8], NOPE), ALU.mult))
            dve.sem_inc(ev("k_normed"), 1)
            inverse("og", stat[:, 6, 0:8])
            for t in range(T):
                done(dve.tensor_tensor(og[:, t], og[:, t], spread(stat[:, 6, 4 * t:4 * t + 4], DV_GLA), ALU.mult))
                done(dve.tensor_tensor(og[:, t], og[:, t],
                                       GAIN["g_gla_out"].unsqueeze(1).broadcast_to([P, H_GLA, DV_GLA]), ALU.mult))
                done(dve.tensor_tensor(r_gla[:, t, :], r_gla[:, t, :], og[:, t].rearrange("p h c -> p (h c)"), ALU.mult))

            dve.wait_ge(ev("keeps_ready"), 1)

            def mla_maxima(i, s, bank):
                diagonal = bank[:].rearrange("p (a b) -> p a b", b=256)[:, :, 0:P]
                done(dve.tensor_tensor(diagonal, diagonal, keep_past[:].unsqueeze(1).broadcast_to([P, 2, P]), ALU.add))
                done(dve.tensor_reduce(s[:, 0:1], bank[:, 0:P], AX.X, ALU.max))
                done(dve.tensor_reduce(s[:, 1:2], bank[:, P:3 * P], AX.X, ALU.max))
                return neg(s, 2, (NOPE + ROPE) ** -0.5)

            gates = ["G10", "G11", "G20", "G21", "G00", "G01"]
            gate_at = {}
            for c in range(6):
                gate_at[(4 * c + 3) // 3] = c

            def mixed(c):
                dve.wait_ge(gate_sig, c + 1)
                part = slice(COLS * (c % 2), COLS * (c % 2) + COLS)
                y, s = r_gla[:, :, part], stage[:, c % 2]
                if c < 2:
                    done(dve.tensor_tensor(y, y, s, ALU.mult))
                else:
                    done(dve.tensor_tensor(s, s, (o_mem if c < 4 else o_mla)[:, :, part], ALU.mult))
                    done(dve.tensor_tensor(y, y, s, ALU.add))

            def mla_after(i):
                if i in gate_at:
                    c = gate_at[i]
                    if c >= 2:
                        mixed(c - 2)
                    biased(gates[c], stage[:, c % 2])

            u0 = PLAN.unit["G10"]
            attend("MLA", H_MLA, mla_maxima, sums2,
                   lambda i, r, bank: weigh2(o_mla[:, :, V_MLA * i:V_MLA * i + V_MLA], bank, r, V_MLA),
                   lambda i: u0 + 3 * max(i - 1, 0), lambda i: u0 + min(3 * i + 2, 24), mla_after)
            for g in (0, 1):
                b, k = T_USE[f"MLA.O{H_MLA - 1 - g}"]
                dve.wait_ge(t_free[b], k + 2)
            mixed(4)
            mixed(5)
            dve.sem_inc(ev("branches_mixed"), 1)
            lt_dve("y", lta)
            for c in range(2):
                name, part = f"WO{c}", slice(COLS * c, COLS * c + COLS)
                p = panel_wait(name)
                frees(name, dve.tensor_tensor(x[:, :, part], x[:, :, part], p[:], ALU.add))
                dve.sem_inc(ev("x1_ready"), 1)
            dve.wait_ge(ev("h2_sum"), T)
            dve.tensor_scalar(stat[:, 1, 2:4], stat[:, 1, 0:2], 1.0 / D, EPS, ALU.mult, ALU.add)\
                .then_inc(ev("h2_var"), 1)
            lt_dve("hc", lta, modx[:, 8:16], modx[:, 0:8])
            inverse("h2", stat[:, 1, 2:4])
            for t in range(T):
                dve.tensor_scalar(work[:, t], x[:, t], stat[:, 1, 2 + t:3 + t], None, ALU.mult)\
                   .then_inc(ev("h2_scaled"), 1)
            biased("CX", kvx[:])
            lt_dve("h2", ltb, col("g_ffn", 0, 8))

            def up_square(c, i=None):
                s, k = PLAN.bank(f"WU{c}")
                dve.wait_ge(panel_out[s], k + 2 + (i if i is not None else 0))
                dve.tensor_tensor(up[:, c % 2], up[:, c % 2], up[:, c % 2], ALU.mult).then_inc(up_done, 1)

            def up_lo(c, i=None):
                for g in range(2):
                    b, _ = T_USE[f"WU{c}.{g}"]
                    ft = 4 * c + 2 * g
                    dve.wait_ge(up_hi, 2 * c + g + 1 + (4 * i if i is not None else 0))
                    hi, lo = (v[:, ft:ft + 2, :] if i is None else v[:, bass.ds(8 * i + ft, 2), :] for v in ff)
                    dve.tensor_tensor(lo.rearrange("p a b -> p (a b)"), tb[b][:],
                                      hi.bitcast(F32).rearrange("p a b -> p (a b)"), ALU.subtract)\
                        .then_inc(t_free[b], 1)

            ahead(PLAN.unit["WU1"])
            up_square(0)
            u0 = PLAN.unit["WU1"]
            assert cursor[0] == u0 + AHEAD
            with dve.Fori(0, 3) as i:
                for c in (1, 2):
                    for k in range(4):
                        split(u0 + 4 * (c - 1) + k + AHEAD, i, 8)
                        if k == 1:
                            up_lo(c - 1, i)
                    up_square(c, i)
            cursor[0] += 24
            ahead(PLAN.unit["WU7"] + 2)
            up_lo(6)
            ahead(PLAN.unit["WU7"] + 4)
            up_square(7)
            ahead(PLAN.unit["WD0"] + 2)
            up_lo(7)
            for c in range(2):
                name, part = f"WD{c}", slice(COLS * c, COLS * c + COLS)
                p = panel_wait(name)
                frees(name, dve.tensor_tensor(x[:, :, part], x[:, :, part], p[:], ALU.add))

            lt_dve("x2", lta, modc[:, 8:16], modc[:, 0:8])
            for c in range(3):
                biased(f"IN{c}", qkv[:, :, COLS * c:COLS * c + COLS])

            def heads(v, n):
                return v.rearrange("p (h c) -> p h c", h=n)

            done(dve.memset(stat[:, 3, :], 1.0))
            normed = []
            for t in range(T):
                normed.append((heads(qkv[:, t, 768:1280], HEADS), stat[:, 2, 8 * t:8 * t + 8], "q_norm_g_2"))
                normed.append((heads(qkv[:, t, 1280:1408], KVH), stat[:, 3, 2 * t:2 * t + 2], "k_norm_g_2"))
                normed.append((heads(kvx[:, t, 256:384], KVH), stat[:, 3, 4 + 2 * t:6 + 2 * t], "k_norm_g_2"))
            for v, s, _ in normed:
                squares(v, heads(work[:, 0, 0:64 * v.shape[1]], v.shape[1]), s)
            var(stat[:, 2:4, :], HD).then_inc(ev("ab_var"), 1)

            def rope_2d(dst, src, n, t, room):
                def quarter(v, e):
                    return v.rearrange("p h (f e c) -> p h f e c", f=2, e=2)[:, :, :, e, :]
                ang = [rot[:, f, t, 32:64].rearrange("p (f c) -> p f c", f=2).unsqueeze(1).broadcast_to([P, n, 2, 16])
                       for f in (1, 0)]
                rope(quarter(dst, 0), quarter(dst, 1), quarter(src, 0), quarter(src, 1), *ang,
                     room[:, 0:32 * n].rearrange("p (h f c) -> p h f c", f=2, c=16))

            def twice(dst, src):
                d = dst.rearrange("p (h e c) -> p h e c", e=2, c=HD)
                done(dve.tensor_copy(d, src.unsqueeze(2).broadcast_to([P, KVH, 2, HD])))

            def branch(br):
                q0, k0, x0 = 768 * br, 768 * br + 512, 256 * br
                kn, qn = (("kA", "qA"), ("kB", "qB"))[br]
                for t in range(T):
                    rope_2d(heads(work[:, t, 512:640], KVH), heads(qkv[:, t, k0:k0 + 128], KVH), KVH, t, work[:, t, 640:1024])
                    twice(kdup[:, 2 * br, t, :], heads(work[:, t, 512:640], KVH))
                    twice(kdup[:, 2 * br + 1, t, :], heads(kvx[:, t, x0:x0 + 128], KVH))
                dve.sem_inc(ev(f"{kn}_normed"), 1)
                for t in range(T):
                    src = heads(qkv[:, t, q0:q0 + 512], HEADS)
                    rope_2d(heads(work[:, t, 0:512], HEADS), src, HEADS, t, work[:, t, 640:1024])
                    done(dve.tensor_copy(src, heads(work[:, t, 0:512], HEADS)))
                dve.sem_inc(ev(f"{qn}_normed"), 1)

            branch(0)
            inverse("ab", stat[:, 2:4, :])
            for v, s, gain in normed:
                done(dve.tensor_tensor(v, v, spread(s, HD), ALU.mult))
                done(dve.tensor_tensor(v, v, GAIN[gain].unsqueeze(1).broadcast_to([P, v.shape[1], HD]), ALU.mult))
            branch(1)

            def ab_step(i):
                return i // (HEADS * T), i % (HEADS * T) // T, i % T

            def ab_maxima(i, s, bank):
                br, h, t = ab_step(i)
                if br == 0:
                    far = bank[:, P * (1 - t):P * (1 - t) + P]
                    done(dve.tensor_tensor(far, far, (keep_past if t == 0 else keep_next)[:], ALU.add))
                done(dve.tensor_reduce(s[:, 0:1], bank[:], AX.X, ALU.max))
                if br == 0:
                    done(dve.tensor_scalar(s[:, 0:1], s[:, 0:1], HD ** -0.5, None, ALU.mult))
                    done(dve.tensor_tensor(s[:, 0:1], s[:, 0:1], GAIN["attn_sink_2"][:, h:h + 1], ALU.max))
                    return neg(s, 1, 1.0)
                return neg(s, 1, HD ** -0.5)

            def ab_sums(i, s):
                if ab_step(i)[0] == 0:
                    done(dve.tensor_tensor(s[:, 4:5], s[:, 4:5], s[:, 6:7], ALU.add))
                done(dve.reciprocal(s[:, 8:9], s[:, 4:5]))

            def ab_weigh(i, r, bank):
                br, h, t = ab_step(i)
                c = 512 * br + HD * h
                return dve.tensor_scalar(oab[:, t, c:c + HD], bank[:, 0:HD], r[:, 0:1], None, ALU.mult)

            def ab_after(i):
                if i % 8 == 7:
                    c = i // 8
                    biased(f"IN{3 + c}", gate2[:, :, COLS * c:COLS * c + COLS])

            u0 = PLAN.unit["IN3"]
            attend("AB", 2 * HEADS * T, ab_maxima, ab_sums, ab_weigh, lambda i: u0 + i // 2,
                   lambda i: u0 + min(i // 2 + 1, 16), ab_after)
            lt_dve("oab", ltb)
            dve.wait_ge(gate_sig, 6 + 4)
            for br in range(2):
                for c in range(2):
                    name, part = f"B{'AB'[br]}{c}", slice(COLS * c, COLS * c + COLS)
                    p = panel_wait(name)
                    g = gate2[:, :, D * br + COLS * c:D * br + COLS * c + COLS]
                    if br == 0:
                        frees(name, dve.tensor_tensor(ym[:, :, part], p[:], g, ALU.mult))
                    else:
                        frees(name, dve.tensor_tensor(g, p[:], g, ALU.mult))
                        done(dve.tensor_tensor(ym[:, :, part], ym[:, :, part], g, ALU.add))
            dve.sem_inc(ev("ym_ready"), 1)
            lt_dve("ym", lta)

            def gated_residual(name, src, first):
                for g in range(2):
                    if g == 1:
                        b, k = T_USE[f"{name}.0"]
                        dve.wait_ge(t_full[b], k + 1)
                    for j in range(4):
                        done(dve.tensor_scalar(diag[:, j, :], ident[:], modc[:, first + 4 * g + j:first + 4 * g + j + 1],
                                               None, ALU.mult))
                    dve.sem_inc(ev(f"{name}_diag"), 1)
                for g in range(2):
                    part = slice(COLS * g, COLS * g + COLS)
                    evacuated(f"{src}{g}")
                    b, k = T_USE[f"{name}.{g}"]
                    dve.wait_ge(t_full[b], k + 1)
                    done(dve.tensor_tensor(work[:, :, part], work[:, :, part],
                                           tb[b][:].unsqueeze(1).broadcast_to([P, T, COLS]), ALU.mult))
                    dve.sem_inc(t_free[b], 1)
                    done(dve.scalar_tensor_tensor(x[:, :, part], x[:, :, part], ALPHA, work[:, :, part], ALU.mult,
                                                  ALU.add))

            def layer_norm(name, each):
                for t in range(T):
                    done(dve.tensor_reduce(stat[:, 1, t:t + 1], x[:, t, :], AX.X, ALU.add))
                done(dve.tensor_scalar(stat[:, 1, 2:4], stat[:, 1, 0:2], 1.0 / D, None, ALU.mult))
                for t in range(T):
                    done(dve.tensor_scalar(x[:, t, :], x[:, t, :], stat[:, 1, 2 + t:3 + t], None, ALU.subtract))
                    done(dve.tensor_tensor_reduce(work[:, t, :], x[:, t, :], x[:, t, :], 1.0, 0.0, ALU.mult, ALU.add,
                                                  stat[:, 1, 4 + t:5 + t]))
                var(stat[:, 1, 4:6], D, LN_EPS).then_inc(ev(f"{name}_var"), 1)
                inverse(name, stat[:, 1, 4:6])
                dve.wait_ge(ev(f"{name}_landed"), 32)
                for t in range(T):
                    done(dve.scalar_tensor_tensor(x[:, t, :], x[:, t, :], stat[:, 1, 4 + t:5 + t], lnrow[:, 0], ALU.mult,
                                                  ALU.mult))
                    done(dve.tensor_tensor(x[:, t, :], x[:, t, :], lnrow[:, 1], ALU.add))
                    dve.sem_inc(ev(each), 1)

            ahead(PLAN.unit["UP0"])
            gated_residual("gate1", "OUT", 16)
            layer_norm("ln1", "x3_ready")
            dve.sem_inc(ev("ln1_done"), 1)
            lt_dve("x3", ltb, modc[:, 32:40], modc[:, 24:32])

            def taps(c, i=None):
                v = ccol[:].rearrange("p v (g f) -> p v g f", g=2)
                v = v[:, :, :, 2 * c:2 * c + 2] if i is None else v[:, :, :, bass.ds(4 * i + 2 * c, 2)]
                dve.tensor_copy(tap[:].rearrange("p v (g f) -> p v g f", g=2), v).then_inc(ev("tap_ready"), 1)

            def conv_taps(c, i=None):
                d = i if i is not None else 0
                for j in range(4):
                    b, _ = T_USE[f"UP{c}.{j // 2}"]
                    u = tb[b][:, 256 * (j % 2):256 * (j % 2) + 256]
                    if j % 2 == 0:
                        dve.wait_ge(conv_lin, 4 * c + j + 2 + 8 * d)
                    done(dve.scalar_tensor_tensor(conv[:, j, 1:SEQ], u[:, 0:SEQ - 1], tap[:, 0, j:j + 1],
                                                  conv[:, j, 1:SEQ], ALU.mult, ALU.add))
                    done(dve.scalar_tensor_tensor(conv[:, j, 0:SEQ - 1], u[:, 1:SEQ], tap[:, 2, j:j + 1],
                                                  conv[:, j, 0:SEQ - 1], ALU.mult, ALU.add))
                    if j % 2 == 1:
                        dve.sem_inc(t_free[b], 1)
                done(dve.tensor_tensor(conv[:, 2:4], conv[:, 0:2], conv[:, 2:4], ALU.mult))
                dve.wait_ge(conv_sig, c + 1 + 2 * d)
                done(dve.tensor_tensor(conv[:, 2:4], conv[:, 2:4], sig[:], ALU.mult))
                dve.sem_inc(ev("conv_prod"), 1)

            def conv_lo(c, i=None):
                d = i if i is not None else 0
                dve.wait_ge(ev("conv_hi"), c + 1 + 2 * d)
                hi, lo = (v[:, 2 * c:2 * c + 2, :] if i is None else v[:, bass.ds(4 * i + 2 * c, 2), :] for v in actT)
                dve.tensor_tensor(lo, conv[:, 2:4], hi.bitcast(F32), ALU.subtract).then_inc(conv_mul, 1)
                dve.wait_ge(conv_mul, c + 1 + 2 * d)

            ahead(PLAN.unit["UP1"])
            u0 = PLAN.unit["UP1"]
            assert cursor[0] == u0 + AHEAD
            with dve.Fori(0, 5) as i:
                order.enter(i, 20)
                for c in (1, 2):
                    taps(c - 1, i)
                    for k in range(4):
                        split(u0 + 4 * (c - 1) + k + AHEAD, i, 8)
                        if k == 1:
                            conv_taps(c - 1, i)
                        if k == 2:
                            conv_lo(c - 1, i)
                order.leave(5)
            cursor[0] += 40
            taps(10)
            ahead(PLAN.unit["DN0"] + 2)
            conv_taps(10)
            conv_lo(10)
            ahead(PLAN.units)
            gated_residual("gate2", "DN", 40)
            layer_norm("ln2", "y_ready")


_INS = ["x", "mem", "positions", "g_mix", "w_in", "b_gate", "g_ckv", "w_ukv", "g_q_nope", "g_k_nope", "g_q_rope",
        "g_k_rope", "w_gla_gate", "b_gla_gate", "g_gla_out", "g_mem", "w_mem_kv", "g_q_mem", "g_k_mem", "w_o", "g_ffn",
        "w_up", "w_down", "c_2", "ctx_2", "c_ctx_2", "w_mod_2", "b_mod_2", "w_in_2", "b_in_2", "attn_sink_2",
        "q_norm_g_2", "k_norm_g_2", "w_branch_a_2", "w_branch_b_2", "w_out_2", "ln1_g_2", "ln1_b_2", "w_up_2",
        "conv_w_2", "conv_b_2", "w_down_2", "ln2_g_2", "ln2_b_2"]


def build(nc, shapes):
    views = {}
    for name in _INS:
        shape, dt = shapes[name]
        v = nc.dram_tensor(f"in_{name}", shape, dt, kind="ExternalInput").ap()
        views[name] = v[0] if len(shape) > 1 and shape[0] == 1 else v
    out = nc.dram_tensor("out", (1, SEQ, D), F32, kind="ExternalOutput").ap()
    hybrid_kernel(nc, views, out[0])


def kernel(**inputs):
    import concourse.bacc as bacc
    from concourse.bass_utils import run_bass_kernel_spmd

    nc = bacc.Bacc("TRN2", target_bir_lowering=False, num_devices=1)
    arrays = {f"in_{name}": np.ascontiguousarray(inputs[name]) for name in _INS}
    build(nc, {name: (arrays[f"in_{name}"].shape, mybir.dt.from_np(arrays[f"in_{name}"].dtype)) for name in _INS})
    r = run_bass_kernel_spmd(nc, [arrays], core_ids=[0])
    return r.results[0]["out"]
```

```python
from contextlib import ExitStack

import numpy as np

import concourse.bass as bass
import concourse.mybir as mybir

F32 = mybir.dt.float32
F32R = mybir.dt.float32r
I32 = mybir.dt.int32
I8 = mybir.dt.int8
ALU = mybir.AluOpType
ACT = mybir.ActivationFunctionType
AX = mybir.AxisListType

P = 128
D = 1024
SEQ = 256
T = SEQ // P
KT = D // P
NEG = -1e30
EPS = 1e-6

H_MLA, NOPE, ROPE, V_MLA, KV_RANK = 8, 128, 64, 128, 256
H_GLA, DK_GLA, DV_GLA, GATE_RANK = 4, 128, 256, 16
H_MEM, DQ_MEM, DV_MEM = 4, 64, 256
D_FF = 4 * D
WIDTHS = dict(q=H_MLA * (NOPE + ROPE), ck=KV_RANK + ROPE, gq=H_GLA * DK_GLA, gk=H_GLA * DK_GLA,
              gv=H_GLA * DV_GLA, a=GATE_RANK, r=H_GLA * DV_GLA, qm=H_MEM * DQ_MEM, gates=3 * D)
COL = {}
for _name, _w in WIDTHS.items():
    COL[_name] = sum(WIDTHS[n] for n in list(WIDTHS)[:list(WIDTHS).index(_name)])
HEADS, KVH, HD = 8, 2, 64
GROUP = HEADS // KVH
FF2 = 2816
FT2 = FF2 // P
GRID_W = 64
ALPHA = 2.0 ** 0.25
LN_EPS = 1e-5

RING = 4
UNIT = 2
COLS = 512
AHEAD = 3


class Order:

    def __init__(self, eng, sem):
        self.eng, self.sem, self.n, self.i, self.per = eng, sem, 0, None, 0

    def done(self, ins):
        self.n += 1
        ins.then_inc(self.sem, 1)
        self.eng.wait_ge(self.sem, self.n if self.i is None else self.n + self.per * self.i)

    def enter(self, i, per):
        self.i, self.per, self.n0 = i, per, self.n

    def leave(self, times):
        assert self.n - self.n0 == self.per, (self.n - self.n0, self.per)
        self.n += self.per * (times - 1)
        self.i = None


def panels():
    out = [(f"MK{c}", KT, 1) for c in range(3)]
    out += [("AQ", KT, 2)]
    out += [(n, KT, 1) for n in ("CK", "GQ", "GK", "V0", "V1", "R0", "R1", "Q0", "Q1", "Q2", "G20", "G21")]
    out += [(f"UKV{c}", KV_RANK // P, 1) for c in range(4)]
    out += [(f"G{b}{c}", KT, 1) for b in (1, 0) for c in range(2)]
    out += [("WO0", KT, 1), ("WO1", KT, 1), ("CX", KT, 2)]
    out += [(f"WU{c}", KT, 1) for c in range(D_FF // COLS)]
    out += [("WD0", D_FF // P, 1), ("WD1", D_FF // P, 1)]
    out += [(f"IN{c}", KT, 1) for c in range(7)]
    out += [("BA0", KT // 2, 1), ("BA1", KT // 2, 1), ("BB0", KT // 2, 1), ("BB1", KT // 2, 1)]
    out += [("OUT0", KT, 1), ("OUT1", KT, 1)]
    out += [(f"UP{c}", KT, 2) for c in range(FF2 // (COLS // 2))]
    out += [("DN0", FT2, 2), ("DN1", FT2, 2)]
    return out


NARROW = dict(MK0=H_MEM * DQ_MEM, AQ=GATE_RANK + H_MEM * DQ_MEM, CK=KV_RANK + ROPE)


class Plan:

    def __init__(self):
        self.no, self.unit, self.landed, self.cols = {}, {}, [], []
        loads = [0] * RING
        for i, (name, kts, per_unit) in enumerate(panels()):
            self.no[name], self.unit[name] = i, len(self.landed)
            for u in range(len(self.landed), len(self.landed) + kts // UNIT):
                loads[u % RING] += 16 * per_unit
                self.landed.append(loads[u % RING])
                self.cols.append(NARROW.get(name, COLS))
        self.units = len(self.landed)

    def bank(self, name):
        return self.no[name] % 2, self.no[name] // 2


PLAN = Plan()


def uses(names, banks=2):
    return {n: (i % banks, i // banks) for i, n in enumerate(names)}


def t_names():
    g = lambda n, k: [f"{n}.{i}" for i in range(k)]
    mod = lambda first, n: [f"{v}.{c}" for c in range(first, first + n) for v in ("mod", "modt")]
    out = g("vec", 3) + g("me", 4) + g("h", 4) + ["aT", "z.0", "z.1", "mqT", "mkT", "ck"]
    out += attention_t("MEM", H_MEM)
    out += g("gqT", 2) + g("gkT", 2) + mod(0, 4) + g("go", 4) + ["mod.4", "modt.4", "mod.5", "modt.5"]
    out += ["qn.0", "qn.1", "qn.2", "qn.3", "qr.0", "qr.1", "kp"] + g("kn", 4)
    out += attention_t("MLA", H_MLA)
    out += ["mod.6"] + g("y", 4) + ["modt.6", "mod.7"] + g("hc", 4) + ["modt.7"] + g("h2", 4)
    out += [f"WU{c}.{i}" for c in range(8) for i in range(2)]
    out += ["mod.8"] + g("x2", 4) + ["modt.8", "mod.9"] + g("kA", 2) + ["modt.9", "mod.10"] + g("qA", 2)
    out += ["modt.10", "mod.11"] + g("kB", 2) + ["modt.11"] + g("qB", 2)
    out += attention_t("AB", 2 * HEADS * T)
    out += g("oab", 4) + g("ym", 4) + g("gate1", 2) + g("x3", 4)
    out += [f"UP{c}.{i}" for c in range(11) for i in range(2)]
    out += g("gate2", 2)
    return out


def attention_t(name, n, extra=()):
    out = []
    for i in range(n + 1):
        if i < n:
            out.append(f"{name}.PT{i}")
        if i >= 1:
            out.append(f"{name}.O{i - 1}")
        out += extra[i:i + 1]
    return out


T_USE = uses(t_names())
S_USE = uses([f"MEM.{i}" for i in range(H_MEM)] + ["gla.0.0", "gla.0.1", "gla.off"]
             + [f"gla.{s}.{t}" for s in range(1, 8) for t in range(T)]
             + [f"MLA.{i}" for i in range(H_MLA)] + [f"AB.{i}" for i in range(2 * HEADS * T)])
LT_ORDER = ["me", "h", "y", "hc", "h2", "x2", "oab", "ym", "x3"]


def hybrid_kernel(nc, a, out):
    ctx = ExitStack()
    with ctx:
        def sem(name):
            return ctx.enter_context(nc.semaphore(name))

        def sb(name, shape, dt=F32, scope=ctx):
            return scope.enter_context(nc.sbuf_tensor(name, shape, dt))

        acc = [ctx.enter_context(nc.psum_tensor(f"acc{i}", [P, T, COLS], F32)) for i in range(2)]
        tb = [ctx.enter_context(nc.psum_tensor(f"turned{i}", [P, COLS], F32)) for i in range(2)]
        sc = [ctx.enter_context(nc.psum_tensor(f"scores{i}", [P, COLS], F32)) for i in range(2)]

        raw = sb("raw", [P, RING, UNIT, COLS])
        whi = sb("whi", [P, RING, UNIT, COLS], F32R)
        wlo = sb("wlo", [P, RING, UNIT, COLS], F32R)
        x = sb("x_res", [P, T, D])
        lta = [sb(f"lta_{n}", [P, KT, SEQ], F32R) for n in ("hi", "lo")]
        ident = sb("ident", [P, P])
        keep_past = sb("keep_past", [P, P])
        keep_next = sb("keep_next", [P, P])
        vcol = sb("vcol", [P, 96])
        ccol = sb("ccol", [P, 4, 2 * FT2])
        modc = sb("modc", [P, 48])
        modx = sb("modx", [P, 16])
        sic = sb("sic", [P, 16])
        rot = sb("rot", [P, 2, T, 64])
        bias = sb("bias", [P, 2, COLS])
        wm = sb("wm", [P, KT // UNIT, UNIT, COLS])
        modrow = sb("modrow", [2, COLS])
        turn = sb("turn", [P, 2, COLS])
        prob = sb("prob", [P, 2, COLS])
        probT = sb("probT", [P, 2, COLS])
        work = sb("work", [P, T, D])
        stat = sb("stat", [P, 8, 16])
        soft = sb("soft", [P, 2, 10])
        gains = sb("gains", [P, 6 * 64 + DV_GLA + HEADS])

        ROWS, at = {}, 0
        for name, n in (("g_mix", 8), ("g_mem", 8), ("g_ffn", 8), ("g_ckv", 2), ("c_2", 8), ("c_ctx_2", 8),
                        ("g_q_nope", 1), ("g_k_nope", 1), ("b_gla_gate", 4), ("b_mod_2", 48)):
            ROWS[name] = (at, n)
            at += n
        assert at == 96

        def col(name, k=0, n=1):
            return vcol[:, ROWS[name][0] + k:ROWS[name][0] + k + n]

        GAIN, at = {}, 0
        for name, n in (("g_q_rope", 64), ("g_k_rope", 64), ("g_q_mem", 64), ("g_k_mem", 64), ("q_norm_g_2", 64),
                        ("k_norm_g_2", 64), ("g_gla_out", DV_GLA), ("attn_sink_2", HEADS)):
            GAIN[name] = gains[:, at:at + n]
            at += n

        one = ExitStack()
        arena = sb("arena", [P, 20736], F32, one)
        ckT = [sb(f"ckT_{n}", [P, 2, SEQ], F32R, one) for n in ("hi", "lo")]
        gmask = sb("gmask", [P, 7, P], I8, one)
        one.close()

        def ar(at, *shape):
            v = arena[:, at:at + int(np.prod(shape))]
            if len(shape) == 1:
                return v
            names = "abcd"[:len(shape)]
            return v.rearrange(f"p ({' '.join(names)}) -> p {' '.join(names)}", **dict(zip(names, shape)))

        o_mem = ar(0, T, D)
        r_gla = ar(2048, T, D)
        o_mla = ar(4096, T, D)
        gqT, gkT = ar(4096, H_GLA, SEQ), ar(5120, H_GLA, SEQ)
        mqT, mkT = ar(4096, 2, SEQ), ar(4608, 2, SEQ)
        decay = ar(6144, H_GLA, SEQ)
        eq, ek = ar(7168, 512), ar(7680, 512)
        rsig = ar(5120, T, COLS)
        angle, turns = ar(13312, T, 64), ar(13440, T, 64)
        q = ar(8192, T, 1536)
        kvm = ar(8192, T, 1280)
        kv = ar(11264, T, 2048)
        memx = ar(11264, T, D)
        attn = ar(11264, 3, H_GLA, P)
        og = ar(6144, T, H_GLA, DV_GLA)
        zb, ze = ar(11264, H_GLA, SEQ), ar(12288, H_GLA, SEQ)
        zflag = ar(13312, H_GLA * T, P)
        wg, aT = ar(14336, 512), ar(14848, SEQ)
        ck = ar(15360, T, 320)
        aq = ar(16000, T, 272)
        gv = ar(16544, T, D)
        gq, gk = ar(18592, T, 512), ar(19616, T, 512)
        gqd, gkd = ar(18592, H_GLA, SEQ), ar(19616, H_GLA, SEQ)
        qnT, knT = ar(15360, H_MLA, SEQ), ar(17408, H_MLA, SEQ)
        qrT, kpT = ar(19456, H_MLA // 2, SEQ), ar(20480, SEQ)
        kpe = work[:, 0, 512:768].rearrange("p (t c) -> p t c", t=T)
        room = ar(4096, T * H_MLA, NOPE)
        rope_sq = prob[:].rearrange("p a b -> p (a b)").rearrange("p (h c) -> p h c", c=ROPE)
        qh = ar(8192, T * H_MLA, NOPE + ROPE)
        kh = ar(11264, T * H_MLA, NOPE + V_MLA)[:, :, 0:NOPE]
        og_heads = ar(6144, T * H_GLA, DV_GLA)
        og_sq = probT[:].rearrange("p a b -> p (a b)").rearrange("p (h c) -> p h c", c=DV_GLA)
        vrow = [ar(4096 + 128 * i, 128) for i in range(3)]

        ltb = [sb(f"ltb_{n}", [P, KT, SEQ], F32R) for n in ("hi", "lo")]
        kvx = sb("kvx", [P, T, COLS])
        two = ExitStack()
        ff = [sb(f"ff_{n}", [P, D_FF // P, SEQ], F32R, two) for n in ("hi", "lo")]
        up = [prob, probT]
        two.close()
        three = ExitStack()
        qkv = sb("qkv", [P, T, 1536], F32, three)
        qT = [sb(f"qT_{b}", [P, HEADS // 2, SEQ], F32, three) for b in "ab"]
        kT = [sb(f"kT_{b}", [P, KVH, 2 * SEQ], F32, three) for b in "ab"]
        kdup = sb("kdup", [P, 4, T, KVH * 2 * HD], F32, three)
        gate2 = sb("gate2", [P, T, 2 * D], F32, three)
        oab = sb("oab", [P, T, D], F32, three)
        ym = work
        three.close()
        four = ExitStack()
        diag = sb("diag", [P, 4, P], F32, four)
        ones = sb("ones", [P, P], F32, four)
        lnrow = sb("lnrow", [P, 2, D], F32, four)
        actT = [sb(f"act_{n}", [P, FT2, SEQ], F32R, four) for n in ("hi", "lo")]
        upv = [prob, probT]
        conv = sb("conv", [P, 4, SEQ], F32, four)
        sig = sb("sig", [P, 2, SEQ], F32, four)
        tap = sb("tap", [P, 4, 4], F32, four)
        four.close()

        landed = [sem(f"weights_landed{i}") for i in range(RING)]
        hi_ready, split_ready, unit_used = sem("hi_ready"), sem("split_ready"), sem("unit_used")
        panel_out = [sem(f"panel_out{i}") for i in range(2)]
        t_full = [sem(f"turned_full{i}") for i in range(2)]
        t_free = [sem(f"turned_free{i}") for i in range(2)]
        s_full = [sem(f"scores_full{i}") for i in range(2)]
        s_free = [sem(f"scores_free{i}") for i in range(2)]
        lt_hi, lt_ready = sem("stationary_hi"), sem("stationary_ready")
        soft_ready = sem("maxima_ready")
        mod_landed = [sem(f"mod_landed{i}") for i in range(KT // UNIT)]
        mod_free = sem("mod_free")
        bias_landed = [sem(f"bias_landed{i}") for i in range(2)]
        bias_used = sem("bias_used")
        gate_in, gate_sig = sem("gate_in"), sem("gate_sigmoid")
        up_done, up_hi = sem("up_done"), sem("up_hi")
        conv_lin, conv_sig, conv_mul = sem("conv_lin"), sem("conv_sig"), sem("conv_mul")
        gla_exp, gla_in = sem("gla_exp"), sem("gla_in")
        act_order, dve_order, pool_order = sem("act_order"), sem("dve_order"), sem("pool_order")
        stored = sem("stored")
        once = {}

        def ev(name):
            if name not in once:
                once[name] = sem(name)
            return once[name]

        BIASED = ["G20", "G21", "G10", "G11", "G00", "G01", "CX"] + [f"IN{c}" for c in range(7)]
        STEPS = {"MEM": (0, H_MEM), "MLA": (H_MEM, H_MLA), "AB": (H_MEM + H_MLA, 2 * HEADS * T)}
        n_gate = {n: i for i, n in enumerate(BIASED)}

        def lt_done(name, g=3):
            return 4 * LT_ORDER.index(name) + g + 1

        block = ctx.enter_context(nc.Block())

        def rows(w, k):
            return w[k * UNIT * P:(k + 1) * UNIT * P, :].rearrange("(k p) n -> p k n", p=P)

        def loads_of(name, k):
            w, w2 = a["w_in"], a["w_in_2"]
            kind, c = name.rstrip("0123456789"), int("".join(ch for ch in name if ch.isdigit()) or 0)
            if kind == "MK":
                first, n = [(0, 256), (256, COLS), (256 + COLS, COLS)][c]
                return [(0, rows(a["w_mem_kv"], k)[:, :, first:first + n])]
            if kind == "AQ":
                return [(0, rows(w, k)[:, :, COL["a"]:COL["a"] + GATE_RANK]),
                        (GATE_RANK, rows(w, k)[:, :, COL["qm"]:COL["qm"] + 256])]
            if kind == "CX":
                return [(0, rows(w2, k)[:, :, 512:768]), (256, rows(w2, k)[:, :, 1280:1536])]
            if kind == "CK":
                return [(0, rows(w, k)[:, :, COL["ck"]:COL["ck"] + 320])]
            if kind == "G":
                first = COL["gates"] + (c // 10) * D + (c % 10) * COLS
                return [(0, rows(w, k)[:, :, first:first + COLS])]
            where = {"GQ": (w, COL["gq"]), "GK": (w, COL["gk"]), "V": (w, COL["gv"]), "R": (w, COL["r"]),
                     "Q": (w, COL["q"]), "UKV": (a["w_ukv"], 0), "WO": (a["w_o"], 0), "WU": (a["w_up"], 0),
                     "WD": (a["w_down"], 0), "IN": (w2, 0), "BA": (a["w_branch_a_2"], 0),
                     "BB": (a["w_branch_b_2"], 0), "OUT": (a["w_out_2"], 0)}
            src, first = where[kind]
            return [(0, rows(src, k)[:, :, first + c * COLS:first + (c + 1) * COLS])]

        def units_of(name):
            names = list(PLAN.unit)
            i = names.index(name)
            return (PLAN.unit[names[i + 1]] if i + 1 < len(names) else PLAN.units) - PLAN.unit[name]

        @block.sync
        def _(sp):
            sp.dma_start(memx, a["mem"].rearrange("(t p) d -> p t d", p=P)).then_inc(ev("mem_landed"), 16)
            sp.dma_start(x[:], a["x"].rearrange("(t p) d -> p t d", p=P)).then_inc(ev("x_landed"), 16)

            def bias_load(name):
                n = n_gate[name]
                sp.wait_ge(bias_used, n + 1)
                if name == "CX":
                    for j, first in enumerate((512, 1280)):
                        sp.dma_start(bias[:, n % 2, 256 * j:256 * j + 256],
                                     a["b_in_2"][first:first + 256].partition_broadcast(P))\
                          .then_inc(bias_landed[n % 2], 16)
                    return
                src = a["b_in_2"][int(name[2:]) * COLS:][:COLS] if name.startswith("IN") else \
                    a["b_gate"][int(name[1]) * D + int(name[2]) * COLS:][:COLS]
                sp.dma_start(bias[:, n % 2], src.partition_broadcast(P)).then_inc(bias_landed[n % 2], 16)

            def panel(name):
                for k in range(units_of(name)):
                    u = PLAN.unit[name] + k
                    if k == units_of(name) - 1 and name in n_gate:
                        bias_load(name)
                    sp.wait_ge(split_ready, u + 1)
                    if name.startswith("DN"):
                        for kk in range(UNIT):
                            r = (UNIT * k + kk) * P
                            sp.dma_start(raw[:, u % RING, kk], a["w_down_2"][r:r + P, COLS * int(name[2]):][:, 0:COLS])\
                              .then_inc(landed[u % RING], 16)
                        continue
                    for first, src in loads_of(name, k):
                        sp.dma_start(raw[:, u % RING, :, first:first + src.shape[2]], src)\
                          .then_inc(landed[u % RING], 16)

            for name in PLAN.no:
                if name.startswith("WU"):
                    if name == "WU0":
                        u0 = PLAN.unit[name]
                        with sp.Fori(0, D_FF // COLS) as c:
                            for k in range(KT // UNIT):
                                sp.wait_ge(split_ready, u0 + k + 1 + 4 * c)
                                sp.dma_start(raw[:, (u0 + k) % RING],
                                             rows(a["w_up"], k)[:, :, bass.ds(COLS * c, COLS)])\
                                  .then_inc(landed[(u0 + k) % RING], 16)
                elif name.startswith("UP"):
                    if name == "UP0":
                        u0 = PLAN.unit[name]
                        with sp.Fori(0, FF2 // 256) as c:
                            for k in range(KT // UNIT):
                                sp.wait_ge(split_ready, u0 + k + 1 + 4 * c)
                                for e in range(2):
                                    sp.dma_start(raw[:, (u0 + k) % RING, :, 256 * e:256 * e + 256],
                                                 rows(a["w_up_2"], k)[:, :, bass.ds(FF2 * e + 256 * c, 256)])\
                                      .then_inc(landed[(u0 + k) % RING], 16)
                else:
                    panel(name)
                if name == "G00":
                    b, k = T_USE["qr.1"]
                    sp.wait_ge(t_full[b], k + 1)
                    sp.dma_start(ar(8192, T, D), a["ctx_2"].rearrange("(t p) d -> p t d", p=P))\
                      .then_inc(ev("ctx_landed"), 16)
                if name == "OUT1":
                    b, k = T_USE["ym.3"]
                    sp.wait_ge(t_full[b], k + 1)
                    for i, v in enumerate(("ln1_g_2", "ln1_b_2")):
                        sp.dma_start(lnrow[:, i], a[v].partition_broadcast(P)).then_inc(ev("ln1_landed"), 16)
                if name == "UP10":
                    sp.wait_ge(ev("ln1_done"), 1)
                    for i, v in enumerate(("ln2_g_2", "ln2_b_2")):
                        sp.dma_start(lnrow[:, i], a[v].partition_broadcast(P)).then_inc(ev("ln2_landed"), 16)

            for t in range(T):
                sp.wait_ge(ev("y_ready"), t + 1)
                sp.dma_start(out[t * P:(t + 1) * P, :], x[:, t, :]).then_inc(stored, 16)
            sp.wait_ge(stored, 16 * T)

        @block.gpsimd
        def _(pool):
            order = Order(pool, pool_order)
            for m, fill in ((ident, 0.0), (keep_past, 0.0), (keep_next, 0.0), (gmask, 0)):
                ins = pool.memset(m[:], fill)
            order.done(ins)
            pool.affine_select(out=ident[:], in_=ident[:], compare_op=ALU.not_equal, fill=1.0, base=0,
                               pattern=[[-1, P]], channel_multiplier=1).then_inc(ev("ident_ready"), 1)
            pool.affine_select(out=keep_past[:], in_=keep_past[:], compare_op=ALU.is_ge, fill=NEG, base=0,
                               pattern=[[-1, P]], channel_multiplier=1)
            pool.affine_select(out=keep_next[:], in_=keep_next[:], compare_op=ALU.is_ge, fill=NEG, base=0,
                               pattern=[[1, P]], channel_multiplier=-1).then_inc(ev("keeps_ready"), 1)
            freq = ar(13568, 64)
            for i in range(32):
                f = np.float32(1.0) / (np.float32(10000.0) ** np.float32(2 * i / np.float32(ROPE)))
                pool.memset(freq[:, i:i + 1], float(np.float32(f)))
            for i in range(16):
                f = np.float32(10000.0) ** (-np.float32(i) / np.float32(16))
                ins = pool.memset(freq[:, 32 + i:64:16], float(np.float32(f)))
            order.done(ins)
            for half in range(2):
                lane = slice(64 * half, 64 * half + 64)
                for t in range(T):
                    order.done(pool.memset(stat[lane, 7, t:t + 1], float(2 * t + half)))
                order.done(pool.iota(stat[lane, 7, 2:3].bitcast(I32), pattern=[[0, 1]], base=0, channel_multiplier=1))
            pool.sem_inc(ev("grid_ready"), 1)
            for n, s in enumerate((64, 32, 16, 8, 4, 2, 1)):
                odd = gmask[:, n, :].rearrange("p (m e w) -> p m e w", e=2, w=s)[:, :, 1, :]
                order.done(pool.memset(odd, 1))
                order.done(pool.affine_select(out=odd, in_=odd, compare_op=ALU.is_ge, fill=0.0, base=0,
                                              pattern=[[-2 * s, P // (2 * s)], [0, s]], channel_multiplier=1))
                ins = pool.affine_select(out=odd, in_=odd, compare_op=ALU.is_ge, fill=0.0, base=s - 1,
                                         pattern=[[2 * s, P // (2 * s)], [0, s]], channel_multiplier=-1)
                if n < 6:
                    order.done(ins)
            ins.then_inc(ev("gmask_ready"), 1)
            with pool.Fori(0, 6 * D // COLS) as c:
                for k in range(KT // UNIT):
                    pool.wait_ge(mod_free, 4 * c + k + 1)
                    pool.dma_start(wm[:, k], rows(a["w_mod_2"], k)[:, :, bass.ds(COLS * c, COLS)])\
                        .then_inc(mod_landed[k], 16)
            b, k = T_USE["ym.3"]
            pool.wait_ge(t_full[b], k + 1)
            pool.memset(ones[:], 1.0).then_inc(ev("ones_ready"), 1)

        @block.tensor
        def _(pe):
            pe.sem_inc(unit_used, RING)

            def unit(name, k, lhs, n=COLS, first_kt=None, i=None, per=0):
                u, (s, cnt) = PLAN.unit[name] + k, PLAN.bank(name)
                du, dc = (per * i, per // 8 * i) if i is not None else (0, 0)
                kt0 = UNIT * k if first_kt is None else first_kt
                last = k == units_of(name) - 1
                if k == 0:
                    pe.wait_ge(panel_out[s], cnt + 1 + dc)
                pe.wait_ge(split_ready, RING + u + 1 + du)
                for t in range(T):
                    for kk in range(UNIT):
                        tok = slice(t * P, (t + 1) * P)
                        pairs = [(1, whi), (0, whi), (0, wlo)]
                        for j, (part, w) in enumerate(pairs):
                            ins = pe.matmul(acc[s][:, t, 0:n], lhs[part][:, kt0 + kk, tok], w[:, u % RING, kk, 0:n],
                                            start=(k == 0 and kk == 0 and j == 0),
                                            stop=(last and kk == UNIT - 1 and j == 2))
                ins.then_inc(unit_used, 1)

            def panel(name, lhs, n=COLS, new=None):
                for k in range(units_of(name)):
                    if new:
                        lt_wait(new, k)
                    unit(name, k, lhs, n)

            def t_begin(name):
                b, k = T_USE[name]
                pe.wait_ge(t_free[b], k + 1)
                return tb[b], t_full[b]

            def turn_tokens(name, src, kts=KT, ready=None):
                for g in range(kts // 2):
                    if ready and g % 2 == 0:
                        pe.wait_ge(ev(ready), g // 2 + 1)
                    bank, full = t_begin(f"{name}.{g}" if kts > 2 else name)
                    for kk in range(2):
                        for t in range(T):
                            c = P * (2 * g + kk)
                            ins = pe.transpose(bank[:, 256 * kk + P * t:256 * kk + P * t + P],
                                               src[:, t, c:c + P], ident[:])
                    ins.then_inc(full, 1)

            def s_begin(name):
                b, k = S_USE[name]
                pe.wait_ge(s_free[b], k + 1)
                return sc[b], s_full[b]

            def attend(name, n, scores, blocks, values, fill_a=None, fill_b=None, after=None):
                def score(i):
                    bank, full = s_begin(f"{name}.{i}")
                    scores(i, bank).then_inc(full, 1)

                score(0)
                for i in range(n + 1):
                    if i + 1 < n:
                        score(i + 1)
                    if i < n:
                        if fill_a:
                            fill_a(i)
                        b, k = S_USE[f"{name}.{i}"]
                        pe.wait_ge(s_free[b], k + 2)
                        bank, full = t_begin(f"{name}.PT{i}")
                        for j in range(blocks):
                            ins = pe.transpose(bank[:, P * j:P * j + P],
                                               prob[:, (STEPS[name][0] + i) % 2, P * j:P * j + P], ident[:])
                        ins.then_inc(full, 1)
                        if fill_b:
                            fill_b(i)
                    if i >= 1:
                        b, k = T_USE[f"{name}.PT{i - 1}"]
                        pe.wait_ge(t_free[b], k + 2)
                        bank, full = t_begin(f"{name}.O{i - 1}")
                        values(i - 1, bank, probT[:, (STEPS[name][0] + i - 1) % 2, :]).then_inc(full, 1)
                    if after:
                        after(i)

            def mod_panel(c):
                bank, full = t_begin(f"mod.{c}")
                if c == 0:
                    pe.wait_ge(ev("sic_ready"), 1)
                pe.wait_ge(mod_free, 4 * c + 4)
                for k in range(KT // UNIT):
                    pe.wait_ge(mod_landed[k], 16 * (c + 1))
                    for kk in range(UNIT):
                        kt = UNIT * k + kk
                        ins = pe.matmul(bank[0:2, :], sic[:, kt:kt + KT + 1:KT], wm[:, k, kk],
                                        start=(kt == 0), stop=(kt == KT - 1))
                    ins.then_inc(mod_free if kt < KT - 1 else full, 1)

            def mod_turn(c):
                b, k = T_USE[f"mod.{c}"]
                pe.wait_ge(t_free[b], k + 2)
                bank, full = t_begin(f"modt.{c}")
                for j in range(4):
                    ins = pe.transpose(bank[:, 2 * j:2 * j + 2], modrow[:, P * j:P * j + P], ident[0:2, 0:2])
                ins.then_inc(full, 1)

            def lt_wait(name, g=3):
                pe.wait_ge(lt_ready, lt_done(name, g))

            pe.wait_ge(ev("ident_ready"), 1)
            pe.wait_ge(ev("rows_landed"), 16 * 14)
            for g, n in enumerate((96, 4 * FT2, 4 * FT2)):
                bank, full = t_begin(f"vec.{g}")
                pe.transpose(bank[:, 0:n], vrow[g][0:n, :], ident[0:n, 0:n]).then_inc(full, 1)

            pe.wait_ge(ev("me_scaled"), T)
            turn_tokens("me", work)
            panel("MK0", lta, 256, new="me")
            panel("MK1", lta)
            panel("MK2", lta)
            pe.wait_ge(ev("h_scaled"), T)
            turn_tokens("h", work)

            panel("AQ", lta, NARROW["AQ"], new="h")
            panel("CK", lta, NARROW["CK"])
            s, k = PLAN.bank("AQ")
            pe.wait_ge(panel_out[s], k + 2)
            bank, full = t_begin("aT")
            for t in range(T):
                ins = pe.transpose(bank[:, P * t:P * t + P], aq[:, t, 0:P], ident[:])
            ins.then_inc(full, 1)
            panel("GQ", lta)
            b, k = T_USE["aT"]
            pe.wait_ge(t_free[b], k + 2)
            pe.wait_ge(ev("wg_landed"), 16)
            for g in range(2):
                bank, full = t_begin(f"z.{g}")
                for j in range(2):
                    h = 2 * g + j
                    ins = pe.matmul(bank[:, 256 * j:256 * j + 256], wg[0:GATE_RANK, P * h:P * h + P],
                                    aT[0:GATE_RANK, :], start=True, stop=True)
                ins.then_inc(full, 1)
            panel("GK", lta)
            panel("V0", lta)

            for name, src in (("mqT", aq[:, :, GATE_RANK:272]), ("mkT", kvm[:, :, 0:256])):
                pe.wait_ge(ev(f"{name}_normed"), 1)
                turn_tokens(name, src, 2)
            pe.wait_ge(ev("ck_normed"), 1)
            turn_tokens("ck", ck, 2)
            for name in ("mqT", "mkT"):
                b, k = T_USE[name]
                pe.wait_ge(t_free[b], k + 2)

            def mem_scores(h, bank):
                lane = slice(64 * (h % 2), 64 * (h % 2) + 64)
                for t in range(T):
                    ins = pe.matmul(bank[:, 256 * t:256 * t + 256], mqT[lane, h // 2, P * t:P * t + P],
                                    mkT[lane, h // 2, :], start=True, stop=True)
                return ins

            def mem_values(h, bank, pT):
                for t in range(T):
                    for kt in range(T):
                        ins = pe.matmul(bank[:, 256 * t:256 * t + 256], pT[:, 256 * t + P * kt:256 * t + P * kt + P],
                                        kvm[:, kt, 256 + 256 * h:512 + 256 * h], start=(kt == 0), stop=(kt == T - 1))
                return ins

            def fill(names, first, n):
                for j in range(first, first + n):
                    unit(names[j // 4], j % 4, lta)

            vr = ["V1", "R0", "R1", "Q0"]
            attend("MEM", H_MEM, mem_scores, 4, mem_values, lambda i: fill(vr, 4 * i, 2),
                   lambda i: fill(vr, 4 * i + 2, 2))

            for name, src in (("gqT", gq), ("gkT", gk)):
                turn_tokens(name, src, 4)
            for g in ("gqT.0", "gqT.1", "gkT.0", "gkT.1"):
                b, k = T_USE[g]
                pe.wait_ge(t_free[b], k + 2)
            qg = ["Q1", "Q2", "G20", "G21"]
            for s in range(9):
                lhs, rhs = (gkT, gqT) if s == 0 else (gkd, gqd)
                if s >= 1:
                    pe.wait_ge(gla_in, s)
                if s == 1:
                    bank, full = s_begin("gla.off")
                    for h in range(H_GLA):
                        ins = pe.matmul(bank[:, P * h:P * h + P], lhs[:, h, 0:P], rhs[:, h, P:2 * P],
                                        start=True, stop=True)
                    ins.then_inc(full, 1)
                else:
                    for t in range(T):
                        bank, full = s_begin(f"gla.{max(s - 1, 0)}.{t}")
                        for h in range(H_GLA):
                            tok = slice(P * t, P * t + P)
                            ins = pe.matmul(bank[:, P * h:P * h + P], lhs[:, h, tok], rhs[:, h, tok],
                                            start=True, stop=True)
                        ins.then_inc(full, 1)
                if s < 8:
                    fill(qg, 2 * s, 2)
                if s % 2 == 1:
                    mod_panel(s // 2)
                elif s >= 2:
                    mod_turn(s // 2 - 1)
            for name in ("gla.off", "gla.7.0", "gla.7.1"):
                b, k = S_USE[name]
                pe.wait_ge(s_free[b], k + 2)
            for t in range(T):
                for g in range(2):
                    bank, full = t_begin(f"go.{2 * t + g}")
                    for j in range(2):
                        h = 2 * g + j
                        o = bank[:, 256 * j:256 * j + 256]
                        if t == 1:
                            pe.matmul(o, attn[:, 2, h, :], gv[:, 0, 256 * h:256 * h + 256], start=True, stop=False)
                        ins = pe.matmul(o, attn[:, t, h, :], gv[:, t, 256 * h:256 * h + 256],
                                        start=(t == 0), stop=True)
                    ins.then_inc(full, 1)

            pe.wait_ge(ev("ckT_ready"), 1)
            for c in range(4):
                unit(f"UKV{c}", 0, ckT)
            panel("G10", lta)
            mod_panel(4)
            mod_turn(4)
            mod_panel(5)
            mod_turn(5)
            pe.wait_ge(ev("q_normed"), 1)
            for g in range(4):
                bank, full = t_begin(f"qn.{g}")
                for j in range(2):
                    for t in range(T):
                        c = 192 * (2 * g + j)
                        ins = pe.transpose(bank[:, 256 * j + P * t:256 * j + P * t + P], q[:, t, c:c + P], ident[:])
                ins.then_inc(full, 1)
                unit("G11", g, lta)
            for g in range(2):
                bank, full = t_begin(f"qr.{g}")
                for j in range(2):
                    for t in range(T):
                        ins = pe.transpose(bank[:, 256 * j + P * t:256 * j + P * t + P],
                                           work[:, t, 0:512][:, P * (2 * g + j):P * (2 * g + j) + P], ident[:])
                ins.then_inc(full, 1)
            bank, full = t_begin("kp")
            for t in range(T):
                ins = pe.transpose(bank[:, P * t:P * t + P], kpe[:, t, :], ident[:])
            ins.then_inc(full, 1)
            pe.wait_ge(ev("k_normed"), 1)
            for g in range(4):
                bank, full = t_begin(f"kn.{g}")
                for j in range(2):
                    for t in range(T):
                        c = 256 * (2 * g + j)
                        ins = pe.transpose(bank[:, 256 * j + P * t:256 * j + P * t + P], kv[:, t, c:c + P], ident[:])
                ins.then_inc(full, 1)
            for g in ("kn.2", "kn.3"):
                b, k = T_USE[g]
                pe.wait_ge(t_free[b], k + 2)

            def mla_scores(h, bank):
                lane = slice(64 * (h % 2), 64 * (h % 2) + 64)
                for t in range(T):
                    o = bank[:, P * t:P * t + P * (t + 1)]
                    pe.matmul(o, qnT[:, h, P * t:P * t + P], knT[:, h, 0:P * (t + 1)], start=True, stop=False)
                    ins = pe.matmul(o, qrT[lane, h // 2, P * t:P * t + P], kpT[lane, 0:P * (t + 1)],
                                    start=False, stop=True)
                return ins

            def mla_values(h, bank, pT):
                for t in range(T):
                    for kt in range(t + 1):
                        ins = pe.matmul(bank[:, P * t:P * t + P], pT[:, P * (t + kt):P * (t + kt) + P],
                                        kv[:, kt, 256 * h + P:256 * h + 2 * P], start=(kt == 0), stop=(kt == t))
                return ins

            attend("MLA", H_MLA, mla_scores, 3, mla_values, lambda i: fill(["G00", "G01"], i, 1))

            mod_panel(6)
            turn_tokens("y", r_gla, ready="branches_mixed")
            panel("WO0", lta, new="y")
            mod_turn(6)
            panel("WO1", lta)
            mod_panel(7)
            pe.wait_ge(ev("ctx_landed"), 16)
            turn_tokens("hc", ar(8192, T, D))
            mod_turn(7)
            panel("CX", lta, new="hc")

            pe.wait_ge(ev("h2_scaled"), T)
            turn_tokens("h2", work)

            def up_turn(c, i=None):
                pe.wait_ge(up_done, c + 1 + (2 * i if i is not None else 0))
                for g in range(2):
                    b, k = T_USE[f"WU{c}.{g}"]
                    pe.wait_ge(t_free[b], k + 1 + (2 * i if i is not None else 0))
                    for kk in range(2):
                        for t in range(T):
                            ins = pe.transpose(tb[b][:, 256 * kk + P * t:256 * kk + P * t + P],
                                               up[c % 2][:, t, P * (2 * g + kk):P * (2 * g + kk) + P], ident[:])
                    ins.then_inc(t_full[b], 1)

            panel("WU0", ltb, new="h2")
            with pe.Fori(0, 3) as i:
                for c in (1, 2):
                    for k in range(4):
                        unit(f"WU{c}", k, ltb, i=i, per=8)
                        if k == 1:
                            up_turn(c - 1, i)
            for k in range(4):
                unit("WU7", k, ltb)
                if k == 1:
                    up_turn(6)
            for c in range(2):
                for k in range(D_FF // P // UNIT):
                    if c == 0 and k == 2:
                        up_turn(7)
                    if c == 0 and k % 2 == 0:
                        for g in range(2):
                            b, n = T_USE[f"WU{k // 2}.{g}"]
                            pe.wait_ge(t_free[b], n + 2)
                    unit(f"WD{c}", k, ff)

            mod_panel(8)
            for s in range(2):
                p, k = PLAN.bank(f"WD{s}")
                pe.wait_ge(panel_out[p], k + 2)
            turn_tokens("x2", x)
            for c in range(3):
                panel(f"IN{c}", lta, new="x2" if c == 0 else None)
                if c == 0:
                    mod_turn(8)
            mod_panel(9)
            for br, (kn, qn) in enumerate((("kA", "qA"), ("kB", "qB"))):
                pe.wait_ge(ev(f"{kn}_normed"), 1)
                for g in range(KVH):
                    bank, full = t_begin(f"{kn}.{g}")
                    for j in range(2):
                        for t in range(T):
                            ins = pe.transpose(bank[:, 256 * j + P * t:256 * j + P * t + P],
                                               kdup[:, 2 * br + j, t, P * g:P * g + P], ident[:])
                    ins.then_inc(full, 1)
                mod_turn(9 + 2 * br)
                if br == 0:
                    mod_panel(10)
                pe.wait_ge(ev(f"{qn}_normed"), 1)
                for g in range(2):
                    bank, full = t_begin(f"{qn}.{g}")
                    for j in range(2):
                        for t in range(T):
                            c = 768 * br + P * (2 * g + j)
                            ins = pe.transpose(bank[:, 256 * j + P * t:256 * j + P * t + P],
                                               qkv[:, t, c:c + P], ident[:])
                    ins.then_inc(full, 1)
                if br == 0:
                    mod_turn(10)
                    mod_panel(11)
            for g in ("kA.0", "kA.1", "qA.0", "qA.1", "kB.0", "kB.1", "qB.0", "qB.1"):
                b, k = T_USE[g]
                pe.wait_ge(t_free[b], k + 2)

            def ab_step(i):
                return i // (HEADS * T), i % (HEADS * T) // T, i % T

            def ab_scores(i, bank):
                br, h, t = ab_step(i)
                lane = slice(64 * (h % 2), 64 * (h % 2) + 64)
                return pe.matmul(bank[:, :], qT[br][lane, h // 2, P * t:P * t + P], kT[br][lane, h // GROUP, :],
                                 start=True, stop=True)

            def ab_values(i, bank, pT):
                br, h, t = ab_step(i)
                for kt in range(4):
                    v = qkv[:, kt, 768 * br + 640:768 * br + 768] if kt < 2 else \
                        kvx[:, kt - 2, 256 * br + 128:256 * br + 256]
                    ins = pe.matmul(bank[:, 0:HD], pT[:, P * kt:P * kt + P], v[:, HD * (h // GROUP):][:, 0:HD],
                                    start=(kt == 0), stop=(kt == 3))
                return ins

            in2 = ["IN3", "IN4", "IN5", "IN6"]
            attend("AB", 2 * HEADS * T, ab_scores, 4, ab_values,
                   lambda i: fill(in2, i // 2, 1) if i % 2 == 0 else None)

            b, k = T_USE[f"AB.O{2 * HEADS * T - 1}"]
            pe.wait_ge(t_free[b], k + 2)
            b, k = T_USE[f"AB.O{2 * HEADS * T - 2}"]
            pe.wait_ge(t_free[b], k + 2)
            turn_tokens("oab", oab)
            lt_wait("oab", 1)
            for name in ("BA0", "BA1", "BB0", "BB1"):
                if name == "BB0":
                    lt_wait("oab")
                for k in range(2):
                    unit(name, k, ltb, first_kt=2 * k + (4 if name[1] == "B" else 0))
            turn_tokens("ym", ym, ready="ym_ready")
            panel("OUT0", lta, new="ym")
            panel("OUT1", lta)

            def gate_rows(name):
                for g in range(2):
                    bank, full = t_begin(f"{name}.{g}")
                    pe.wait_ge(ev("ones_ready"), 1)
                    pe.wait_ge(ev(f"{name}_diag"), g + 1)
                    for j in range(4):
                        ins = pe.matmul(bank[:, P * j:P * j + P], ones[:], diag[:, j, :], start=True, stop=True)
                    ins.then_inc(full, 1)

            gate_rows("gate1")

            pe.wait_ge(ev("x3_ready"), T)
            turn_tokens("x3", x)

            def conv_turn(c, i=None):
                s, k = PLAN.bank(f"UP{c}")
                pe.wait_ge(panel_out[s], k + 2 + (i if i is not None else 0))
                for g in range(2):
                    b, k = T_USE[f"UP{c}.{g}"]
                    pe.wait_ge(t_free[b], k + 1 + (2 * i if i is not None else 0))
                    for kk in range(2):
                        for t in range(T):
                            ins = pe.transpose(tb[b][:, 256 * kk + P * t:256 * kk + P * t + P],
                                               upv[c % 2][:, t, P * (2 * g + kk):P * (2 * g + kk) + P], ident[:])
                    ins.then_inc(t_full[b], 1)

            panel("UP0", ltb, new="x3")
            with pe.Fori(0, 5) as i:
                for c in (1, 2):
                    for k in range(4):
                        unit(f"UP{c}", k, ltb, i=i, per=8)
                        if k == 1:
                            conv_turn(c - 1, i)
            for c in range(2):
                for k in range(FT2 // UNIT):
                    if c == 0 and k == 2:
                        conv_turn(10)
                    if c == 0:
                        pe.wait_ge(conv_mul, k + 1)
                    unit(f"DN{c}", k, actT)
            gate_rows("gate2")

        def last_unit(name):
            return PLAN.unit[name] + units_of(name) - 1

        @block.scalar
        def _(act):
            order = Order(act, act_order)

            def split(u, i=None, per=0, landings=0):
                s = u % RING
                du = per * i if i is not None else 0
                act.wait_ge(landed[s], PLAN.landed[u] + (landings * i if i is not None else 0))
                act.wait_ge(unit_used, u + 1 + du)
                n = PLAN.cols[u]
                act.copy(whi[:, s, :, 0:n], raw[:, s, :, 0:n]).then_inc(hi_ready, 1)

            cursor = [0]

            def ahead(pos):
                while cursor[0] < min(pos + AHEAD, PLAN.units):
                    split(cursor[0])
                    cursor[0] += 1

            def panel_wait(name, du=0):
                act.wait_ge(unit_used, RING + last_unit(name) + 1 + du)

            def evac(name, dst, n=COLS, func=ACT.Copy):
                ahead(last_unit(name) + 1)
                panel_wait(name)
                s, _ = PLAN.bank(name)
                act.activation(dst, acc[s][:, :, 0:n], func).then_inc(panel_out[s], 1)

            def lt_act(name, lt):
                for g in range(4):
                    b, k = T_USE[f"{name}.{g}"]
                    act.wait_ge(t_free[b], k + 2)
                    act.copy(lt[0][:, 2 * g:2 * g + 2, :].rearrange("p a b -> p (a b)"), turn[:, g % 2])\
                        .then_inc(lt_hi, 1)

            def sqrt(name, view):
                act.wait_ge(ev(f"{name}_var"), 1)
                act.activation(view, view, ACT.Sqrt).then_inc(ev(f"{name}_std"), 1)

            def t_out(name, dst, n=COLS, scale=1.0, parts=None):
                b, k = T_USE[name]
                act.wait_ge(t_full[b], k + 1)
                act.activation(dst, tb[b][0:(parts or P), 0:n], ACT.Copy, scale=scale).then_inc(t_free[b], 1)

            def attend(name, n, exps, at_scores, at_turn, blocks, after=None):
                def exp(i):
                    ahead(at_scores(i))
                    g = STEPS[name][0] + i
                    b, _ = S_USE[f"{name}.{i}"]
                    act.wait_ge(soft_ready, g + 1)
                    exps(i, g % 2, sc[b]).then_inc(s_free[b], 1)

                exp(0)
                for i in range(n):
                    if i + 1 < n:
                        exp(i + 1)
                    ahead(at_turn(i))
                    if i >= 2:
                        b, k = T_USE[f"{name}.O{i - 2}"]
                        act.wait_ge(t_full[b], k + 1)
                    t_out(f"{name}.PT{i}", probT[:, (STEPS[name][0] + i) % 2, 0:P * blocks], P * blocks)
                    if after:
                        after(i)

            for name, (first, n) in ROWS.items():
                act.dma_start(vrow[0][first:first + n, :], a[name].rearrange("(r c) -> r c", c=P))\
                    .then_inc(ev("rows_landed"), 16)
            for k, src in enumerate((a["conv_w_2"][0], a["conv_w_2"][1], a["conv_w_2"][2], a["conv_b_2"])):
                act.dma_start(vrow[1 + k // 2][44 * (k % 2):44 * (k % 2) + 44, :],
                              src.rearrange("(r c) -> r c", c=P)).then_inc(ev("rows_landed"), 16)
            for name, src, s in (("me", memx, 0), ("h", x[:], 1)):
                act.wait_ge(ev("mem_landed" if name == "me" else "x_landed"), 16)
                for t in range(T):
                    act.activation(prob[:].rearrange("p a b -> p (a b)"), src[:, t, :], ACT.Square,
                                   accum_out=stat[:, s, t:t + 1]).then_inc(ev(f"{name}_sum"), 1)
                    act.wait_ge(ev(f"{name}_sum"), t + 1)
                sqrt(name, stat[:, s, 2:4])
                if name == "me":
                    ahead(0)
            act.dma_start(stat[:, 7, 4:6].bitcast(I32), a["positions"].rearrange("(t p) -> p t", p=P),
                          allow_slow_non_contiguous=True).then_inc(ev("pos_landed"), 16)
            for name, view in GAIN.items():
                act.dma_start(view, a[name].partition_broadcast(P)).then_inc(ev("gains_landed"), 16)
            act.wait_ge(ev("vec_ready"), 1)
            act.activation(sic[:], vcol[:, ROWS["c_2"][0]:ROWS["c_2"][0] + 16], ACT.Sigmoid).then_inc(ev("c_sig"), 1)
            lt_act("me", lta)
            evac("MK0", kvm[:, :, 0:256], 256)
            evac("MK1", kvm[:, :, 256:768])
            act.wait_ge(ev("rot_arg"), 1)
            act.activation(rot[:, 0:2], rot[:, 0:2], ACT.Sin).then_inc(ev("rot_ready"), 1)
            evac("MK2", kvm[:, :, 768:1280])
            lt_act("h", lta)
            act.wait_ge(ev("memx_free"), 1)
            act.dma_start(wg[0:GATE_RANK, :], a["w_gla_gate"]).then_inc(ev("wg_landed"), 16)
            evac("AQ", aq[:], NARROW["AQ"])
            evac("CK", ck, NARROW["CK"])
            t_out("aT", aT[0:GATE_RANK, :], 256, parts=GATE_RANK)
            sqrt("mm", stat[:, 2, 0:16])
            evac("GQ", gq)
            act.wait_ge(ev("zb_ready"), 1)
            order.done(act.activation(ze, zb, ACT.Abs))
            order.done(act.activation(ze, ze, ACT.Exp, scale=-1.0))
            act.activation(ze, ze, ACT.Ln, bias=1.0).then_inc(ev("zln_ready"), 1)
            sqrt("ck", stat[:, 3, 0:4])
            evac("GK", gk)
            evac("V0", gv[:, :, 0:COLS])
            for name, dst in (("mqT", mqT), ("mkT", mkT)):
                t_out(name, dst.rearrange("p a b -> p (a b)"))
            act.wait_ge(ev("ck_turned"), 1)
            act.copy(ckT[0][:].rearrange("p a b -> p (a b)"), turn[:, 0]).then_inc(ev("ckT_hi"), 1)

            def mem_exps(i, slot, bank):
                for t in range(T):
                    ins = act.activation(prob[:, slot, 256 * t:256 * t + 256], bank[:, 256 * t:256 * t + 256], ACT.Exp,
                                         bias=soft[:, slot, 2 + t:3 + t], scale=DQ_MEM ** -0.5,
                                         accum_out=soft[:, slot, 4 + t:5 + t])
                return ins

            def mem_after(i):
                if i == 0:
                    evac("V1", gv[:, :, COLS:2 * COLS])
                elif i < 3:
                    name = f"R{i - 1}"
                    ahead(last_unit(name) + 1)
                    panel_wait(name)
                    if i == 2:
                        b, k = PLAN.bank("R0")
                        act.wait_ge(panel_out[b], k + 2)
                    act.activation(rsig, acc[PLAN.bank(name)[0]][:], ACT.Sigmoid).then_inc(ev("r_sig"), 1)

            def gate(name):
                ahead(last_unit(name) + 1)
                act.wait_ge(gate_in, BIASED.index(name) + 1)
                p = acc[PLAN.bank(name)[0]]
                act.activation(p[:], p[:], ACT.Sigmoid).then_inc(gate_sig, 1)

            u0 = PLAN.unit["V1"]
            attend("MEM", H_MEM, mem_exps, lambda i: u0 + 4 * max(i - 1, 0), lambda i: u0 + 4 * i + 2, 4, mem_after)

            b, k = T_USE[f"MEM.O{H_MEM - 1}"]
            act.wait_ge(t_full[b], k + 1)
            evac("Q0", q[:, :, 0:COLS])
            for name, dst, f in (("gqT", gqT, DK_GLA ** -0.5), ("gkT", gkT, 1.0)):
                for g in range(2):
                    t_out(f"{name}.{g}", dst[:, 2 * g:2 * g + 2, :].rearrange("p a b -> p (a b)"), scale=f)
            u0 = PLAN.unit["Q1"]
            for s in range(1, 9):
                ahead(u0 + 2 * s)
                act.wait_ge(gla_exp, s)
                e = arena[:, 7168:8192]
                act.activation(e, e, ACT.Exp).then_inc(ev("gla_expd"), 1)
                if s in (2, 4):
                    c = s // 2
                    evac(f"Q{c}", q[:, :, COLS * c:COLS * c + COLS])
                elif s in (6, 8):
                    gate(f"G2{s // 2 - 3}")
            for t in range(T):
                for g in range(2):
                    t_out(f"go.{2 * t + g}", og[:, t, 2 * g:2 * g + 2, :].rearrange("p a b -> p (a b)"))
            act.activation(room, qh[:, :, 0:NOPE], ACT.Square).then_inc(ev("qq_sq"), 1)
            act.activation(rope_sq, qh[:, :, NOPE:], ACT.Square).then_inc(ev("qq_sq"), 1)
            for c in range(4):
                evac(f"UKV{c}", kv[:, :, COLS * c:COLS * c + COLS])
            ahead(PLAN.unit["G10"])
            sqrt("qq", stat[:, 4:6, :])
            ahead(PLAN.unit["G10"] + 1)
            b, k = T_USE["go.3"]
            act.wait_ge(t_free[b], k + 2)
            for h in range(T * H_GLA):
                if h >= 4:
                    act.wait_ge(ev("og_sum"), h - 3)
                act.activation(og_sq[:, h % 4], og_heads[:, h], ACT.Square, accum_out=stat[:, 6, h:h + 1]).then_inc(ev("og_sum"), 1)
            ahead(PLAN.unit["G10"] + 3)
            act.wait_ge(ev("kk_free"), 1)
            act.activation(room, kh, ACT.Square).then_inc(ev("kk_sq"), 1)
            ahead(PLAN.unit["G11"])
            sqrt("kk", stat[:, 2, 0:16])
            gate("G10")
            sqrt("og", stat[:, 6, 0:8])
            for g in range(4):
                ahead(PLAN.unit["G11"] + g)
                t_out(f"qn.{g}", qnT[:, 2 * g:2 * g + 2, :].rearrange("p a b -> p (a b)"), scale=col("g_q_nope"))
            for g in range(2):
                t_out(f"qr.{g}", qrT[:, 2 * g:2 * g + 2, :].rearrange("p a b -> p (a b)"))
            t_out("kp", kpT, 256)
            for g in range(4):
                t_out(f"kn.{g}", knT[:, 2 * g:2 * g + 2, :].rearrange("p a b -> p (a b)"), scale=col("g_k_nope"))

            def mla_exps(i, slot, bank):
                for t, (first, n) in enumerate(((0, P), (P, 2 * P))):
                    ins = act.activation(prob[:, slot, first:first + n], bank[:, first:first + n], ACT.Exp,
                                         bias=soft[:, slot, 2 + t:3 + t], scale=(NOPE + ROPE) ** -0.5,
                                         accum_out=soft[:, slot, 4 + t:5 + t])
                return ins

            def mla_after(i):
                if i in (0, 3, 7):
                    gate(("G11", "G00", "G01")[(i + 1) // 4])

            u0 = PLAN.unit["G00"]
            attend("MLA", H_MLA, mla_exps, lambda i: u0 + max(i - 1, 0), lambda i: u0 + i + 1, 3, mla_after)

            lt_act("y", lta)
            ahead(PLAN.unit["CX"])
            for t in range(T):
                act.wait_ge(ev("x1_ready"), 2)
                act.activation(prob[:].rearrange("p a b -> p (a b)"), x[:, t, :], ACT.Square,
                               accum_out=stat[:, 1, t:t + 1]).then_inc(ev("h2_sum"), 1)
                act.wait_ge(ev("h2_sum"), t + 1)
            sqrt("h2", stat[:, 1, 2:4])
            lt_act("hc", lta)
            ahead(PLAN.unit["WU0"])
            lt_act("h2", ltb)

            def up_hi_of(c, i=None):
                d = 2 * i if i is not None else 0
                for g in range(2):
                    b, k = T_USE[f"WU{c}.{g}"]
                    act.wait_ge(t_full[b], k + 1 + d)
                    ft = 4 * c + 2 * g
                    dst = ff[0][:, ft:ft + 2, :] if i is None else ff[0][:, bass.ds(8 * i + ft, 2), :]
                    act.copy(dst.rearrange("p a b -> p (a b)"), tb[b][:]).then_inc(up_hi, 1)

            def up_relu(c, i=None):
                s, _ = PLAN.bank(f"WU{c}")
                panel_wait(f"WU{c}", 8 * i if i is not None else 0)
                act.activation(up[c % 2][:], acc[s][:], ACT.Relu).then_inc(panel_out[s], 1)

            evac("WU0", up[0][:], func=ACT.Relu)
            u0 = PLAN.unit["WU1"]
            assert cursor[0] == u0 + AHEAD
            with act.Fori(0, 3) as i:
                for c in (1, 2):
                    for k in range(4):
                        split(u0 + 4 * (c - 1) + k + AHEAD, i, 8, 32)
                        if k == 1:
                            up_hi_of(c - 1, i)
                    up_relu(c, i)
            cursor[0] += 24
            ahead(PLAN.unit["WU7"] + 2)
            up_hi_of(6)
            ahead(PLAN.unit["WU7"] + 4)
            up_relu(7)
            ahead(PLAN.unit["WD0"] + 2)
            up_hi_of(7)
            ahead(PLAN.unit["IN0"])

            lt_act("x2", lta)
            ahead(PLAN.unit["IN3"])
            sqrt("ab", stat[:, 2:4, :])
            for br, names in enumerate((("kA", "qA"), ("kB", "qB"))):
                for g in range(2):
                    t_out(f"{names[0]}.{g}", kT[br][:, g, :])
                for g in range(2):
                    t_out(f"{names[1]}.{g}", qT[br][:, 2 * g:2 * g + 2, :].rearrange("p a b -> p (a b)"))

            def ab_exps(i, slot, bank):
                br, h = i // (HEADS * T), i % (HEADS * T) // T
                if br == 0:
                    act.activation(soft[:, slot, 6:7], GAIN["attn_sink_2"][:, h:h + 1], ACT.Exp,
                                   bias=soft[:, slot, 2:3])
                return act.activation(prob[:, slot, :], bank[:], ACT.Exp, bias=soft[:, slot, 2:3],
                                      scale=HD ** -0.5, accum_out=soft[:, slot, 4:5])

            def ab_after(i):
                if i % 8 == 7:
                    name = f"IN{3 + i // 8}"
                    s, k = PLAN.bank(name)
                    c = COLS * (i // 8)
                    ahead(last_unit(name) + 1)
                    act.wait_ge(panel_out[s], k + 2)
                    act.activation(gate2[:, :, c:c + COLS], gate2[:, :, c:c + COLS], ACT.Sigmoid).then_inc(gate_sig, 1)

            u0 = PLAN.unit["IN3"]
            attend("AB", 2 * HEADS * T, ab_exps, lambda i: u0 + max(i, 0) // 2, lambda i: u0 + i // 2 + 1, 4, ab_after)
            lt_act("oab", ltb)
            ahead(PLAN.unit["OUT0"])
            lt_act("ym", lta)
            for c in range(2):
                evac(f"OUT{c}", work[:, :, COLS * c:COLS * c + COLS])
            sqrt("ln1", stat[:, 1, 4:6])
            ahead(PLAN.unit["UP0"])
            lt_act("x3", ltb)

            def conv_of(c, i=None):
                d = i if i is not None else 0
                act.wait_ge(ev("tap_ready"), c + 1 + 2 * d)
                for j in range(4):
                    b, k = T_USE[f"UP{c}.{j // 2}"]
                    act.wait_ge(t_full[b], k + 1 + 2 * d)
                    act.activation(conv[:, j], tb[b][:, 256 * (j % 2):256 * (j % 2) + 256], ACT.Identity,
                                   bias=tap[:, 3, j:j + 1], scale=tap[:, 1, j:j + 1]).then_inc(conv_lin, 1)
                b, k = T_USE[f"UP{c}.0"]
                act.wait_ge(t_free[b], k + 2 + 2 * d)
                act.activation(sig[:], conv[:, 0:2], ACT.Sigmoid).then_inc(conv_sig, 1)

            def conv_hi(c, i=None):
                d = i if i is not None else 0
                act.wait_ge(ev("conv_prod"), c + 1 + 2 * d)
                dst = actT[0][:, 2 * c:2 * c + 2, :] if i is None else actT[0][:, bass.ds(4 * i + 2 * c, 2), :]
                act.copy(dst, conv[:, 2:4]).then_inc(ev("conv_hi"), 1)

            def upv_out(c, i=None):
                s, _ = PLAN.bank(f"UP{c}")
                panel_wait(f"UP{c}", 8 * i if i is not None else 0)
                act.copy(upv[c % 2][:], acc[s][:]).then_inc(panel_out[s], 1)

            evac("UP0", upv[0][:])
            u0 = PLAN.unit["UP1"]
            assert cursor[0] == u0 + AHEAD
            with act.Fori(0, 5) as i:
                for c in (1, 2):
                    for k in range(4):
                        split(u0 + 4 * (c - 1) + k + AHEAD, i, 8, 64)
                        if k == 1:
                            conv_of(c - 1, i)
                        if k == 2:
                            conv_hi(c - 1, i)
                    upv_out(c, i)
            cursor[0] += 40
            ahead(PLAN.unit["DN0"] + 2)
            conv_of(10)
            conv_hi(10)
            ahead(PLAN.units)
            for c in range(2):
                evac(f"DN{c}", work[:, :, COLS * c:COLS * c + COLS])
            sqrt("ln2", stat[:, 1, 4:6])

        @block.vector
        def _(dve):
            order = Order(dve, dve_order)
            done = order.done
            for s in panel_out + t_free + s_free:
                dve.sem_inc(s, 1)
            dve.sem_inc(split_ready, RING)
            dve.sem_inc(mod_free, KT // UNIT)
            dve.sem_inc(bias_used, 2)

            def split(u, i=None, per=0):
                s = u % RING
                dve.wait_ge(hi_ready, u + 1 + (per * i if i is not None else 0))
                n = PLAN.cols[u]
                dve.tensor_tensor(wlo[:, s, :, 0:n], raw[:, s, :, 0:n], whi[:, s, :, 0:n].bitcast(F32), ALU.subtract)\
                   .then_inc(split_ready, 1)

            cursor = [0]

            def ahead(pos):
                while cursor[0] < min(pos + AHEAD, PLAN.units):
                    split(cursor[0])
                    cursor[0] += 1

            def panel_wait(name):
                ahead(last_unit(name) + 1)
                dve.wait_ge(unit_used, RING + last_unit(name) + 1)
                return acc[PLAN.bank(name)[0]]

            def evacuated(name):
                s, k = PLAN.bank(name)
                dve.wait_ge(panel_out[s], k + 2)

            def frees(name, ins):
                s, k = PLAN.bank(name)
                ins.then_inc(panel_out[s], 1)
                dve.wait_ge(panel_out[s], k + 2)

            def biased(name, dst):
                p, n = panel_wait(name), n_gate[name]
                twice = (n // 2 + 1) + (1 if n % 2 == 0 and n >= n_gate["CX"] else 0)
                dve.wait_ge(bias_landed[n % 2], 16 * twice)
                frees(name, dve.tensor_tensor(dst, p[:], bias[:, n % 2].unsqueeze(1).broadcast_to([P, T, COLS]),
                                              ALU.add))
                dve.sem_inc(bias_used, 1)

            def lt_dve(name, lt, scale=None, shift=None):
                def low(g):
                    dve.wait_ge(lt_hi, lt_done(name, g))
                    dve.tensor_tensor(lt[1][:, 2 * g:2 * g + 2, :].rearrange("p a b -> p (a b)"), turn[:, g % 2],
                                      lt[0][:, 2 * g:2 * g + 2, :].bitcast(F32).rearrange("p a b -> p (a b)"),
                                      ALU.subtract).then_inc(lt_ready, 1)

                for g in range(4):
                    b, k = T_USE[f"{name}.{g}"]
                    if lt_done(name, g) > 2:
                        dve.wait_ge(lt_ready, lt_done(name, g) - 2)
                    dve.wait_ge(t_full[b], k + 1)
                    if scale is None:
                        ins = dve.tensor_copy(turn[:, g % 2], tb[b][:])
                    else:
                        for kk in range(2):
                            half, c = slice(256 * kk, 256 * kk + 256), 2 * g + kk
                            if shift is None:
                                ins = dve.tensor_scalar(turn[:, g % 2, half], tb[b][:, half], scale[:, c:c + 1], None,
                                                        ALU.mult)
                            else:
                                ins = dve.tensor_scalar(turn[:, g % 2, half], tb[b][:, half], scale[:, c:c + 1],
                                                        shift[:, c:c + 1], ALU.mult, ALU.add)
                    ins.then_inc(t_free[b], 1)
                    if g >= 1:
                        low(g - 1)
                low(3)

            def spread(v, n):
                return v.unsqueeze(2).broadcast_to([P, v.shape[1], n])

            def squares(src, scratch, dst):
                done(dve.tensor_tensor(scratch, src, src, ALU.mult))
                done(dve.tensor_reduce(dst, scratch, AX.X, ALU.add))

            def var(view, n, eps=EPS):
                return dve.tensor_scalar(view, view, 1.0 / n, eps, ALU.mult, ALU.add)

            def inverse(name, view):
                dve.wait_ge(ev(f"{name}_std"), 1)
                done(dve.reciprocal(view, view))

            def rope(y1, y2, x1, x2, cos, sin, tmp):
                done(dve.tensor_tensor(y1, x1, cos, ALU.mult))
                done(dve.tensor_tensor(tmp, x2, sin, ALU.mult))
                done(dve.tensor_tensor(y1, y1, tmp, ALU.subtract))
                done(dve.tensor_tensor(y2, x2, cos, ALU.mult))
                done(dve.tensor_tensor(tmp, x1, sin, ALU.mult))
                done(dve.tensor_tensor(y2, y2, tmp, ALU.add))

            def mod_row(c):
                b, k = T_USE[f"mod.{c}"]
                dve.wait_ge(t_full[b], k + 1)
                dve.tensor_copy(modrow[:], tb[b][0:2, :]).then_inc(t_free[b], 1)
                dve.sem_inc(mod_free, 1)

            def mod_out(c):
                b, k = T_USE[f"modt.{c}"]
                dve.wait_ge(t_full[b], k + 1)
                m = tb[b][:, 0:8].rearrange("p (j e) -> p j e", e=2)
                if c < 4:
                    done(dve.tensor_tensor(modx[:, 4 * c:4 * c + 4], m[:, :, 1], col("b_mod_2", 4 * c, 4), ALU.add))
                dve.tensor_tensor(modc[:, 4 * c:4 * c + 4], m[:, :, 0], col("b_mod_2", 4 * c, 4), ALU.add)\
                    .then_inc(t_free[b], 1)
                dve.wait_ge(t_free[b], k + 2)

            def attend(name, n, maxima, sums, weigh, at_scores, at_turn, after=None):
                def softmax(i):
                    ahead(at_scores(i))
                    g = STEPS[name][0] + i
                    b, k = S_USE[f"{name}.{i}"]
                    dve.wait_ge(s_full[b], k + 1)
                    maxima(i, soft[:, g % 2], sc[b]).then_inc(soft_ready, 1)

                softmax(0)
                for i in range(n + 1):
                    if i >= 1:
                        b, k = S_USE[f"{name}.{i - 1}"]
                        dve.wait_ge(s_free[b], k + 2)
                        sums(i - 1, soft[:, (STEPS[name][0] + i - 1) % 2])
                    if i + 1 < n:
                        softmax(i + 1)
                    ahead(at_turn(i))
                    if i >= 1:
                        b, k = T_USE[f"{name}.O{i - 1}"]
                        dve.wait_ge(t_full[b], k + 1)
                        weigh(i - 1, soft[:, (STEPS[name][0] + i - 1) % 2, 8:10], tb[b]).then_inc(t_free[b], 1)
                    if after:
                        after(i)

            def mean_square(s, name):
                dve.wait_ge(ev(f"{name}_sum"), T)
                dve.tensor_scalar(stat[:, s, 2:4], stat[:, s, 0:2], 1.0 / D, EPS, ALU.mult, ALU.add)\
                    .then_inc(ev(f"{name}_var"), 1)

            mean_square(0, "me")
            inverse("me", stat[:, 0, 2:4])
            for t in range(T):
                dve.tensor_scalar(work[:, t], memx[:, t], stat[:, 0, 2 + t:3 + t], None, ALU.mult)\
                   .then_inc(ev("me_scaled"), 1)
            for g, dst in enumerate((vcol[:], ccol[:, 0:2], ccol[:, 2:4])):
                b, k = T_USE[f"vec.{g}"]
                dve.wait_ge(t_full[b], k + 1)
                n = (96, 88, 88)[g]
                src = tb[b][:, 0:n] if g == 0 else tb[b][:, 0:n].rearrange("p (a c) -> p a c", a=2)
                dve.tensor_copy(dst, src).then_inc(t_free[b], 1)
                dve.wait_ge(t_free[b], k + 2)
            dve.sem_inc(ev("vec_ready"), 1)
            ahead(0)
            mean_square(1, "h")
            lt_dve("me", lta, col("g_mem", 0, 8))
            dve.wait_ge(ev("me_scaled"), T)
            dve.sem_inc(ev("memx_free"), 1)
            inverse("h", stat[:, 1, 2:4])
            for t in range(T):
                dve.tensor_scalar(work[:, t], x[:, t], stat[:, 1, 2 + t:3 + t], None, ALU.mult)\
                   .then_inc(ev("h_scaled"), 1)
            dve.wait_ge(ev("c_sig"), 1)
            done(dve.tensor_tensor(sic[:], sic[:], vcol[:, ROWS["c_2"][0]:ROWS["c_2"][0] + 16], ALU.mult))
            dve.sem_inc(ev("sic_ready"), 1)
            ahead(PLAN.unit["MK1"])

            dve.wait_ge(ev("grid_ready"), 1)
            dve.wait_ge(ev("pos_landed"), 16)
            done(dve.tensor_copy(stat[:, 7, 6:8], stat[:, 7, 4:6].bitcast(I32)))
            done(dve.tensor_copy(stat[:, 7, 8:9], stat[:, 7, 2:3].bitcast(I32)))
            freq = ar(13568, 64)
            for t in range(T):
                for first, n, p in ((0, 32, stat[:, 7, 6 + t:7 + t]), (32, 16, stat[:, 7, t:t + 1]),
                                    (48, 16, stat[:, 7, 8:9])):
                    done(dve.tensor_scalar(angle[:, t, first:first + n], freq[:, first:first + n], p, None, ALU.mult))
            magic = 1.5 * 2.0 ** 23
            done(dve.tensor_scalar(turns, angle, float(1 / (2 * np.pi)), magic, ALU.mult, ALU.add))
            done(dve.tensor_scalar(turns, turns, magic, None, ALU.subtract))
            rest = 2 * np.pi
            for bits in (5, 14, 23, 60):
                part = float(np.float32(np.floor(rest * 2.0 ** bits) / 2.0 ** bits)) if bits < 60 else \
                    float(np.float32(rest))
                rest -= part
                done(dve.scalar_tensor_tensor(angle, turns, -part, angle, ALU.mult, ALU.add))
            pi = float(np.nextafter(np.float32(np.pi), np.float32(0)))
            done(dve.tensor_scalar(rot[:, 0], angle, pi, -pi, ALU.min, ALU.max))
            done(dve.scalar_tensor_tensor(turns, rot[:, 0], -1.0, rot[:, 0], ALU.mult, ALU.max))
            dve.tensor_scalar(rot[:, 1], turns, -1.0, float(np.pi / 2), ALU.mult, ALU.add)\
                .then_inc(ev("rot_arg"), 1)

            ahead(PLAN.unit["AQ"])
            lt_dve("h", lta, col("g_mix", 0, 8))

            ahead(PLAN.unit["CK"])
            evacuated("AQ")
            evacuated("MK0")
            views = []
            for t in range(T):
                views.append((aq[:, t, GATE_RANK:272].rearrange("p (h c) -> p h c", c=DQ_MEM), stat[:, 2, 4 * t:4 * t + 4],
                              "g_q_mem"))
            for t in range(T):
                views.append((kvm[:, t, 0:256].rearrange("p (h c) -> p h c", c=DQ_MEM),
                              stat[:, 2, 8 + 4 * t:12 + 4 * t], "g_k_mem"))
            b, k = T_USE["h.3"]
            dve.wait_ge(t_full[b], k + 1)
            scratch = work[:, 0, 0:256].rearrange("p (h c) -> p h c", c=DQ_MEM)
            for v, s, _ in views:
                squares(v, scratch, s)
            var(stat[:, 2, :], DQ_MEM).then_inc(ev("mm_var"), 1)
            ahead(PLAN.unit["GQ"])
            evacuated("CK")
            for t in range(T):
                squares(ck[:, t:t + 1, 0:256], work[:, t:t + 1, 0:256], stat[:, 3, t:t + 1])
                squares(ck[:, t:t + 1, 256:320], work[:, t:t + 1, 0:64], stat[:, 3, 2 + t:3 + t])
            done(var(stat[:, 3, 0:2], KV_RANK))
            var(stat[:, 3, 2:4], ROPE).then_inc(ev("ck_var"), 1)

            done(dve.memset(zflag, 1.0))
            done(dve.memset(zflag[:, :, 0:1], 0.0))
            ahead(PLAN.unit["GK"])
            for g in range(2):
                b, k = T_USE[f"z.{g}"]
                dve.wait_ge(t_full[b], k + 1)
                for j in range(2):
                    ins = dve.tensor_scalar(zb[:, 2 * g + j, :], tb[b][:, 256 * j:256 * j + 256],
                                            col("b_gla_gate", 2 * g + j), None, ALU.add)
                ins.then_inc(t_free[b], 1)
                dve.wait_ge(t_free[b], k + 2)
            dve.sem_inc(ev("zb_ready"), 1)
            inverse("mm", stat[:, 2, :])
            dve.wait_ge(ev("gains_landed"), 16 * len(GAIN))
            for i, (v, s, gain) in enumerate(views):
                done(dve.tensor_tensor(v, v, spread(s, DQ_MEM), ALU.mult))
                done(dve.tensor_tensor(v, v, GAIN[gain].unsqueeze(1).broadcast_to([P, H_MEM, DQ_MEM]), ALU.mult))
                if i % 2 == 1:
                    dve.sem_inc(ev(("mqT_normed", "mkT_normed")[i // 2]), 1)
            ahead(PLAN.unit["V0"])
            dve.wait_ge(ev("zln_ready"), 1)
            done(dve.scalar_tensor_tensor(zb, zb, 0.0, ze, ALU.min, ALU.subtract))
            done(dve.tensor_scalar(zb, zb, 1.0 / 16.0, None, ALU.mult))
            done(dve.tensor_tensor_scan(arena[:, 6144:7168], arena[:, 13312:14336], arena[:, 11264:12288], 0.0,
                                        ALU.mult, ALU.add))
            inverse("ck", stat[:, 3, 0:4])
            for t in range(T):
                done(dve.tensor_scalar(ck[:, t, 0:256], ck[:, t, 0:256], stat[:, 3, t:t + 1], None, ALU.mult))
            dve.sem_inc(ev("ck_normed"), 1)
            ahead(PLAN.unit["V1"])
            b, k = T_USE["ck"]
            dve.wait_ge(t_full[b], k + 1)
            for kk in range(2):
                ins = dve.tensor_scalar(turn[:, 0, 256 * kk:256 * kk + 256], tb[b][:, 256 * kk:256 * kk + 256],
                                        col("g_ckv", kk), None, ALU.mult)
            ins.then_inc(t_free[b], 1)
            dve.wait_ge(t_free[b], k + 2)
            dve.sem_inc(ev("ck_turned"), 1)
            dve.wait_ge(ev("ckT_hi"), 1)
            dve.tensor_tensor(ckT[1][:].rearrange("p a b -> p (a b)"), turn[:, 0],
                              ckT[0][:].bitcast(F32).rearrange("p a b -> p (a b)"), ALU.subtract)\
                .then_inc(ev("ckT_ready"), 1)
            dve.wait_ge(ev("ckT_ready"), 1)

            def neg(s, n, scale):
                return dve.tensor_scalar(s[:, 2:2 + n], s[:, 0:n], -scale, None, ALU.mult)

            def mem_maxima(i, s, bank):
                done(dve.tensor_reduce(s[:, 0:2], bank[:].rearrange("p (t k) -> p t k", t=T), AX.X, ALU.max))
                return neg(s, 2, DQ_MEM ** -0.5)

            def sums2(i, s):
                done(dve.reciprocal(s[:, 8:10], s[:, 4:6]))

            def weigh2(dst, bank, r, n):
                return dve.tensor_tensor(dst, bank[:, 0:T * n].rearrange("p (t c) -> p t c", t=T), spread(r, n), ALU.mult)

            def mem_after(i):
                if 1 <= i < 3:
                    name, c = f"R{i - 1}", COLS * (i - 1)
                    p = panel_wait(name)
                    dve.wait_ge(ev("r_sig"), i)
                    v = r_gla[:, :, c:c + COLS]
                    frees(name, dve.tensor_tensor(v, p[:], rsig, ALU.mult))
                    for t in range(T):
                        g = v[:, t].rearrange("p (h c) -> p h c", c=DV_GLA)
                        done(dve.tensor_tensor(g, g, GAIN["g_gla_out"].unsqueeze(1).broadcast_to([P, 2, DV_GLA]), ALU.mult))

            def gate_in_psum(name):
                p, n = panel_wait(name), n_gate[name]
                dve.wait_ge(bias_landed[n % 2], 16 * (n // 2 + 1))
                dve.tensor_tensor(p[:], p[:], bias[:, n % 2].unsqueeze(1).broadcast_to([P, T, COLS]), ALU.add)\
                   .then_inc(gate_in, 1)
                dve.wait_ge(gate_in, n + 1)
                dve.sem_inc(bias_used, 1)

            def gate_on(name, branch):
                dve.wait_ge(gate_sig, n_gate[name] + 1)
                part = slice(COLS * int(name[2]), COLS * int(name[2]) + COLS)
                frees(name, dve.tensor_tensor(branch[:, :, part], branch[:, :, part], acc[PLAN.bank(name)[0]][:], ALU.mult))

            u0 = PLAN.unit["V1"]
            attend("MEM", H_MEM, mem_maxima, sums2,
                   lambda i, r, bank: weigh2(o_mem[:, :, DV_MEM * i:DV_MEM * i + DV_MEM], bank, r, DV_MEM),
                   lambda i: u0 + 4 * max(i - 1, 0), lambda i: u0 + min(4 * i + 2, 14), mem_after)

            u0 = PLAN.unit["Q1"]
            for g in ("gqT.0", "gqT.1", "gkT.0", "gkT.1"):
                b, k = T_USE[g]
                dve.wait_ge(t_free[b], k + 2)
            done(dve.memset(attn, 0.0))
            done(dve.memset(arena[:, 18592:20640], 0.0))
            dve.wait_ge(ev("gmask_ready"), 1)

            def halves(v, w):
                return v.rearrange("p h (m e w) -> p (h m) e w", e=2, w=w)

            def exponents(s):
                if s == 1:
                    e = eq.rearrange("p (h c) -> p h c", h=H_GLA), ek.rearrange("p (h c) -> p h c", h=H_GLA)
                    done(dve.tensor_copy(e[0], decay[:, :, P:2 * P]))
                    ins = dve.tensor_tensor(e[1], decay[:, :, P - 1:P].broadcast_to([P, H_GLA, P]), decay[:, :, 0:P],
                                            ALU.subtract)
                else:
                    w = P >> (s - 1)
                    d = halves(decay, w)
                    ref = d[:, :, 0, w - 1:w].broadcast_to([P, d.shape[1], w])
                    done(dve.tensor_tensor(eq.rearrange("p (m w) -> p m w", w=w), d[:, :, 1, :], ref, ALU.subtract))
                    ins = dve.tensor_tensor(ek.rearrange("p (m w) -> p m w", w=w), ref, d[:, :, 0, :], ALU.subtract)
                ins.then_inc(gla_exp, 1)

            def decayed(s):
                if s >= 2:
                    b, k = S_USE["gla.off" if s == 2 else f"gla.{s - 2}.1"]
                    dve.wait_ge(s_full[b], k + 1)
                dve.wait_ge(ev("gla_expd"), s)
                if s == 1:
                    done(dve.tensor_tensor(gqd[:, :, P:2 * P], gqT[:, :, P:2 * P],
                                           eq.rearrange("p (h c) -> p h c", h=H_GLA), ALU.mult))
                    ins = dve.tensor_tensor(gkd[:, :, 0:P], gkT[:, :, 0:P],
                                            ek.rearrange("p (h c) -> p h c", h=H_GLA), ALU.mult)
                else:
                    w = P >> (s - 1)
                    done(dve.tensor_tensor(halves(gqd, w)[:, :, 1, :], halves(gqT, w)[:, :, 1, :],
                                           eq.rearrange("p (m w) -> p m w", w=w), ALU.mult))
                    ins = dve.tensor_tensor(halves(gkd, w)[:, :, 0, :], halves(gkT, w)[:, :, 0, :],
                                            ek.rearrange("p (m w) -> p m w", w=w), ALU.mult)
                ins.then_inc(gla_in, 1)
                dve.wait_ge(gla_in, s)

            def weights(s):
                if s == 1:
                    b, k = S_USE["gla.off"]
                    dve.wait_ge(s_full[b], k + 1)
                    dve.tensor_copy(attn[:, 2], sc[b][:].rearrange("p (h c) -> p h c", h=H_GLA)).then_inc(s_free[b], 1)
                    return
                mask = ident[:].bitcast(I32) if s == 0 else gmask[:, s - 2, :]
                for t in range(T):
                    b, k = S_USE[f"gla.{max(s - 1, 0)}.{t}"]
                    dve.wait_ge(s_full[b], k + 1)
                    dve.copy_predicated(attn[:, t], mask.unsqueeze(1).broadcast_to([P, H_GLA, P]),
                                        sc[b][:].rearrange("p (h c) -> p h c", h=H_GLA)).then_inc(s_free[b], 1)
                    dve.wait_ge(s_free[b], k + 2)

            exponents(1)
            for s in range(1, 9):
                ahead(u0 + 2 * s)
                decayed(s)
                if s < 8:
                    exponents(s + 1)
                weights(s - 1)
                if s in (6, 8):
                    gate_in_psum(f"G2{s // 2 - 3}")
                if s == 7:
                    gate_on("G20", o_mem)
                if s % 2 == 0:
                    mod_row(s // 2 - 1)
                elif s >= 3:
                    mod_out(s // 2 - 1)
            mod_out(3)
            weights(8)
            gate_on("G21", o_mem)
            for v in (modc[:, 8:16], modx[:, 8:16]):
                done(dve.tensor_scalar(v, v, 1.0, None, ALU.add))

            dve.wait_ge(ev("qq_sq"), 2)
            done(dve.tensor_reduce(stat[:, 4, :], room, AX.X, ALU.add))
            done(dve.tensor_reduce(stat[:, 5, :], rope_sq, AX.X, ALU.add))
            done(var(stat[:, 4, :], NOPE))
            var(stat[:, 5, :], ROPE).then_inc(ev("qq_var"), 1)
            dve.sem_inc(ev("kk_free"), 1)
            for t in range(T):
                done(dve.scalar_tensor_tensor(ck[:, t, 256:320], ck[:, t, 256:320], stat[:, 3, 2 + t:3 + t],
                                              GAIN["g_k_rope"], ALU.mult, ALU.mult))
            dve.wait_ge(ev("rot_ready"), 1)
            x1, x2 = ck[:, :, 256:288], ck[:, :, 288:320]
            rope(kpe[:, :, 0:32], kpe[:, :, 32:64], x1, x2, rot[:, 1, :, 0:32], rot[:, 0, :, 0:32], work[:, :, 768:800])
            done(dve.tensor_copy(kpe[:, :, 64:128], kpe[:, :, 0:64]))
            ahead(PLAN.unit["G10"])
            inverse("qq", stat[:, 4:6, :])
            done(dve.tensor_tensor(qh[:, :, 0:NOPE], qh[:, :, 0:NOPE], spread(stat[:, 4, :], NOPE), ALU.mult))
            done(dve.tensor_tensor(qh[:, :, NOPE:], qh[:, :, NOPE:], spread(stat[:, 5, :], ROPE), ALU.mult))
            done(dve.tensor_tensor(qh[:, :, NOPE:], qh[:, :, NOPE:],
                                   GAIN["g_q_rope"].unsqueeze(1).broadcast_to([P, T * H_MLA, ROPE]), ALU.mult))
            ahead(PLAN.unit["G10"] + 1)
            for t in range(T):
                y = work[:, t, 0:512].rearrange("p (h c) -> p h c", c=ROPE)
                x12 = qh[:, H_MLA * t:H_MLA * t + H_MLA, NOPE:]
                ang = [rot[:, f, t, 0:32].unsqueeze(1).broadcast_to([P, H_MLA, 32]) for f in (1, 0)]
                rope(y[:, :, 0:32], y[:, :, 32:64], x12[:, :, 0:32], x12[:, :, 32:], *ang,
                     work[:, t, 768:1024].rearrange("p (h c) -> p h c", c=32))
                ahead(PLAN.unit["G10"] + 2 + t)
            dve.sem_inc(ev("q_normed"), 1)
            dve.wait_ge(ev("kk_sq"), 1)
            done(dve.tensor_reduce(stat[:, 2, :], room, AX.X, ALU.add))
            var(stat[:, 2, :], NOPE).then_inc(ev("kk_var"), 1)
            ahead(PLAN.unit["G11"])
            inverse("kk", stat[:, 2, :])
            done(dve.tensor_tensor(kh, kh, spread(stat[:, 2, :], NOPE), ALU.mult))
            dve.sem_inc(ev("k_normed"), 1)
            gate_in_psum("G10")
            for c in (4, 5):
                mod_row(c)
                mod_out(c)
            dve.wait_ge(ev("og_sum"), T * H_GLA)
            var(stat[:, 6, 0:8], DV_GLA).then_inc(ev("og_var"), 1)
            ahead(PLAN.unit["G11"] + 1)
            inverse("og", stat[:, 6, 0:8])
            for t in range(T):
                for h in range(H_GLA):
                    v = r_gla[:, t, DV_GLA * h:DV_GLA * h + DV_GLA]
                    ins = dve.scalar_tensor_tensor(v, og[:, t, h], stat[:, 6, 4 * t + h:4 * t + h + 1], v, ALU.mult, ALU.mult)
            done(ins)
            gate_on("G10", r_gla)

            dve.wait_ge(ev("keeps_ready"), 1)

            def mla_maxima(i, s, bank):
                diagonal = bank[:].rearrange("p (a b) -> p a b", b=256)[:, :, 0:P]
                done(dve.tensor_tensor(diagonal, diagonal, keep_past[:].unsqueeze(1).broadcast_to([P, 2, P]), ALU.add))
                done(dve.tensor_reduce(s[:, 0:1], bank[:, 0:P], AX.X, ALU.max))
                done(dve.tensor_reduce(s[:, 1:2], bank[:, P:3 * P], AX.X, ALU.max))
                return neg(s, 2, (NOPE + ROPE) ** -0.5)

            def mla_after(i):
                if i in (0, 3, 7):
                    gate_in_psum(("G11", "G00", "G01")[(i + 1) // 4])
                if i == 1:
                    gate_on("G11", r_gla)
                    done(dve.tensor_tensor(r_gla, r_gla, o_mem, ALU.add))

            u0 = PLAN.unit["G00"]
            attend("MLA", H_MLA, mla_maxima, sums2,
                   lambda i, r, bank: weigh2(o_mla[:, :, V_MLA * i:V_MLA * i + V_MLA], bank, r, V_MLA),
                   lambda i: u0 + max(i - 1, 0), lambda i: u0 + min(i + 1, 8), mla_after)
            for g in (0, 1):
                b, k = T_USE[f"MLA.O{H_MLA - 1 - g}"]
                dve.wait_ge(t_free[b], k + 2)
            for c in range(2):
                part = slice(COLS * c, COLS * c + COLS)
                gate_on(f"G0{c}", o_mla)
                done(dve.tensor_tensor(r_gla[:, :, part], r_gla[:, :, part], o_mla[:, :, part], ALU.add))
                dve.sem_inc(ev("branches_mixed"), 1)
            mod_row(6)
            lt_dve("y", lta)
            for c in range(2):
                name, part = f"WO{c}", slice(COLS * c, COLS * c + COLS)
                p = panel_wait(name)
                frees(name, dve.tensor_tensor(x[:, :, part], x[:, :, part], p[:], ALU.add))
                dve.sem_inc(ev("x1_ready"), 1)
                if c == 0:
                    mod_out(6)
            mod_row(7)
            dve.wait_ge(ev("h2_sum"), T)
            dve.tensor_scalar(stat[:, 1, 2:4], stat[:, 1, 0:2], 1.0 / D, EPS, ALU.mult, ALU.add)\
                .then_inc(ev("h2_var"), 1)
            lt_dve("hc", lta, modx[:, 8:16], modx[:, 0:8])
            mod_out(7)
            inverse("h2", stat[:, 1, 2:4])
            for t in range(T):
                dve.tensor_scalar(work[:, t], x[:, t], stat[:, 1, 2 + t:3 + t], None, ALU.mult)\
                   .then_inc(ev("h2_scaled"), 1)
            biased("CX", kvx[:])
            lt_dve("h2", ltb, col("g_ffn", 0, 8))

            def up_square(c, i=None):
                s, k = PLAN.bank(f"WU{c}")
                dve.wait_ge(panel_out[s], k + 2 + (i if i is not None else 0))
                dve.tensor_tensor(up[c % 2][:], up[c % 2][:], up[c % 2][:], ALU.mult).then_inc(up_done, 1)

            def up_lo(c, i=None):
                for g in range(2):
                    b, _ = T_USE[f"WU{c}.{g}"]
                    ft = 4 * c + 2 * g
                    dve.wait_ge(up_hi, 2 * c + g + 1 + (4 * i if i is not None else 0))
                    hi, lo = (v[:, ft:ft + 2, :] if i is None else v[:, bass.ds(8 * i + ft, 2), :] for v in ff)
                    dve.tensor_tensor(lo.rearrange("p a b -> p (a b)"), tb[b][:],
                                      hi.bitcast(F32).rearrange("p a b -> p (a b)"), ALU.subtract)\
                        .then_inc(t_free[b], 1)

            ahead(PLAN.unit["WU1"])
            up_square(0)
            u0 = PLAN.unit["WU1"]
            assert cursor[0] == u0 + AHEAD
            with dve.Fori(0, 3) as i:
                for c in (1, 2):
                    for k in range(4):
                        split(u0 + 4 * (c - 1) + k + AHEAD, i, 8)
                        if k == 1:
                            up_lo(c - 1, i)
                    up_square(c, i)
            cursor[0] += 24
            ahead(PLAN.unit["WU7"] + 2)
            up_lo(6)
            ahead(PLAN.unit["WU7"] + 4)
            up_square(7)
            ahead(PLAN.unit["WD0"] + 2)
            up_lo(7)
            for c in range(2):
                name, part = f"WD{c}", slice(COLS * c, COLS * c + COLS)
                p = panel_wait(name)
                frees(name, dve.tensor_tensor(x[:, :, part], x[:, :, part], p[:], ALU.add))

            mod_row(8)
            lt_dve("x2", lta, modc[:, 8:16], modc[:, 0:8])
            for c in range(3):
                biased(f"IN{c}", qkv[:, :, COLS * c:COLS * c + COLS])
                if c == 0:
                    mod_out(8)

            def heads(v, n):
                return v.rearrange("p (h c) -> p h c", h=n)

            done(dve.memset(stat[:, 3, :], 1.0))
            normed = []
            for t in range(T):
                normed.append((heads(qkv[:, t, 768:1280], HEADS), stat[:, 2, 8 * t:8 * t + 8], "q_norm_g_2"))
                normed.append((heads(qkv[:, t, 1280:1408], KVH), stat[:, 3, 2 * t:2 * t + 2], "k_norm_g_2"))
                normed.append((heads(kvx[:, t, 256:384], KVH), stat[:, 3, 4 + 2 * t:6 + 2 * t], "k_norm_g_2"))
            for v, s, _ in normed:
                squares(v, heads(work[:, 0, 0:64 * v.shape[1]], v.shape[1]), s)
            var(stat[:, 2:4, :], HD).then_inc(ev("ab_var"), 1)

            def rope_2d(dst, src, n, t, room):
                def quarter(v, e):
                    return v.rearrange("p h (f e c) -> p h f e c", f=2, e=2)[:, :, :, e, :]
                ang = [rot[:, f, t, 32:64].rearrange("p (f c) -> p f c", f=2).unsqueeze(1).broadcast_to([P, n, 2, 16])
                       for f in (1, 0)]
                rope(quarter(dst, 0), quarter(dst, 1), quarter(src, 0), quarter(src, 1), *ang,
                     room[:, 0:32 * n].rearrange("p (h f c) -> p h f c", f=2, c=16))

            def twice(dst, src):
                d = dst.rearrange("p (h e c) -> p h e c", e=2, c=HD)
                done(dve.tensor_copy(d, src.unsqueeze(2).broadcast_to([P, KVH, 2, HD])))

            def branch(br):
                q0, k0, x0 = 768 * br, 768 * br + 512, 256 * br
                kn, qn = (("kA", "qA"), ("kB", "qB"))[br]
                for t in range(T):
                    rope_2d(heads(work[:, t, 512:640], KVH), heads(qkv[:, t, k0:k0 + 128], KVH), KVH, t, work[:, t, 640:1024])
                    twice(kdup[:, 2 * br, t, :], heads(work[:, t, 512:640], KVH))
                    twice(kdup[:, 2 * br + 1, t, :], heads(kvx[:, t, x0:x0 + 128], KVH))
                dve.sem_inc(ev(f"{kn}_normed"), 1)
                if br == 0:
                    mod_row(9)
                for t in range(T):
                    src = heads(qkv[:, t, q0:q0 + 512], HEADS)
                    rope_2d(heads(work[:, t, 0:512], HEADS), src, HEADS, t, work[:, t, 640:1024])
                    done(dve.tensor_copy(src, heads(work[:, t, 0:512], HEADS)))
                    if br == 0 and t == 0:
                        mod_out(9)
                        done(dve.tensor_scalar(modc[:, 32:40], modc[:, 32:40], 1.0, None, ALU.add))
                        mod_row(10)
                dve.sem_inc(ev(f"{qn}_normed"), 1)

            branch(0)
            inverse("ab", stat[:, 2:4, :])
            for v, s, gain in normed:
                done(dve.tensor_tensor(v, v, spread(s, HD), ALU.mult))
                done(dve.tensor_tensor(v, v, GAIN[gain].unsqueeze(1).broadcast_to([P, v.shape[1], HD]), ALU.mult))
            mod_out(10)
            mod_row(11)
            branch(1)
            mod_out(11)

            def ab_step(i):
                return i // (HEADS * T), i % (HEADS * T) // T, i % T

            def ab_maxima(i, s, bank):
                br, h, t = ab_step(i)
                if br == 0:
                    far = bank[:, P * (1 - t):P * (1 - t) + P]
                    done(dve.tensor_tensor(far, far, (keep_past if t == 0 else keep_next)[:], ALU.add))
                done(dve.tensor_reduce(s[:, 0:1], bank[:], AX.X, ALU.max))
                if br == 0:
                    done(dve.tensor_scalar(s[:, 0:1], s[:, 0:1], HD ** -0.5, None, ALU.mult))
                    done(dve.tensor_tensor(s[:, 0:1], s[:, 0:1], GAIN["attn_sink_2"][:, h:h + 1], ALU.max))
                    return neg(s, 1, 1.0)
                return neg(s, 1, HD ** -0.5)

            def ab_sums(i, s):
                if ab_step(i)[0] == 0:
                    done(dve.tensor_tensor(s[:, 4:5], s[:, 4:5], s[:, 6:7], ALU.add))
                done(dve.reciprocal(s[:, 8:9], s[:, 4:5]))

            def ab_weigh(i, r, bank):
                br, h, t = ab_step(i)
                c = 512 * br + HD * h
                return dve.tensor_scalar(oab[:, t, c:c + HD], bank[:, 0:HD], r[:, 0:1], None, ALU.mult)

            def ab_after(i):
                if i % 8 == 7:
                    c = i // 8
                    biased(f"IN{3 + c}", gate2[:, :, COLS * c:COLS * c + COLS])

            u0 = PLAN.unit["IN3"]
            attend("AB", 2 * HEADS * T, ab_maxima, ab_sums, ab_weigh, lambda i: u0 + i // 2,
                   lambda i: u0 + min(i // 2 + 1, 16), ab_after)
            lt_dve("oab", ltb)
            dve.wait_ge(gate_sig, 6 + 4)
            for br in range(2):
                for c in range(2):
                    name, part = f"B{'AB'[br]}{c}", slice(COLS * c, COLS * c + COLS)
                    p = panel_wait(name)
                    g = gate2[:, :, D * br + COLS * c:D * br + COLS * c + COLS]
                    if br == 0:
                        frees(name, dve.tensor_tensor(ym[:, :, part], p[:], g, ALU.mult))
                    else:
                        frees(name, dve.tensor_tensor(g, p[:], g, ALU.mult))
                        done(dve.tensor_tensor(ym[:, :, part], ym[:, :, part], g, ALU.add))
                        dve.sem_inc(ev("ym_ready"), 1)
            lt_dve("ym", lta)

            def gated_residual(name, src, first):
                for g in range(2):
                    if g == 1:
                        b, k = T_USE[f"{name}.0"]
                        dve.wait_ge(t_full[b], k + 1)
                    for j in range(4):
                        done(dve.tensor_scalar(diag[:, j, :], ident[:], modc[:, first + 4 * g + j:first + 4 * g + j + 1],
                                               None, ALU.mult))
                    dve.sem_inc(ev(f"{name}_diag"), 1)
                for g in range(2):
                    part = slice(COLS * g, COLS * g + COLS)
                    evacuated(f"{src}{g}")
                    b, k = T_USE[f"{name}.{g}"]
                    dve.wait_ge(t_full[b], k + 1)
                    done(dve.tensor_tensor(work[:, :, part], work[:, :, part],
                                           tb[b][:].unsqueeze(1).broadcast_to([P, T, COLS]), ALU.mult))
                    dve.sem_inc(t_free[b], 1)
                    done(dve.scalar_tensor_tensor(x[:, :, part], x[:, :, part], ALPHA, work[:, :, part], ALU.mult,
                                                  ALU.add))

            def layer_norm(name, each):
                for t in range(T):
                    done(dve.tensor_reduce(stat[:, 1, t:t + 1], x[:, t, :], AX.X, ALU.add))
                done(dve.tensor_scalar(stat[:, 1, 2:4], stat[:, 1, 0:2], 1.0 / D, None, ALU.mult))
                for t in range(T):
                    done(dve.tensor_scalar(x[:, t, :], x[:, t, :], stat[:, 1, 2 + t:3 + t], None, ALU.subtract))
                    done(dve.tensor_tensor_reduce(work[:, t, :], x[:, t, :], x[:, t, :], 1.0, 0.0, ALU.mult, ALU.add,
                                                  stat[:, 1, 4 + t:5 + t]))
                var(stat[:, 1, 4:6], D, LN_EPS).then_inc(ev(f"{name}_var"), 1)
                inverse(name, stat[:, 1, 4:6])
                dve.wait_ge(ev(f"{name}_landed"), 32)
                for t in range(T):
                    done(dve.scalar_tensor_tensor(x[:, t, :], x[:, t, :], stat[:, 1, 4 + t:5 + t], lnrow[:, 0], ALU.mult,
                                                  ALU.mult))
                    done(dve.tensor_tensor(x[:, t, :], x[:, t, :], lnrow[:, 1], ALU.add))
                    dve.sem_inc(ev(each), 1)

            ahead(PLAN.unit["UP0"])
            gated_residual("gate1", "OUT", 16)
            layer_norm("ln1", "x3_ready")
            dve.sem_inc(ev("ln1_done"), 1)
            lt_dve("x3", ltb, modc[:, 32:40], modc[:, 24:32])

            def taps(c, i=None):
                v = ccol[:].rearrange("p v (g f) -> p v g f", g=2)
                v = v[:, :, :, 2 * c:2 * c + 2] if i is None else v[:, :, :, bass.ds(4 * i + 2 * c, 2)]
                dve.tensor_copy(tap[:].rearrange("p v (g f) -> p v g f", g=2), v).then_inc(ev("tap_ready"), 1)

            def conv_taps(c, i=None):
                d = i if i is not None else 0
                for j in range(4):
                    b, _ = T_USE[f"UP{c}.{j // 2}"]
                    u = tb[b][:, 256 * (j % 2):256 * (j % 2) + 256]
                    if j % 2 == 0:
                        dve.wait_ge(conv_lin, 4 * c + j + 2 + 8 * d)
                    done(dve.scalar_tensor_tensor(conv[:, j, 1:SEQ], u[:, 0:SEQ - 1], tap[:, 0, j:j + 1],
                                                  conv[:, j, 1:SEQ], ALU.mult, ALU.add))
                    done(dve.scalar_tensor_tensor(conv[:, j, 0:SEQ - 1], u[:, 1:SEQ], tap[:, 2, j:j + 1],
                                                  conv[:, j, 0:SEQ - 1], ALU.mult, ALU.add))
                    if j % 2 == 1:
                        dve.sem_inc(t_free[b], 1)
                done(dve.tensor_tensor(conv[:, 2:4], conv[:, 0:2], conv[:, 2:4], ALU.mult))
                dve.wait_ge(conv_sig, c + 1 + 2 * d)
                done(dve.tensor_tensor(conv[:, 2:4], conv[:, 2:4], sig[:], ALU.mult))
                dve.sem_inc(ev("conv_prod"), 1)

            def conv_lo(c, i=None):
                d = i if i is not None else 0
                dve.wait_ge(ev("conv_hi"), c + 1 + 2 * d)
                hi, lo = (v[:, 2 * c:2 * c + 2, :] if i is None else v[:, bass.ds(4 * i + 2 * c, 2), :] for v in actT)
                dve.tensor_tensor(lo, conv[:, 2:4], hi.bitcast(F32), ALU.subtract).then_inc(conv_mul, 1)
                dve.wait_ge(conv_mul, c + 1 + 2 * d)

            ahead(PLAN.unit["UP1"])
            u0 = PLAN.unit["UP1"]
            assert cursor[0] == u0 + AHEAD
            with dve.Fori(0, 5) as i:
                order.enter(i, 20)
                for c in (1, 2):
                    taps(c - 1, i)
                    for k in range(4):
                        split(u0 + 4 * (c - 1) + k + AHEAD, i, 8)
                        if k == 1:
                            conv_taps(c - 1, i)
                        if k == 2:
                            conv_lo(c - 1, i)
                order.leave(5)
            cursor[0] += 40
            taps(10)
            ahead(PLAN.unit["DN0"] + 2)
            conv_taps(10)
            conv_lo(10)
            ahead(PLAN.units)
            gated_residual("gate2", "DN", 40)
            layer_norm("ln2", "y_ready")


_INS = ["x", "mem", "positions", "g_mix", "w_in", "b_gate", "g_ckv", "w_ukv", "g_q_nope", "g_k_nope", "g_q_rope",
        "g_k_rope", "w_gla_gate", "b_gla_gate", "g_gla_out", "g_mem", "w_mem_kv", "g_q_mem", "g_k_mem", "w_o", "g_ffn",
        "w_up", "w_down", "c_2", "ctx_2", "c_ctx_2", "w_mod_2", "b_mod_2", "w_in_2", "b_in_2", "attn_sink_2",
        "q_norm_g_2", "k_norm_g_2", "w_branch_a_2", "w_branch_b_2", "w_out_2", "ln1_g_2", "ln1_b_2", "w_up_2",
        "conv_w_2", "conv_b_2", "w_down_2", "ln2_g_2", "ln2_b_2"]


def build(nc, shapes):
    views = {}
    for name in _INS:
        shape, dt = shapes[name]
        v = nc.dram_tensor(f"in_{name}", shape, dt, kind="ExternalInput").ap()
        views[name] = v[0] if len(shape) > 1 and shape[0] == 1 else v
    out = nc.dram_tensor("out", (1, SEQ, D), F32, kind="ExternalOutput").ap()
    hybrid_kernel(nc, views, out[0])


def kernel(**inputs):
    import concourse.bacc as bacc
    from concourse.bass_utils import run_bass_kernel_spmd

    nc = bacc.Bacc("TRN2", target_bir_lowering=False, num_devices=1)
    arrays = {f"in_{name}": np.ascontiguousarray(inputs[name]) for name in _INS}
    build(nc, {name: (arrays[f"in_{name}"].shape, mybir.dt.from_np(arrays[f"in_{name}"].dtype)) for name in _INS})
    r = run_bass_kernel_spmd(nc, [arrays], core_ids=[0])
    return r.results[0]["out"]
```

```python
from contextlib import ExitStack

import numpy as np

import concourse.bass as bass
import concourse.mybir as mybir

F32 = mybir.dt.float32
F32R = mybir.dt.float32r
I32 = mybir.dt.int32
I8 = mybir.dt.int8
ALU = mybir.AluOpType
ACT = mybir.ActivationFunctionType
AX = mybir.AxisListType

P = 128
D = 1024
SEQ = 256
T = SEQ // P
KT = D // P
NEG = -1e30
EPS = 1e-6

H_MLA, NOPE, ROPE, V_MLA, KV_RANK = 8, 128, 64, 128, 256
H_GLA, DK_GLA, DV_GLA, GATE_RANK = 4, 128, 256, 16
H_MEM, DQ_MEM, DV_MEM = 4, 64, 256
D_FF = 4 * D
WIDTHS = dict(q=H_MLA * (NOPE + ROPE), ck=KV_RANK + ROPE, gq=H_GLA * DK_GLA, gk=H_GLA * DK_GLA,
              gv=H_GLA * DV_GLA, a=GATE_RANK, r=H_GLA * DV_GLA, qm=H_MEM * DQ_MEM, gates=3 * D)
COL = {}
for _name, _w in WIDTHS.items():
    COL[_name] = sum(WIDTHS[n] for n in list(WIDTHS)[:list(WIDTHS).index(_name)])
HEADS, KVH, HD = 8, 2, 64
GROUP = HEADS // KVH
FF2 = 2816
FT2 = FF2 // P
GRID_W = 64
ALPHA = 2.0 ** 0.25
LN_EPS = 1e-5

RING = 4
UNIT = 2
COLS = 512
AHEAD = 3


class Order:

    def __init__(self, eng, sem):
        self.eng, self.sem, self.n, self.i, self.per = eng, sem, 0, None, 0

    def done(self, ins):
        self.n += 1
        ins.then_inc(self.sem, 1)
        self.eng.wait_ge(self.sem, self.n if self.i is None else self.n + self.per * self.i)

    def enter(self, i, per):
        self.i, self.per, self.n0 = i, per, self.n

    def leave(self, times):
        assert self.n - self.n0 == self.per, (self.n - self.n0, self.per)
        self.n += self.per * (times - 1)
        self.i = None


def panels():
    out = [(f"MK{c}", KT, 1) for c in range(3)]
    out += [("AQ", KT, 2)]
    out += [(n, KT, 1) for n in ("CK", "GQ", "GK", "V0", "V1", "R0", "R1", "Q0", "Q1", "Q2", "G20", "G21")]
    out += [(f"UKV{c}", KV_RANK // P, 1) for c in range(4)]
    out += [(f"G{b}{c}", KT, 1) for b in (1, 0) for c in range(2)]
    out += [("WO0", KT, 1), ("WO1", KT, 1), ("CX", KT, 2)]
    out += [(f"WU{c}", KT, 1) for c in range(D_FF // COLS)]
    out += [("WD0", D_FF // P, 1), ("WD1", D_FF // P, 1)]
    out += [(f"IN{c}", KT, 1) for c in range(7)]
    out += [("BA0", KT // 2, 1), ("BA1", KT // 2, 1), ("BB0", KT // 2, 1), ("BB1", KT // 2, 1)]
    out += [("OUT0", KT, 1), ("OUT1", KT, 1)]
    out += [(f"UP{c}", KT, 2) for c in range(FF2 // (COLS // 2))]
    out += [("DN0", FT2, 2), ("DN1", FT2, 2)]
    return out


NARROW = dict(MK0=H_MEM * DQ_MEM, AQ=GATE_RANK + H_MEM * DQ_MEM, CK=KV_RANK + ROPE)


class Plan:

    def __init__(self):
        self.no, self.unit, self.landed, self.cols = {}, {}, [], []
        loads = [0] * RING
        for i, (name, kts, per_unit) in enumerate(panels()):
            self.no[name], self.unit[name] = i, len(self.landed)
            for u in range(len(self.landed), len(self.landed) + kts // UNIT):
                loads[u % RING] += 16 * per_unit
                self.landed.append(loads[u % RING])
                self.cols.append(NARROW.get(name, COLS))
        self.units = len(self.landed)

    def bank(self, name):
        return self.no[name] % 2, self.no[name] // 2


PLAN = Plan()


def uses(names, banks=2):
    return {n: (i % banks, i // banks) for i, n in enumerate(names)}


AB_KEYS, AB_QUERIES, AB_OUT = 12, 13, 18
AB_GATE = 2
MOD_CTX = 4
MOD_LOOP = 3
MOD_UNIT = 3
MOD_DOWN = (2, 8, 17, 21, 26)
MOD_TURN = (9, 14, 22, 27)


AB_STEPS = 2 * HEADS * T
AB_FILL = ["IN4", "IN5", "IN6", "BA0", "BA1"]
AB_LAST = 2


def ab_units(i):
    n, steps = (3 * KT + 2 * KT // 2) // UNIT - AB_LAST, AB_STEPS - 1
    return min(n, (2 * n * i + 3 * steps) // (2 * steps)) if i > 0 else 0


def ab_done(units):
    return next(i for i in range(AB_STEPS) if ab_units(i + 1) >= units)


IN_DONE, BA_DONE = [ab_done(4 * c) for c in (1, 2, 3)], ab_done(14)


def t_names():
    g = lambda n, k: [f"{n}.{i}" for i in range(k)]
    mod = lambda first, n: [f"{v}.{c}" for c in range(first, first + n) for v in ("mod", "modt")]
    out = ["vec.0"] + g("me", 4) + ["vec.1", "vec.2", "vec.3"] + g("h", 4) + ["aT", "z.0", "z.1", "mqT", "mkT", "ck"]
    out += attention_t("MEM", H_MEM)
    out += g("gqT", 2) + g("gkT", 2) + mod(0, 4) + g("go", 4)
    out += ["qn.0", "qn.1", "qn.2", "qn.3", "qr.0", "qr.1", "kp"] + g("kn", 4)
    out += attention_t("MLA", H_MLA)
    out += g("y", 4) + g("hc", 4) + g("h2", 4)
    out += [f"WU{c}.{i}" for c in range(8) for i in range(2)] + g("mod", 12)[MOD_CTX:]
    out += g("x2", 4) + g("kA", 2) + g("qA", 2)
    out += attention_t("AB", 2 * HEADS * T, {AB_GATE: g("gate1", 2), AB_KEYS: g("kB", 2), AB_QUERIES: g("qB", 2),
                                             AB_OUT: g("oab", 4)[:2]})
    out += g("oab", 4)[2:] + g("ym", 4) + g("gate2", 2) + g("x3", 4)
    out += [f"UP{c}.{i}" for c in range(11) for i in range(2)]
    return out


def attention_t(name, n, extra={}):
    out = []
    for i in range(n + 1):
        if i < n:
            out.append(f"{name}.PT{i}")
        if i >= 1:
            out.append(f"{name}.O{i - 1}")
        out += extra.get(i, [])
    return out


T_USE = uses(t_names())
S_USE = uses([f"MEM.{i}" for i in range(H_MEM)] + ["gla.0.0", "gla.0.1", "gla.off"]
             + [f"gla.{s}.{t}" for s in range(1, 8) for t in range(T)]
             + [f"MLA.{i}" for i in range(H_MLA)] + [f"AB.{i}" for i in range(2 * HEADS * T)])
LT_ORDER = ["me", "h", "y", "hc", "h2", "x2", "oab", "ym", "x3"]


def hybrid_kernel(nc, a, out):
    ctx = ExitStack()
    with ctx:
        def sem(name):
            return ctx.enter_context(nc.semaphore(name))

        def sb(name, shape, dt=F32, scope=ctx):
            return scope.enter_context(nc.sbuf_tensor(name, shape, dt))

        acc = [ctx.enter_context(nc.psum_tensor(f"acc{i}", [P, T, COLS], F32)) for i in range(2)]
        tb = [ctx.enter_context(nc.psum_tensor(f"turned{i}", [P, COLS], F32)) for i in range(2)]
        sc = [ctx.enter_context(nc.psum_tensor(f"scores{i}", [P, COLS], F32)) for i in range(2)]

        raw = sb("raw", [P, RING, UNIT, COLS])
        whi = sb("whi", [P, RING, UNIT, COLS], F32R)
        wlo = sb("wlo", [P, RING, UNIT, COLS], F32R)
        x = sb("x_res", [P, T, D])
        lta = [sb(f"lta_{n}", [P, KT, SEQ], F32R) for n in ("hi", "lo")]
        ident = sb("ident", [P, P])
        keep_past = sb("keep_past", [P, P])
        keep_next = sb("keep_next", [P, P])
        vcol = sb("vcol", [P, 96])
        ccol = sb("ccol", [P, 4, 2 * FT2])
        modc = sb("modc", [P, 48])
        modx = sb("modx", [P, 16])
        ln1c = sb("ln1c", [P, 16])
        x3c = sb("x3c", [P, 16])
        one_col = sb("one_col", [P, 1])
        sic = sb("sic", [P, 16])
        rot = sb("rot", [P, 2, T, 64])
        bias = sb("bias", [P, 2, COLS])
        wm = sb("wm", [P, KT // UNIT, UNIT, COLS])
        modrow = sb("modrow", [2, COLS])
        turn = sb("turn", [P, 2, COLS])
        prob = sb("prob", [P, 2, COLS])
        probT = sb("probT", [P, 2, COLS])
        work = sb("work", [P, T, D])
        stat = sb("stat", [P, 8, 16])
        soft = sb("soft", [P, 4, 10])
        gains = sb("gains", [P, 6 * 64 + DV_GLA + HEADS])

        ROWS, at = {}, 0
        for name, n in (("g_mem", 8), ("g_mix", 8), ("g_ffn", 8), ("g_ckv", 2), ("c_2", 8), ("c_ctx_2", 8),
                        ("g_q_nope", 1), ("g_k_nope", 1), ("b_gla_gate", 4), ("b_mod_2", 48)):
            ROWS[name] = (at, n)
            at += n
        assert at == 96

        def col(name, k=0, n=1):
            return vcol[:, ROWS[name][0] + k:ROWS[name][0] + k + n]

        GAIN, at = {}, 0
        for name, n in (("g_q_rope", 64), ("g_k_rope", 64), ("g_q_mem", 64), ("g_k_mem", 64), ("q_norm_g_2", 64),
                        ("k_norm_g_2", 64), ("g_gla_out", DV_GLA), ("attn_sink_2", HEADS)):
            GAIN[name] = gains[:, at:at + n]
            at += n

        one = ExitStack()
        arena = sb("arena", [P, 20736], F32, one)
        ckT = [sb(f"ckT_{n}", [P, 2, SEQ], F32R, one) for n in ("hi", "lo")]
        gmask = sb("gmask", [P, 7, P], I8, one)
        one.close()

        def ar(at, *shape):
            v = arena[:, at:at + int(np.prod(shape))]
            if len(shape) == 1:
                return v
            names = "abcd"[:len(shape)]
            return v.rearrange(f"p ({' '.join(names)}) -> p {' '.join(names)}", **dict(zip(names, shape)))

        o_mem = ar(0, T, D)
        r_gla = ar(2048, T, D)
        o_mla = ar(4096, T, D)
        gqT, gkT = ar(4096, H_GLA, SEQ), ar(5120, H_GLA, SEQ)
        mqT, mkT = ar(4096, 2, SEQ), ar(4608, 2, SEQ)
        decay = ar(6144, H_GLA, SEQ)
        eq, ek = ar(7168, 512), ar(7680, 512)
        rsig = ar(5120, T, COLS)
        angle, turns = ar(13312, T, 64), ar(13440, T, 64)
        q = ar(8192, T, 1536)
        kvm = ar(8192, T, 1280)
        kv = ar(11264, T, 2048)
        memx = ar(11264, T, D)
        attn = ar(11264, 3, H_GLA, P)
        og = ar(6144, T, H_GLA, DV_GLA)
        zb, ze = ar(11264, H_GLA, SEQ), ar(12288, H_GLA, SEQ)
        zflag = ar(13312, H_GLA * T, P)
        wg, aT = ar(14336, 512), ar(14848, SEQ)
        ck = ar(15360, T, 320)
        aq = ar(16000, T, 272)
        gv = ar(16544, T, D)
        gq, gk = ar(18592, T, 512), ar(19616, T, 512)
        gqd, gkd = ar(18592, H_GLA, SEQ), ar(19616, H_GLA, SEQ)
        qnT, knT = ar(15360, H_MLA, SEQ), ar(17408, H_MLA, SEQ)
        qrT, kpT = ar(19456, H_MLA // 2, SEQ), ar(20480, SEQ)
        kpe = work[:, 0, 512:768].rearrange("p (t c) -> p t c", t=T)
        room = ar(4096, T * H_MLA, NOPE)
        qh = ar(8192, T * H_MLA, NOPE + ROPE)
        kh = ar(11264, T * H_MLA, NOPE + V_MLA)[:, :, 0:NOPE]
        og_heads = ar(6144, T * H_GLA, DV_GLA)
        og_sq = probT[:].rearrange("p a b -> p (a b)").rearrange("p (h c) -> p h c", c=DV_GLA)
        vrow = [ar(4096 + 128 * i, 128) for i in range(3)]

        ltb = [sb(f"ltb_{n}", [P, KT, SEQ], F32R) for n in ("hi", "lo")]
        kvx = sb("kvx", [P, T, COLS])
        two = ExitStack()
        msum = [work[:].rearrange("p t (j c) -> p (t j) c", c=COLS), turn]
        ff = [sb(f"ff_{n}", [P, D_FF // P, SEQ], F32R, two) for n in ("hi", "lo")]
        up = [prob, probT]
        two.close()
        diag = sb("diag", [P, KT, P])
        ones = sb("ones", [P, P])
        gate_row = sb("gate_row", [P, D])
        three = ExitStack()
        qkv = sb("qkv", [P, T, 1536], F32, three)
        qT = [sb(f"qT_{b}", [P, HEADS // 2, SEQ], F32, three) for b in "ab"]
        kT = [sb(f"kT_{b}", [P, KVH, 2 * SEQ], F32, three) for b in "ab"]
        kdup = sb("kdup", [P, 2, T, KVH * 2 * HD], F32, three)
        gate2 = sb("gate2", [P, T, 2 * D], F32, three)
        oab = sb("oab", [P, T, D], F32, three)
        ym = work
        three.close()
        four = ExitStack()
        lnrow = sb("lnrow", [P, 2, D], F32, four)
        actT = [sb(f"act_{n}", [P, FT2, SEQ], F32R, four) for n in ("hi", "lo")]
        upv = [prob, probT]
        conv = [sb("conv", [P, 4, SEQ], F32, four)[:], work[:, 0].rearrange("p (j s) -> p j s", j=4)]
        sig = sb("sig", [P, 2, SEQ], F32, four)
        tap = sb("tap", [P, 4, 4], F32, four)
        four.close()

        landed = [sem(f"weights_landed{i}") for i in range(RING)]
        hi_ready, split_ready, unit_used = sem("hi_ready"), sem("split_ready"), sem("unit_used")
        panel_out = [sem(f"panel_out{i}") for i in range(2)]
        t_full = [sem(f"turned_full{i}") for i in range(2)]
        t_free = [sem(f"turned_free{i}") for i in range(2)]
        s_full = [sem(f"scores_full{i}") for i in range(2)]
        s_free = [sem(f"scores_free{i}") for i in range(2)]
        lt_hi, lt_ready = sem("stationary_hi"), sem("stationary_ready")
        soft_ready = sem("maxima_ready")
        mod_landed = [sem(f"mod_landed{i}") for i in range(KT // UNIT)]
        mod_free, mod_sum = sem("mod_free"), sem("mod_sum")
        bias_landed = [sem(f"bias_landed{i}") for i in range(2)]
        bias_used = sem("bias_used")
        gate_in, gate_sig = sem("gate_in"), sem("gate_sigmoid")
        up_done, up_hi = sem("up_done"), sem("up_hi")
        conv_lin, conv_sig, conv_mul, conv_free = sem("conv_lin"), sem("conv_sig"), sem("conv_mul"), sem("conv_free")
        gla_exp, gla_in = sem("gla_exp"), sem("gla_in")
        act_order, dve_order, pool_order = sem("act_order"), sem("dve_order"), sem("pool_order")
        stored = sem("stored")
        once = {}

        def ev(name):
            if name not in once:
                once[name] = sem(name)
            return once[name]

        def rope(eng, done, y1, y2, x1, x2, cos, sin, tmp):
            done(eng.tensor_tensor(y1, x1, cos, ALU.mult))
            done(eng.tensor_tensor(tmp, x2, sin, ALU.mult))
            done(eng.tensor_tensor(y1, y1, tmp, ALU.subtract))
            done(eng.tensor_tensor(y2, x2, cos, ALU.mult))
            done(eng.tensor_tensor(tmp, x1, sin, ALU.mult))
            done(eng.tensor_tensor(y2, y2, tmp, ALU.add))

        def heads(v, n):
            return v.rearrange("p (h c) -> p h c", h=n)

        def rope_2d(eng, done, dst, src, n, t, room):
            def quarter(v, e):
                return v.rearrange("p h (f e c) -> p h f e c", f=2, e=2)[:, :, :, e, :]
            ang = [rot[:, f, t, 32:64].rearrange("p (f c) -> p f c", f=2).unsqueeze(1).broadcast_to([P, n, 2, 16])
                   for f in (1, 0)]
            rope(eng, done, quarter(dst, 0), quarter(dst, 1), quarter(src, 0), quarter(src, 1), *ang,
                 room[:, 0:32 * n].rearrange("p (h f c) -> p h f c", f=2, c=16))

        def keys(eng, done, br):
            k0, x0 = 768 * br + 512, 256 * br
            for t in range(T):
                turned_keys = heads(work[:, t, 512:640], KVH)
                rope_2d(eng, done, turned_keys, heads(qkv[:, t, k0:k0 + 128], KVH), KVH, t, work[:, t, 640:1024])
                for j, src in enumerate((turned_keys, heads(kvx[:, t, x0:x0 + 128], KVH))):
                    done(eng.tensor_copy(kdup[:, j, t, :].rearrange("p (h e c) -> p h e c", e=2, c=HD),
                                         src.unsqueeze(2).broadcast_to([P, KVH, 2, HD])))
            eng.sem_inc(ev(("kA_normed", "kB_normed")[br]), 1)

        def queries(eng, done, br, t):
            src = heads(qkv[:, t, 768 * br:768 * br + 512], HEADS)
            rope_2d(eng, done, heads(work[:, t, 0:512], HEADS), src, HEADS, t, work[:, t, 640:1024])

        def normed(t):
            room = oab[:, t, 512:1024]
            return ((heads(qkv[:, t, 768:1280], HEADS), stat[:, 2, 8 * t:8 * t + 8], "q_norm_g_2", heads(room, HEADS)),
                    (heads(qkv[:, t, 1280:1408], KVH), stat[:, 3, 2 * t:2 * t + 2], "k_norm_g_2",
                     heads(qT[1][:, t, 0:128], KVH)),
                    (heads(kvx[:, t, 256:384], KVH), stat[:, 3, 4 + 2 * t:6 + 2 * t], "k_norm_g_2",
                     heads(qT[1][:, 2 + t, 0:128], KVH)))

        BIASED = ["G20", "G21", "G10", "G11", "G00", "G01", "CX"] + [f"IN{c}" for c in range(7)]
        STEPS = {"MEM": (0, H_MEM), "MLA": (H_MEM, H_MLA), "AB": (H_MEM + H_MLA, 2 * HEADS * T)}
        n_gate = {n: i for i, n in enumerate(BIASED)}

        def lt_done(name, g=3):
            return 4 * LT_ORDER.index(name) + g + 1

        block = ctx.enter_context(nc.Block())

        def rows(w, k):
            return w[k * UNIT * P:(k + 1) * UNIT * P, :].rearrange("(k p) n -> p k n", p=P)

        def loads_of(name, k):
            w, w2 = a["w_in"], a["w_in_2"]
            kind, c = name.rstrip("0123456789"), int("".join(ch for ch in name if ch.isdigit()) or 0)
            if kind == "MK":
                first, n = [(0, 256), (256, COLS), (256 + COLS, COLS)][c]
                return [(0, rows(a["w_mem_kv"], k)[:, :, first:first + n])]
            if kind == "AQ":
                return [(0, rows(w, k)[:, :, COL["a"]:COL["a"] + GATE_RANK]),
                        (GATE_RANK, rows(w, k)[:, :, COL["qm"]:COL["qm"] + 256])]
            if kind == "CX":
                return [(0, rows(w2, k)[:, :, 512:768]), (256, rows(w2, k)[:, :, 1280:1536])]
            if kind == "CK":
                return [(0, rows(w, k)[:, :, COL["ck"]:COL["ck"] + 320])]
            if kind == "G":
                first = COL["gates"] + (c // 10) * D + (c % 10) * COLS
                return [(0, rows(w, k)[:, :, first:first + COLS])]
            where = {"GQ": (w, COL["gq"]), "GK": (w, COL["gk"]), "V": (w, COL["gv"]), "R": (w, COL["r"]),
                     "Q": (w, COL["q"]), "UKV": (a["w_ukv"], 0), "WO": (a["w_o"], 0), "WU": (a["w_up"], 0),
                     "WD": (a["w_down"], 0), "IN": (w2, 0), "BA": (a["w_branch_a_2"], 0),
                     "BB": (a["w_branch_b_2"], 0), "OUT": (a["w_out_2"], 0)}
            src, first = where[kind]
            return [(0, rows(src, k)[:, :, first + c * COLS:first + (c + 1) * COLS])]

        def units_of(name):
            names = list(PLAN.unit)
            i = names.index(name)
            return (PLAN.unit[names[i + 1]] if i + 1 < len(names) else PLAN.units) - PLAN.unit[name]

        @block.sync
        def _(sp):
            for t in range(T):
                sp.dma_start(memx[:, t], a["mem"][t * P:(t + 1) * P, :]).then_inc(ev(f"mem{t}_landed"), 16)

            def bias_load(name):
                n = n_gate[name]
                sp.wait_ge(bias_used, n + 1)
                if name == "CX":
                    for j, first in enumerate((512, 1280)):
                        sp.dma_start(bias[:, n % 2, 256 * j:256 * j + 256],
                                     a["b_in_2"][first:first + 256].partition_broadcast(P))\
                          .then_inc(bias_landed[n % 2], 16)
                    return
                src = a["b_in_2"][int(name[2:]) * COLS:][:COLS] if name.startswith("IN") else \
                    a["b_gate"][int(name[1]) * D + int(name[2]) * COLS:][:COLS]
                sp.dma_start(bias[:, n % 2], src.partition_broadcast(P)).then_inc(bias_landed[n % 2], 16)

            def panel(name):
                for k in range(units_of(name)):
                    u = PLAN.unit[name] + k
                    if k == units_of(name) - 1 and name in n_gate:
                        bias_load(name)
                    sp.wait_ge(split_ready, u + 1)
                    if name.startswith("DN"):
                        for kk in range(UNIT):
                            r = (UNIT * k + kk) * P
                            sp.dma_start(raw[:, u % RING, kk], a["w_down_2"][r:r + P, COLS * int(name[2]):][:, 0:COLS])\
                              .then_inc(landed[u % RING], 16)
                        continue
                    for first, src in loads_of(name, k):
                        sp.dma_start(raw[:, u % RING, :, first:first + src.shape[2]], src)\
                          .then_inc(landed[u % RING], 16)

            for name in PLAN.no:
                if name.startswith("WU"):
                    if name == "WU0":
                        u0 = PLAN.unit[name]
                        with sp.Fori(0, D_FF // COLS) as c:
                            for k in range(KT // UNIT):
                                sp.wait_ge(split_ready, u0 + k + 1 + 4 * c)
                                sp.dma_start(raw[:, (u0 + k) % RING],
                                             rows(a["w_up"], k)[:, :, bass.ds(COLS * c, COLS)])\
                                  .then_inc(landed[(u0 + k) % RING], 16)
                elif name.startswith("UP"):
                    if name == "UP0":
                        u0 = PLAN.unit[name]
                        with sp.Fori(0, FF2 // 256) as c:
                            for k in range(KT // UNIT):
                                sp.wait_ge(split_ready, u0 + k + 1 + 4 * c)
                                for e in range(2):
                                    sp.dma_start(raw[:, (u0 + k) % RING, :, 256 * e:256 * e + 256],
                                                 rows(a["w_up_2"], k)[:, :, bass.ds(FF2 * e + 256 * c, 256)])\
                                      .then_inc(landed[(u0 + k) % RING], 16)
                else:
                    panel(name)
                if name == "MK0":
                    sp.dma_start(x[:], a["x"].rearrange("(t p) d -> p t d", p=P)).then_inc(ev("x_landed"), 16)
                    for row, (first, n) in list(ROWS.items())[1:]:
                        sp.dma_start(vrow[0][first:first + n, :], a[row].rearrange("(r c) -> r c", c=P))\
                          .then_inc(ev("rows_landed"), 16)
                if name == "MK1":
                    for k, src in enumerate((a["conv_w_2"][0], a["conv_w_2"][1], a["conv_w_2"][2], a["conv_b_2"])):
                        sp.dma_start(vrow[1 + k // 2][44 * (k % 2):44 * (k % 2) + 44, :],
                                     src.rearrange("(r c) -> r c", c=P)).then_inc(ev("conv_rows_landed"), 16)
                    for k, vec in enumerate(("ln1_g_2", "ln1_b_2")):
                        sp.dma_start(vrow[1][4 * FT2 + 8 * k:4 * FT2 + 8 * k + 8, :], a[vec].rearrange("(r c) -> r c", c=P))\
                            .then_inc(ev("conv_rows_landed"), 16)
                    sp.dma_start(stat[:, 7, 4:6].bitcast(I32), a["positions"].rearrange("(t p) -> p t", p=P),
                                  allow_slow_non_contiguous=True).then_inc(ev("pos_landed"), 16)
                if name == "G00":
                    b, k = T_USE["qr.1"]
                    sp.wait_ge(t_full[b], k + 1)
                    sp.dma_start(ar(8192, T, D), a["ctx_2"].rearrange("(t p) d -> p t d", p=P))\
                      .then_inc(ev("ctx_landed"), 16)
                if name == "OUT1":
                    b, k = T_USE["ym.3"]
                    sp.wait_ge(t_full[b], k + 1)
                    for i, v in enumerate(("ln1_g_2", "ln1_b_2")):
                        sp.dma_start(lnrow[:, i], a[v].partition_broadcast(P)).then_inc(ev("ln1_landed"), 16)
                if name == "UP10":
                    sp.wait_ge(ev("x3_residual"), 1)
                    for i, v in enumerate(("ln2_g_2", "ln2_b_2")):
                        sp.dma_start(lnrow[:, i], a[v].partition_broadcast(P)).then_inc(ev("ln2_landed"), 16)

            for t in range(T):
                sp.wait_ge(ev("y_ready"), t + 1)
                sp.dma_start(out[t * P:(t + 1) * P, :], x[:, t, :]).then_inc(stored, 16)
            sp.wait_ge(stored, 16 * T)

        @block.gpsimd
        def _(pool):
            order = Order(pool, pool_order)
            order.done(pool.memset(ident[:], 0.0))
            pool.affine_select(out=ident[:], in_=ident[:], compare_op=ALU.not_equal, fill=1.0, base=0,
                               pattern=[[-1, P]], channel_multiplier=1).then_inc(ev("ident_ready"), 1)
            pool.memset(one_col[:], 1.0)
            for m, fill in ((keep_past, 0.0), (keep_next, 0.0), (gmask, 0)):
                ins = pool.memset(m[:], fill)
            order.done(ins)
            pool.affine_select(out=keep_past[:], in_=keep_past[:], compare_op=ALU.is_ge, fill=NEG, base=0,
                               pattern=[[-1, P]], channel_multiplier=1)
            pool.affine_select(out=keep_next[:], in_=keep_next[:], compare_op=ALU.is_ge, fill=NEG, base=0,
                               pattern=[[1, P]], channel_multiplier=-1).then_inc(ev("keeps_ready"), 1)
            freq = ar(13568, 64)
            for i in range(32):
                f = np.float32(1.0) / (np.float32(10000.0) ** np.float32(2 * i / np.float32(ROPE)))
                pool.memset(freq[:, i:i + 1], float(np.float32(f)))
            for i in range(16):
                f = np.float32(10000.0) ** (-np.float32(i) / np.float32(16))
                ins = pool.memset(freq[:, 32 + i:64:16], float(np.float32(f)))
            order.done(ins)
            for half in range(P // GRID_W):
                lane = slice(GRID_W * half, GRID_W * half + GRID_W)
                for t in range(T):
                    order.done(pool.memset(stat[lane, 7, t:t + 1], float(P // GRID_W * t + half)))
                order.done(pool.iota(stat[lane, 7, 2:3].bitcast(I32), pattern=[[0, 1]], base=0, channel_multiplier=1))
            pool.sem_inc(ev("grid_ready"), 1)
            for n, s in enumerate((64, 32, 16, 8, 4, 2, 1)):
                odd = gmask[:, n, :].rearrange("p (m e w) -> p m e w", e=2, w=s)[:, :, 1, :]
                order.done(pool.memset(odd, 1))
                order.done(pool.affine_select(out=odd, in_=odd, compare_op=ALU.is_ge, fill=0.0, base=0,
                                              pattern=[[-2 * s, P // (2 * s)], [0, s]], channel_multiplier=1))
                ins = pool.affine_select(out=odd, in_=odd, compare_op=ALU.is_ge, fill=0.0, base=s - 1,
                                         pattern=[[2 * s, P // (2 * s)], [0, s]], channel_multiplier=-1)
                if n < 6:
                    order.done(ins)
            ins.then_inc(ev("gmask_ready"), 1)
            for name, view in GAIN.items():
                pool.dma_start(view, a[name].partition_broadcast(P)).then_inc(ev("gains_landed"), 16)
            def mod_loads(first, n):
                with pool.Fori(first, first + n) as c:
                    for k in range(KT // UNIT):
                        pool.wait_ge(mod_free, 4 * c + k + 1)
                        pool.dma_start(wm[:, k], rows(a["w_mod_2"], k)[:, :, bass.ds(COLS * c, COLS)])\
                            .then_inc(mod_landed[k], 16)

            mod_loads(0, 5)
            pool.wait_ge(ev("ck_normed"), 1)
            pool.wait_ge(ev("gains_landed"), 16 * len(GAIN))
            pool.wait_ge(ev("rot_ready"), 1)
            pool.wait_ge(gla_exp, 1)
            for t in range(T):
                k_rope = ck[:, t, 256:320]
                order.done(pool.tensor_tensor(k_rope, k_rope, stat[:, 3, 2 + t:3 + t].broadcast_to([P, ROPE]), ALU.mult))
                order.done(pool.tensor_tensor(k_rope, k_rope, GAIN["g_k_rope"], ALU.mult))
            rope(pool, order.done, kpe[:, :, 0:32], kpe[:, :, 32:64], ck[:, :, 256:288], ck[:, :, 288:320],
                 rot[:, 1, :, 0:32], rot[:, 0, :, 0:32], work[:, :, 768:800])
            order.done(pool.tensor_copy(kpe[:, :, 64:128], kpe[:, :, 0:64]))
            pool.sem_inc(ev("kpe_ready"), 1)
            pool.wait_ge(ev("qq_inverse"), 1)
            q_rope = qh[:, :, NOPE:]
            order.done(pool.tensor_tensor(q_rope, q_rope, stat[:, 5, :].unsqueeze(2).broadcast_to([P, T * H_MLA, ROPE]), ALU.mult))
            order.done(pool.tensor_tensor(q_rope, q_rope, GAIN["g_q_rope"].unsqueeze(1).broadcast_to([P, T * H_MLA, ROPE]),
                                          ALU.mult))
            for t in range(T):
                y = work[:, t, 0:512].rearrange("p (h c) -> p h c", c=ROPE)
                x12 = qh[:, H_MLA * t:H_MLA * t + H_MLA, NOPE:]
                ang = [rot[:, f, t, 0:32].unsqueeze(1).broadcast_to([P, H_MLA, 32]) for f in (1, 0)]
                rope(pool, order.done, y[:, :, 0:32], y[:, :, 32:64], x12[:, :, 0:32], x12[:, :, 32:], *ang,
                     work[:, t, 768:1024].rearrange("p (h c) -> p h c", c=32))
            pool.sem_inc(ev("rope_turned"), 1)
            mod_loads(5, 6 * D // COLS - 5)
            b, k = T_USE["x2.0"]
            pool.wait_ge(t_full[b], k + 1)
            pool.memset(ones[:], 1.0).then_inc(ev("ones_ready"), 1)
            for name in ("IN1", "IN2"):
                s, k = PLAN.bank(name)
                pool.wait_ge(panel_out[s], k + 2)
            for t in range(T):
                for v, _, _, square in normed(t):
                    order.done(pool.tensor_tensor(square, v, v, ALU.mult))
                pool.sem_inc(ev("ab_sq"), 1)
            pool.wait_ge(ev("ab_inverse"), 1)
            for t in range(T):
                for v, s, gain, _ in normed(t):
                    order.done(pool.tensor_tensor(v, v, s.unsqueeze(2).broadcast_to([P, v.shape[1], HD]), ALU.mult))
                    order.done(pool.tensor_tensor(v, v, GAIN[gain].unsqueeze(1).broadcast_to([P, v.shape[1], HD]), ALU.mult))
            pool.wait_ge(ev("qA_normed"), 1)
            b, k = T_USE["qA.1"]
            pool.wait_ge(t_full[b], k + 1)
            keys(pool, order.done, 1)
            for t in range(T):
                queries(pool, order.done, 1, t)
            pool.sem_inc(ev("qB_normed"), 1)

            pool.wait_ge(ev("ln1_landed"), 32)
            b, k = T_USE["x3.3"]
            pool.wait_ge(t_full[b], k + 1)
            order.done(pool.tensor_tensor(x[:], x[:], lnrow[:, 0].unsqueeze(1).broadcast_to([P, T, D]), ALU.mult))
            pool.tensor_tensor(x[:], x[:], lnrow[:, 1].unsqueeze(1).broadcast_to([P, T, D]), ALU.add)\
                .then_inc(ev("x3_residual"), 1)

            pool.sem_inc(conv_free, 2)

            def conv_product(c, i=None):
                d, cv = i if i is not None else 0, conv[c % 2]
                pool.wait_ge(ev("conv_sums"), c + 1 + 2 * d)
                order.done(pool.tensor_tensor(cv[:, 2:4], cv[:, 0:2], cv[:, 2:4], ALU.mult))
                pool.wait_ge(conv_sig, c + 1 + 2 * d)
                pool.tensor_tensor(cv[:, 2:4], cv[:, 2:4], sig[:], ALU.mult).then_inc(ev("conv_prod"), 1)
                pool.wait_ge(ev("conv_hi"), c + 1 + 2 * d)
                hi, lo = (v[:, 2 * c:2 * c + 2, :] if i is None else v[:, bass.ds(4 * i + 2 * c, 2), :] for v in actT)
                pool.tensor_tensor(lo, cv[:, 2:4], hi.bitcast(F32), ALU.subtract).then_inc(conv_mul, 1)
                pool.wait_ge(conv_mul, c + 1 + 2 * d)
                pool.sem_inc(conv_free, 1)

            with pool.Fori(0, 5) as i:
                order.enter(i, 2)
                for c in range(2):
                    conv_product(c, i)
                order.leave(5)
            conv_product(10)

        @block.tensor
        def _(pe):
            pe.sem_inc(unit_used, RING)

            def unit(name, k, lhs, n=COLS, first_kt=None, i=None, per=0):
                u, (s, cnt) = PLAN.unit[name] + k, PLAN.bank(name)
                du, dc = (per * i, per // 8 * i) if i is not None else (0, 0)
                kt0 = UNIT * k if first_kt is None else first_kt
                last = k == units_of(name) - 1
                if k == 0:
                    pe.wait_ge(panel_out[s], cnt + 1 + dc)
                pe.wait_ge(split_ready, RING + u + 1 + du)
                for t in range(T):
                    for kk in range(UNIT):
                        tok = slice(t * P, (t + 1) * P)
                        pairs = [(1, whi), (0, whi), (0, wlo)]
                        for j, (part, w) in enumerate(pairs):
                            ins = pe.matmul(acc[s][:, t, 0:n], lhs[part][:, kt0 + kk, tok], w[:, u % RING, kk, 0:n],
                                            start=(k == 0 and kk == 0 and j == 0),
                                            stop=(last and kk == UNIT - 1 and j == 2))
                ins.then_inc(unit_used, 1)

            def panel(name, lhs, n=COLS, new=None):
                for k in range(units_of(name)):
                    if new:
                        lt_wait(new, k)
                    unit(name, k, lhs, n)

            def t_begin(name):
                b, k = T_USE[name]
                pe.wait_ge(t_free[b], k + 1)
                return tb[b], t_full[b]

            def turn_tokens(name, src, kts=KT, ready=None, per=2, groups=None):
                for g in groups or range(kts // 2):
                    if ready and g % per == 0:
                        pe.wait_ge(ev(ready), g // per + 1)
                    bank, full = t_begin(f"{name}.{g}" if kts > 2 else name)
                    for kk in range(2):
                        for t in range(T):
                            c = P * (2 * g + kk)
                            ins = pe.transpose(bank[:, 256 * kk + P * t:256 * kk + P * t + P],
                                               src[:, t, c:c + P], ident[:])
                    ins.then_inc(full, 1)

            def s_begin(name):
                b, k = S_USE[name]
                pe.wait_ge(s_free[b], k + 1)
                return sc[b], s_full[b]

            def attend(name, n, scores, blocks, values, fill_a=None, fill_b=None, after=None):
                def score(i):
                    bank, full = s_begin(f"{name}.{i}")
                    scores(i, bank).then_inc(full, 1)

                score(0)
                for i in range(n + 1):
                    if i + 1 < n:
                        score(i + 1)
                    if i < n:
                        if fill_a:
                            fill_a(i)
                        b, k = S_USE[f"{name}.{i}"]
                        pe.wait_ge(s_free[b], k + 2)
                        bank, full = t_begin(f"{name}.PT{i}")
                        for j in range(blocks):
                            ins = pe.transpose(bank[:, P * j:P * j + P],
                                               prob[:, (STEPS[name][0] + i) % 2, P * j:P * j + P], ident[:])
                        ins.then_inc(full, 1)
                        if fill_b:
                            fill_b(i)
                    if i >= 1:
                        b, k = T_USE[f"{name}.PT{i - 1}"]
                        pe.wait_ge(t_free[b], k + 2)
                        bank, full = t_begin(f"{name}.O{i - 1}")
                        values(i - 1, bank, probT[:, (STEPS[name][0] + i - 1) % 2, :]).then_inc(full, 1)
                    if after:
                        after(i)

            def mod_panel(c):
                bank, full = t_begin(f"mod.{c}")
                if c == 0:
                    pe.wait_ge(ev("sic_ready"), 1)
                pe.wait_ge(mod_free, 4 * c + 4)
                for k in range(KT // UNIT):
                    pe.wait_ge(mod_landed[k], 16 * (c + 1))
                    for kk in range(UNIT):
                        kt = UNIT * k + kk
                        ins = pe.matmul(bank[0:2, :], sic[:, kt:kt + KT + 1:KT], wm[:, k, kk],
                                        start=(kt == 0), stop=(kt == KT - 1))
                    ins.then_inc(mod_free if kt < KT - 1 else full, 1)

            def mod_turn(c):
                b, k = T_USE[f"mod.{c}"]
                pe.wait_ge(t_free[b], k + 2)
                bank, full = t_begin(f"modt.{c}")
                for j in range(4):
                    ins = pe.transpose(bank[:, 2 * j:2 * j + 2], modrow[:, P * j:P * j + P], ident[0:2, 0:2])
                ins.then_inc(full, 1)

            def lt_wait(name, g=3):
                pe.wait_ge(lt_ready, lt_done(name, g))

            def vectors(g, src, n):
                bank, full = t_begin(f"vec.{g}")
                pe.transpose(bank[:, 0:n], src[0:n, :], ident[0:n, 0:n]).then_inc(full, 1)

            pe.wait_ge(ev("ident_ready"), 1)
            pe.wait_ge(ev("g_mem_landed"), 16)
            vectors(0, vrow[0], ROWS["g_mem"][1])
            for t in range(T):
                pe.wait_ge(ev(f"mem{t}_landed"), 16)
            turn_tokens("me", memx)
            panel("MK0", ltb, 256, new="me")
            pe.wait_ge(ev("rows_landed"), 16 * (len(ROWS) - 1))
            vectors(1, vrow[0], 96)
            panel("MK1", ltb)
            pe.wait_ge(ev("conv_rows_landed"), 16 * 6)
            vectors(2, vrow[1], 4 * FT2 + 16)
            vectors(3, vrow[2], 4 * FT2)
            for k in range(4):
                if k == 1:
                    pe.wait_ge(ev("h_scaled"), T)
                if k >= 2:
                    turn_tokens("h", work, groups=(2 * k - 4, 2 * k - 3))
                unit("MK2", k, ltb)

            panel("AQ", lta, NARROW["AQ"], new="h")
            panel("CK", lta, NARROW["CK"])
            s, k = PLAN.bank("AQ")
            pe.wait_ge(panel_out[s], k + 2)
            bank, full = t_begin("aT")
            for t in range(T):
                ins = pe.transpose(bank[:, P * t:P * t + P], aq[:, t, 0:P], ident[:])
            ins.then_inc(full, 1)
            panel("GQ", lta)
            b, k = T_USE["aT"]
            pe.wait_ge(t_free[b], k + 2)
            pe.wait_ge(ev("wg_landed"), 16)
            for g in range(2):
                bank, full = t_begin(f"z.{g}")
                for j in range(2):
                    h = 2 * g + j
                    ins = pe.matmul(bank[:, 256 * j:256 * j + 256], wg[0:GATE_RANK, P * h:P * h + P],
                                    aT[0:GATE_RANK, :], start=True, stop=True)
                ins.then_inc(full, 1)
            panel("GK", lta)
            panel("V0", lta)

            for name, src in (("mqT", aq[:, :, GATE_RANK:272]), ("mkT", kvm[:, :, 0:256])):
                pe.wait_ge(ev(f"{name}_normed"), 1)
                turn_tokens(name, src, 2)
            pe.wait_ge(ev("ck_normed"), 1)
            turn_tokens("ck", ck, 2)
            for name in ("mqT", "mkT"):
                b, k = T_USE[name]
                pe.wait_ge(t_free[b], k + 2)

            def mem_scores(h, bank):
                lane = slice(64 * (h % 2), 64 * (h % 2) + 64)
                for t in range(T):
                    ins = pe.matmul(bank[:, 256 * t:256 * t + 256], mqT[lane, h // 2, P * t:P * t + P],
                                    mkT[lane, h // 2, :], start=True, stop=True)
                return ins

            def mem_values(h, bank, pT):
                for t in range(T):
                    for kt in range(T):
                        ins = pe.matmul(bank[:, 256 * t:256 * t + 256], pT[:, 256 * t + P * kt:256 * t + P * kt + P],
                                        kvm[:, kt, 256 + 256 * h:512 + 256 * h], start=(kt == 0), stop=(kt == T - 1))
                return ins

            def fill(names, first, n):
                for j in range(first, first + n):
                    unit(names[j // 4], j % 4, lta)

            vr = ["V1", "R0", "R1", "Q0"]
            attend("MEM", H_MEM, mem_scores, 4, mem_values, lambda i: fill(vr, 4 * i, 2),
                   lambda i: fill(vr, 4 * i + 2, 2))

            for name, src in (("gqT", gq), ("gkT", gk)):
                turn_tokens(name, src, 4)
            for g in ("gqT.0", "gqT.1", "gkT.0", "gkT.1"):
                b, k = T_USE[g]
                pe.wait_ge(t_free[b], k + 2)
            qg = ["Q1", "Q2", "G20", "G21"]
            for s in range(9):
                lhs, rhs = (gkT, gqT) if s == 0 else (gkd, gqd)
                if s >= 1:
                    pe.wait_ge(gla_in, s)
                if s == 1:
                    bank, full = s_begin("gla.off")
                    for h in range(H_GLA):
                        ins = pe.matmul(bank[:, P * h:P * h + P], lhs[:, h, 0:P], rhs[:, h, P:2 * P],
                                        start=True, stop=True)
                    ins.then_inc(full, 1)
                else:
                    for t in range(T):
                        bank, full = s_begin(f"gla.{max(s - 1, 0)}.{t}")
                        for h in range(H_GLA):
                            tok = slice(P * t, P * t + P)
                            ins = pe.matmul(bank[:, P * h:P * h + P], lhs[:, h, tok], rhs[:, h, tok],
                                            start=True, stop=True)
                        ins.then_inc(full, 1)
                if s < 8:
                    fill(qg, 2 * s, 2)
                if s % 2 == 1:
                    mod_panel(s // 2)
                elif s >= 2:
                    mod_turn(s // 2 - 1)
            for name in ("gla.off", "gla.7.0", "gla.7.1"):
                b, k = S_USE[name]
                pe.wait_ge(s_free[b], k + 2)
            for t in range(T):
                for g in range(2):
                    bank, full = t_begin(f"go.{2 * t + g}")
                    for j in range(2):
                        h = 2 * g + j
                        o = bank[:, 256 * j:256 * j + 256]
                        if t == 1:
                            pe.matmul(o, attn[:, 2, h, :], gv[:, 0, 256 * h:256 * h + 256], start=True, stop=False)
                        ins = pe.matmul(o, attn[:, t, h, :], gv[:, t, 256 * h:256 * h + 256],
                                        start=(t == 0), stop=True)
                    ins.then_inc(full, 1)

            pe.wait_ge(ev("ckT_ready"), 1)
            for c in range(4):
                unit(f"UKV{c}", 0, ckT)
            panel("G10", lta)
            pe.wait_ge(ev("qn_normed"), 1)
            for g in range(4):
                bank, full = t_begin(f"qn.{g}")
                for j in range(2):
                    for t in range(T):
                        c = 192 * (2 * g + j)
                        ins = pe.transpose(bank[:, 256 * j + P * t:256 * j + P * t + P], q[:, t, c:c + P], ident[:])
                ins.then_inc(full, 1)
                unit("G11", g, lta)
            pe.wait_ge(ev("rope_turned"), 1)
            for g in range(2):
                bank, full = t_begin(f"qr.{g}")
                for j in range(2):
                    for t in range(T):
                        ins = pe.transpose(bank[:, 256 * j + P * t:256 * j + P * t + P],
                                           work[:, t, 0:512][:, P * (2 * g + j):P * (2 * g + j) + P], ident[:])
                ins.then_inc(full, 1)
            bank, full = t_begin("kp")
            for t in range(T):
                ins = pe.transpose(bank[:, P * t:P * t + P], kpe[:, t, :], ident[:])
            ins.then_inc(full, 1)
            pe.wait_ge(ev("k_normed"), 1)
            for g in range(4):
                bank, full = t_begin(f"kn.{g}")
                for j in range(2):
                    for t in range(T):
                        c = 256 * (2 * g + j)
                        ins = pe.transpose(bank[:, 256 * j + P * t:256 * j + P * t + P], kv[:, t, c:c + P], ident[:])
                ins.then_inc(full, 1)
            for g in ("kn.2", "kn.3"):
                b, k = T_USE[g]
                pe.wait_ge(t_free[b], k + 2)

            def mla_scores(h, bank):
                lane = slice(64 * (h % 2), 64 * (h % 2) + 64)
                for t in range(T):
                    o = bank[:, P * t:P * t + P * (t + 1)]
                    pe.matmul(o, qnT[:, h, P * t:P * t + P], knT[:, h, 0:P * (t + 1)], start=True, stop=False)
                    ins = pe.matmul(o, qrT[lane, h // 2, P * t:P * t + P], kpT[lane, 0:P * (t + 1)],
                                    start=False, stop=True)
                return ins

            def mla_values(h, bank, pT):
                for t in range(T):
                    for kt in range(t + 1):
                        ins = pe.matmul(bank[:, P * t:P * t + P], pT[:, P * (t + kt):P * (t + kt) + P],
                                        kv[:, kt, 256 * h + P:256 * h + 2 * P], start=(kt == 0), stop=(kt == t))
                return ins

            attend("MLA", H_MLA, mla_scores, 3, mla_values, lambda i: fill(["G00", "G01"], i, 1))

            turn_tokens("y", r_gla, ready="branches_mixed", groups=(0, 1))
            for k in range(4):
                if k == 1:
                    turn_tokens("y", r_gla, ready="branches_mixed", groups=(2, 3))
                lt_wait("y", k)
                unit("WO0", k, lta)
            pe.wait_ge(ev("ctx_landed"), 16)
            for k in range(4):
                if k % 2 == 0:
                    turn_tokens("hc", ar(8192, T, D), groups=(k, k + 1))
                unit("WO1", k, lta)
            for k in range(4):
                if k == 3:
                    pe.wait_ge(ev("h2_scaled"), T)
                    turn_tokens("h2", work, groups=(0, 1))
                lt_wait("hc", k)
                unit("CX", k, ltb)

            turn_tokens("h2", work, groups=(2, 3))

            def up_turn(c, i=None):
                pe.wait_ge(up_done, c + 1 + (2 * i if i is not None else 0))
                for g in range(2):
                    b, k = T_USE[f"WU{c}.{g}"]
                    pe.wait_ge(t_free[b], k + 1 + (2 * i if i is not None else 0))
                    for kk in range(2):
                        for t in range(T):
                            ins = pe.transpose(tb[b][:, 256 * kk + P * t:256 * kk + P * t + P],
                                               up[c % 2][:, t, P * (2 * g + kk):P * (2 * g + kk) + P], ident[:])
                    ins.then_inc(t_full[b], 1)

            panel("WU0", lta, new="h2")
            with pe.Fori(0, 3) as i:
                for c in (1, 2):
                    for k in range(4):
                        unit(f"WU{c}", k, lta, i=i, per=8)
                        if k == 1:
                            up_turn(c - 1, i)
            for k in range(4):
                unit("WU7", k, lta)
                if k == 1:
                    up_turn(6)

            def mod_columns(c):
                bank, full = t_begin(f"mod.{c}")
                n = c - MOD_CTX
                pe.wait_ge(mod_sum, n + 1)
                src = msum[0][:, n] if n < MOD_LOOP else msum[1][:, n % 2]
                for j in range(4):
                    ins = pe.matmul(bank[:, 2 * j:2 * j + 1], src[:, P * j:P * j + P], one_col[:], start=True, stop=True)
                ins.then_inc(full, 1)

            pe.wait_ge(ev("keeps_ready"), 1)
            for c in range(2):
                for k in range(D_FF // P // UNIT):
                    if c == 0 and k == 2:
                        up_turn(7)
                    n = units_of("WD0") * c + k
                    if 0 <= n - MOD_UNIT < MOD_LOOP:
                        mod_columns(MOD_CTX + n - MOD_UNIT)
                    if n == 2 * units_of("WD0") - 1:
                        mod_columns(6 * D // COLS - 1)
                        s, u = PLAN.bank("WD0")
                        pe.wait_ge(panel_out[s], u + 2)
                        turn_tokens("x2", x, groups=(0, 1))
                    if n in MOD_TURN:
                        mod_columns(MOD_CTX + MOD_LOOP + MOD_TURN.index(n))
                    if c == 0 and k % 2 == 0:
                        for g in range(2):
                            b, n = T_USE[f"WU{k // 2}.{g}"]
                            pe.wait_ge(t_free[b], n + 2)
                    unit(f"WD{c}", k, ff)

            for k in range(4):
                if k == 1:
                    p, n = PLAN.bank("WD1")
                    pe.wait_ge(panel_out[p], n + 2)
                    turn_tokens("x2", x, groups=(2, 3))
                lt_wait("x2", k)
                unit("IN0", k, lta)
            for c in (1, 2, 3):
                panel(f"IN{c}", lta)

            def turn_keys(br):
                name = ("kA", "kB")[br]
                pe.wait_ge(ev(f"{name}_normed"), 1)
                for g in range(KVH):
                    bank, full = t_begin(f"{name}.{g}")
                    for j in range(2):
                        for t in range(T):
                            ins = pe.transpose(bank[:, 256 * j + P * t:256 * j + P * t + P],
                                               kdup[:, j, t, P * g:P * g + P], ident[:])
                    ins.then_inc(full, 1)

            def turn_queries(br):
                name = ("qA", "qB")[br]
                pe.wait_ge(ev(f"{name}_normed"), 1)
                for g in range(2):
                    bank, full = t_begin(f"{name}.{g}")
                    for j in range(2):
                        for t in range(T):
                            c = P * (2 * g + j)
                            ins = pe.transpose(bank[:, 256 * j + P * t:256 * j + P * t + P],
                                               work[:, t, c:c + P], ident[:])
                    ins.then_inc(full, 1)

            def turned(*names):
                for g in names:
                    b, k = T_USE[g]
                    pe.wait_ge(t_free[b], k + 2)

            turn_keys(0)
            turn_queries(0)
            turned("kA.0", "kA.1", "qA.0", "qA.1")

            def ab_step(i):
                return i // (HEADS * T), i % (HEADS * T) // T, i % T

            def ab_scores(i, bank):
                br, h, t = ab_step(i)
                lane = slice(64 * (h % 2), 64 * (h % 2) + 64)
                return pe.matmul(bank[:, :], qT[br][lane, h // 2, P * t:P * t + P], kT[br][lane, h // GROUP, :],
                                 start=True, stop=True)

            def ab_values(i, bank, pT):
                br, h, t = ab_step(i)
                for kt in range(4):
                    v = qkv[:, kt, 768 * br + 640:768 * br + 768] if kt < 2 else \
                        kvx[:, kt - 2, 256 * br + 128:256 * br + 256]
                    ins = pe.matmul(bank[:, 0:HD], pT[:, P * kt:P * kt + P], v[:, HD * (h // GROUP):][:, 0:HD],
                                    start=(kt == 0), stop=(kt == 3))
                return ins

            def ab_unit(j):
                if j < 12:
                    unit(AB_FILL[j // 4], j % 4, lta)
                    return
                if j == 12:
                    lt_wait("oab", 1)
                unit(AB_FILL[3 + (j - 12) // 2], j % 2, ltb, first_kt=2 * (j % 2))

            def ab_fill(i):
                for j in range(ab_units(i), ab_units(i + 1)):
                    ab_unit(j)

            def turn_out(first, last):
                for g in range(first, last):
                    bank, full = t_begin(f"oab.{g}")
                    for kk in range(2):
                        for t in range(T):
                            c = P * (2 * g + kk)
                            ins = pe.transpose(bank[:, 256 * kk + P * t:256 * kk + P * t + P], oab[:, t, c:c + P], ident[:])
                    ins.then_inc(full, 1)

            def gate_rows(name):
                pe.wait_ge(ev("ones_ready"), 1)
                pe.wait_ge(ev(f"{name}_diag"), 1)
                for g in range(2):
                    bank, full = t_begin(f"{name}.{g}")
                    for j in range(4):
                        ins = pe.matmul(bank[:, P * j:P * j + P], ones[:], diag[:, 4 * g + j, :], start=True, stop=True)
                    ins.then_inc(full, 1)

            def ab_between(i):
                if i == AB_GATE:
                    gate_rows("gate1")
                elif i == AB_KEYS:
                    turn_keys(1)
                elif i == AB_QUERIES:
                    turn_queries(1)
                elif i == AB_QUERIES + 1:
                    turned("kB.0", "kB.1", "qB.0", "qB.1")
                elif i == AB_OUT:
                    turned("AB.O14", "AB.O15")
                    turn_out(0, 2)

            attend("AB", 2 * HEADS * T, ab_scores, 4, ab_values, ab_fill, after=ab_between)

            ab_unit(14)
            turned(f"AB.O{AB_STEPS - 1}", f"AB.O{AB_STEPS - 2}")
            turn_out(2, 4)
            ab_unit(15)
            lt_wait("oab")
            for name in ("BB0", "BB1"):
                for k in range(2):
                    if name == "BB1" and k == 1:
                        turn_tokens("ym", ym, ready="ym_ready", per=1, groups=(0, 1))
                    unit(name, k, ltb, first_kt=4 + 2 * k)
            for k in range(4):
                if k == 2:
                    turn_tokens("ym", ym, ready="ym_ready", per=1, groups=(2, 3))
                lt_wait("ym", k)
                unit("OUT0", k, lta)
            panel("OUT1", lta)

            gate_rows("gate2")
            turn_tokens("x3", x, ready="x3_ready")

            def conv_turn(c, i=None):
                s, k = PLAN.bank(f"UP{c}")
                pe.wait_ge(panel_out[s], k + 2 + (i if i is not None else 0))
                for g in range(2):
                    b, k = T_USE[f"UP{c}.{g}"]
                    pe.wait_ge(t_free[b], k + 1 + (2 * i if i is not None else 0))
                    for kk in range(2):
                        for t in range(T):
                            ins = pe.transpose(tb[b][:, 256 * kk + P * t:256 * kk + P * t + P],
                                               upv[c % 2][:, t, P * (2 * g + kk):P * (2 * g + kk) + P], ident[:])
                    ins.then_inc(t_full[b], 1)

            panel("UP0", ltb, new="x3")
            with pe.Fori(0, 5) as i:
                for c in (1, 2):
                    for k in range(4):
                        unit(f"UP{c}", k, ltb, i=i, per=8)
                        if k == 1:
                            conv_turn(c - 1, i)
            for c in range(2):
                for k in range(FT2 // UNIT):
                    if c == 0 and k == 2:
                        conv_turn(10)
                    if c == 0:
                        pe.wait_ge(conv_mul, k + 1)
                    unit(f"DN{c}", k, actT)

        def last_unit(name):
            return PLAN.unit[name] + units_of(name) - 1

        @block.scalar
        def _(act):
            order = Order(act, act_order)

            def split(u, i=None, per=0, landings=0):
                s = u % RING
                du = per * i if i is not None else 0
                act.wait_ge(landed[s], PLAN.landed[u] + (landings * i if i is not None else 0))
                act.wait_ge(unit_used, u + 1 + du)
                n = PLAN.cols[u]
                act.copy(whi[:, s, :, 0:n], raw[:, s, :, 0:n]).then_inc(hi_ready, 1)

            cursor = [0]

            def ahead(pos):
                while cursor[0] < min(pos + AHEAD, PLAN.units):
                    split(cursor[0])
                    cursor[0] += 1

            def panel_wait(name, du=0):
                act.wait_ge(unit_used, RING + last_unit(name) + 1 + du)

            def evac(name, dst, n=COLS, func=ACT.Copy):
                ahead(last_unit(name) + 1)
                panel_wait(name)
                s, _ = PLAN.bank(name)
                act.activation(dst, acc[s][:, :, 0:n], func).then_inc(panel_out[s], 1)

            def lt_act(name, lt, groups=range(4), before=None):
                for g in groups:
                    if before:
                        before(g)
                    b, k = T_USE[f"{name}.{g}"]
                    act.wait_ge(t_free[b], k + 2)
                    act.copy(lt[0][:, 2 * g:2 * g + 2, :].rearrange("p a b -> p (a b)"), turn[:, g % 2])\
                        .then_inc(lt_hi, 1)

            def sqrt(name, view):
                act.wait_ge(ev(f"{name}_var"), 1)
                act.activation(view, view, ACT.Sqrt).then_inc(ev(f"{name}_std"), 1)

            def t_out(name, dst, n=COLS, scale=1.0, parts=None):
                b, k = T_USE[name]
                act.wait_ge(t_full[b], k + 1)
                act.activation(dst, tb[b][0:(parts or P), 0:n], ACT.Copy, scale=scale).then_inc(t_free[b], 1)

            def attend(name, n, exps, at_scores, at_turn, blocks, after=None):
                def exp(i):
                    ahead(at_scores(i))
                    g = STEPS[name][0] + i
                    b, _ = S_USE[f"{name}.{i}"]
                    act.wait_ge(soft_ready, g + 1)
                    exps(i, g % 2, g % 4, sc[b]).then_inc(s_free[b], 1)

                exp(0)
                for i in range(n):
                    ahead(at_turn(i))
                    if i >= 2:
                        b, k = T_USE[f"{name}.O{i - 2}"]
                        act.wait_ge(t_full[b], k + 1)
                    t_out(f"{name}.PT{i}", probT[:, (STEPS[name][0] + i) % 2, 0:P * blocks], P * blocks)
                    if i + 1 < n:
                        exp(i + 1)
                    if after:
                        after(i)

            act.dma_start(vrow[0][0:ROWS["g_mem"][1], :], a["g_mem"].rearrange("(r c) -> r c", c=P))\
                .then_inc(ev("g_mem_landed"), 16)
            lt_act("me", ltb, before=lambda g: ahead(g - 2))
            for name, src, s in (("me", memx, 0), ("h", x[:], 1)):
                for t in range(T):
                    act.wait_ge(ev(f"mem{t}_landed" if name == "me" else "x_landed"), 16)
                    act.activation(prob[:].rearrange("p a b -> p (a b)"), src[:, t, :], ACT.Square,
                                   accum_out=stat[:, s, t:t + 1]).then_inc(ev(f"{name}_sum"), 1)
                    act.wait_ge(ev(f"{name}_sum"), t + 1)
                ahead(2 + s)
            for name, s in (("me", 0), ("h", 1)):
                sqrt(name, stat[:, s, 2:4])

            def normed_memory(name, dst, n):
                ahead(last_unit(name) + 1)
                panel_wait(name)
                act.wait_ge(ev("me_inverse"), 1)
                s, _ = PLAN.bank(name)
                for t in range(T):
                    ins = act.activation(dst[:, t], acc[s][:, t, 0:n], ACT.Copy, scale=stat[:, 0, 2 + t:3 + t])
                ins.then_inc(panel_out[s], 1)

            normed_memory("MK0", kvm[:, :, 0:256], 256)
            normed_memory("MK1", kvm[:, :, 256:768], COLS)
            act.wait_ge(ev("rot_arg"), 1)
            act.activation(rot[:, 0:2], rot[:, 0:2], ACT.Sin).then_inc(ev("rot_ready"), 1)
            ahead(PLAN.unit["MK2"] + 2)
            lt_act("h", lta, (0, 1))
            ahead(PLAN.unit["MK2"] + 3)
            lt_act("h", lta, (2, 3))
            normed_memory("MK2", kvm[:, :, 768:1280], COLS)
            act.dma_start(wg[0:GATE_RANK, :], a["w_gla_gate"]).then_inc(ev("wg_landed"), 16)
            evac("AQ", aq[:], NARROW["AQ"])
            evac("CK", ck, NARROW["CK"])
            t_out("aT", aT[0:GATE_RANK, :], 256, parts=GATE_RANK)
            sqrt("mm", stat[:, 2, 0:16])
            evac("GQ", gq)
            act.wait_ge(ev("zb_ready"), 1)
            order.done(act.activation(ze, zb, ACT.Abs))
            ahead(PLAN.unit["GK"] + 1)
            order.done(act.activation(ze, ze, ACT.Exp, scale=-1.0))
            ahead(PLAN.unit["GK"] + 2)
            act.activation(ze, ze, ACT.Ln, bias=1.0).then_inc(ev("zln_ready"), 1)
            sqrt("ck", stat[:, 3, 0:4])
            evac("GK", gk)
            evac("V0", gv[:, :, 0:COLS])
            for name, dst in (("mqT", mqT), ("mkT", mkT)):
                t_out(name, dst.rearrange("p a b -> p (a b)"))
            act.wait_ge(ev("ck_turned"), 1)
            act.copy(ckT[0][:].rearrange("p a b -> p (a b)"), turn[:, 0]).then_inc(ev("ckT_hi"), 1)

            def mem_exps(i, slot, row, bank):
                for t in range(T):
                    ins = act.activation(prob[:, slot, 256 * t:256 * t + 256], bank[:, 256 * t:256 * t + 256], ACT.Exp,
                                         bias=soft[:, row, 2 + t:3 + t], scale=DQ_MEM ** -0.5,
                                         accum_out=soft[:, row, 4 + t:5 + t])
                return ins

            def mem_after(i):
                if i == 0:
                    evac("V1", gv[:, :, COLS:2 * COLS])
                elif i < 3:
                    name = f"R{i - 1}"
                    ahead(last_unit(name) + 1)
                    panel_wait(name)
                    if i == 2:
                        b, k = PLAN.bank("R0")
                        act.wait_ge(panel_out[b], k + 2)
                    act.activation(rsig, acc[PLAN.bank(name)[0]][:], ACT.Sigmoid).then_inc(ev("r_sig"), 1)
                    if i == 1:
                        act.wait_ge(ev("vec_ready"), 1)
                        act.activation(sic[:], vcol[:, ROWS["c_2"][0]:ROWS["c_2"][0] + 16], ACT.Sigmoid)\
                            .then_inc(ev("c_sig"), 1)

            def gate(name):
                ahead(last_unit(name) + 1)
                act.wait_ge(gate_in, BIASED.index(name) + 1)
                p = acc[PLAN.bank(name)[0]]
                act.activation(p[:], p[:], ACT.Sigmoid).then_inc(gate_sig, 1)

            u0 = PLAN.unit["V1"]
            attend("MEM", H_MEM, mem_exps, lambda i: u0 + 4 * max(i - 1, 0), lambda i: u0 + 4 * i + 2, 4, mem_after)

            b, k = T_USE[f"MEM.O{H_MEM - 1}"]
            act.wait_ge(t_full[b], k + 1)
            ahead(last_unit("Q0") + 1)
            for name, dst, f in (("gqT", gqT, DK_GLA ** -0.5), ("gkT", gkT, 1.0)):
                for g in range(2):
                    t_out(f"{name}.{g}", dst[:, 2 * g:2 * g + 2, :].rearrange("p a b -> p (a b)"), scale=f)
            u0 = PLAN.unit["Q1"]
            for s in range(1, 9):
                ahead(u0 + 2 * s - 1)
                act.wait_ge(gla_exp, s)
                e = arena[:, 7168:8192]
                act.activation(e, e, ACT.Exp).then_inc(ev("gla_expd"), 1)
                if s == 1:
                    evac("Q0", q[:, :, 0:COLS])
                ahead(u0 + 2 * s)
                if s in (2, 4):
                    c = s // 2
                    evac(f"Q{c}", q[:, :, COLS * c:COLS * c + COLS])
                elif s in (6, 8):
                    gate(f"G2{s // 2 - 3}")
                if s >= 5:
                    if s == 5:
                        for c in range(3):
                            b, k = PLAN.bank(f"Q{c}")
                            act.wait_ge(panel_out[b], k + 2)
                    if s >= 7:
                        act.wait_ge(ev("qq_sq"), H_MLA * (s - 6))
                    n = (s - 5) // T
                    for h in range(H_MLA):
                        g, spare = H_MLA * ((s - 5) % T) + h, (probT, prob)[(s - 5) % T]
                        src = qh[:, g, 0:NOPE] if n == 0 else qh[:, g, NOPE:]
                        act.activation(spare[:].rearrange("p a b -> p (a b)")[:, P * h:P * h + src.shape[1]], src, ACT.Square,
                                       accum_out=stat[:, 4 + n, g:g + 1]).then_inc(ev("qq_sq"), 1)
            sqrt("qq", stat[:, 4:6, :])
            for t in range(T):
                for g in range(2):
                    t_out(f"go.{2 * t + g}", og[:, t, 2 * g:2 * g + 2, :].rearrange("p a b -> p (a b)"))
            for c in range(4):
                evac(f"UKV{c}", kv[:, :, COLS * c:COLS * c + COLS])
            ahead(PLAN.unit["G10"] + 1)
            b, k = T_USE["go.3"]
            act.wait_ge(t_free[b], k + 2)
            act.wait_ge(ev("qq_sq"), 2 * T * H_MLA)
            for h in range(T * H_GLA):
                if h >= 4:
                    act.wait_ge(ev("og_sum"), h - 3)
                act.activation(og_sq[:, h % 4], og_heads[:, h], ACT.Square, accum_out=stat[:, 6, h:h + 1]).then_inc(ev("og_sum"), 1)
            ahead(PLAN.unit["G10"] + 3)
            act.activation(room, kh, ACT.Square).then_inc(ev("kk_sq"), 1)
            ahead(PLAN.unit["G11"])
            sqrt("kk", stat[:, 2, 0:16])
            sqrt("og", stat[:, 6, 0:8])
            gate("G10")
            act.wait_ge(ev("kpe_ready"), 1)
            for g in range(4):
                ahead(PLAN.unit["G11"] + g)
                t_out(f"qn.{g}", qnT[:, 2 * g:2 * g + 2, :].rearrange("p a b -> p (a b)"), scale=col("g_q_nope"))
            for g in range(2):
                t_out(f"qr.{g}", qrT[:, 2 * g:2 * g + 2, :].rearrange("p a b -> p (a b)"))
            t_out("kp", kpT, 256)
            for g in range(4):
                t_out(f"kn.{g}", knT[:, 2 * g:2 * g + 2, :].rearrange("p a b -> p (a b)"), scale=col("g_k_nope"))

            def mla_exps(i, slot, row, bank):
                for t, (first, n) in enumerate(((0, P), (P, 2 * P))):
                    ins = act.activation(prob[:, slot, first:first + n], bank[:, first:first + n], ACT.Exp,
                                         bias=soft[:, row, 2 + t:3 + t], scale=(NOPE + ROPE) ** -0.5,
                                         accum_out=soft[:, row, 4 + t:5 + t])
                return ins

            def mla_after(i):
                if i in (0, 3, 7):
                    gate(("G11", "G00", "G01")[(i + 1) // 4])

            u0 = PLAN.unit["G00"]
            attend("MLA", H_MLA, mla_exps, lambda i: u0 + max(i - 1, 0), lambda i: u0 + i + 1, 3, mla_after)

            lt_act("y", lta)
            ahead(PLAN.unit["WO1"])
            lt_act("hc", ltb, (0, 1))
            ahead(PLAN.unit["WO1"] + 1)
            lt_act("hc", ltb, (2, 3))
            ahead(PLAN.unit["CX"])
            for t in range(T):
                act.wait_ge(ev("x1_ready"), 2)
                act.activation(prob[:].rearrange("p a b -> p (a b)"), x[:, t, :], ACT.Square,
                               accum_out=stat[:, 1, t:t + 1]).then_inc(ev("h2_sum"), 1)
                act.wait_ge(ev("h2_sum"), t + 1)
            sqrt("h2", stat[:, 1, 2:4])
            ahead(PLAN.unit["CX"] + 1)
            lt_act("h2", lta, (0, 1))
            ahead(PLAN.unit["WU0"])
            lt_act("h2", lta, (2, 3))

            def up_hi_of(c, i=None):
                d = 2 * i if i is not None else 0
                for g in range(2):
                    b, k = T_USE[f"WU{c}.{g}"]
                    act.wait_ge(t_full[b], k + 1 + d)
                    ft = 4 * c + 2 * g
                    dst = ff[0][:, ft:ft + 2, :] if i is None else ff[0][:, bass.ds(8 * i + ft, 2), :]
                    act.copy(dst.rearrange("p a b -> p (a b)"), tb[b][:]).then_inc(up_hi, 1)

            def up_relu(c, i=None):
                s, _ = PLAN.bank(f"WU{c}")
                panel_wait(f"WU{c}", 8 * i if i is not None else 0)
                act.activation(up[c % 2][:], acc[s][:], ACT.Relu).then_inc(panel_out[s], 1)

            evac("WU0", up[0][:], func=ACT.Relu)
            u0 = PLAN.unit["WU1"]
            assert cursor[0] == u0 + AHEAD
            with act.Fori(0, 3) as i:
                for c in (1, 2):
                    for k in range(4):
                        split(u0 + 4 * (c - 1) + k + AHEAD, i, 8, 32)
                        if k == 1:
                            up_hi_of(c - 1, i)
                    up_relu(c, i)
            cursor[0] += 24
            ahead(PLAN.unit["WU7"] + 2)
            up_hi_of(6)
            ahead(PLAN.unit["WU7"] + 4)
            up_relu(7)
            ahead(PLAN.unit["WD0"] + 2)
            up_hi_of(7)
            ahead(PLAN.unit["IN0"] - 1)

            lt_act("x2", lta, (0, 1))
            ahead(PLAN.unit["IN0"] + 1)
            lt_act("x2", lta, (2, 3))
            ahead(PLAN.unit["IN4"])

            def gate2_sigmoid(n):
                name, c = f"IN{3 + n}", COLS * n
                s, k = PLAN.bank(name)
                ahead(last_unit(name) + 1)
                act.wait_ge(panel_out[s], k + 2)
                act.activation(gate2[:, :, c:c + COLS], gate2[:, :, c:c + COLS], ACT.Sigmoid).then_inc(gate_sig, 1)

            def gate_row_out(name):
                for g in range(2):
                    t_out(f"{name}.{g}", gate_row[:, COLS * g:COLS * g + COLS])

            def keys_out(br):
                for g in range(KVH):
                    t_out(f"{('kA', 'kB')[br]}.{g}", kT[br][:, g, :])

            def queries_out(br):
                for g in range(2):
                    t_out(f"{('qA', 'qB')[br]}.{g}", qT[br][:, 2 * g:2 * g + 2, :].rearrange("p a b -> p (a b)"))

            keys_out(0)
            queries_out(0)
            gate2_sigmoid(0)

            def ab_exps(i, slot, row, bank):
                br, h = i // (HEADS * T), i % (HEADS * T) // T
                if br == 0:
                    act.activation(soft[:, row, 6:7], GAIN["attn_sink_2"][:, h:h + 1], ACT.Exp,
                                   bias=soft[:, row, 2:3], scale=-1.0)
                return act.activation(prob[:, slot, :], bank[:], ACT.Exp, bias=soft[:, row, 2:3],
                                      scale=HD ** -0.5, accum_out=soft[:, row, 4:5])

            def ab_after(i):
                if i == 3:
                    sqrt("ab", stat[:, 2:4, :])
                elif i == AB_KEYS:
                    keys_out(1)
                elif i == AB_QUERIES:
                    queries_out(1)
                elif i == AB_OUT:
                    lt_act("oab", ltb, (0, 1))
                elif i == AB_GATE:
                    gate_row_out("gate1")
                if i in IN_DONE:
                    gate2_sigmoid(1 + IN_DONE.index(i))

            u0 = PLAN.unit["IN4"]
            attend("AB", 2 * HEADS * T, ab_exps, lambda i: u0 + ab_units(max(i - 1, 0)), lambda i: u0 + ab_units(i + 1), 4,
                   ab_after)
            lt_act("oab", ltb, (2, 3))
            ahead(PLAN.unit["OUT0"])
            lt_act("ym", lta)
            ahead(PLAN.unit["UP0"])

            def variance(name):
                act.activation(stat[:, 0, 8:9], one_col[:], ACT.Sqrt)
                for t in range(T):
                    act.wait_ge(ev(f"{name}_mean"), t + 1)
                    act.activation([prob, probT][t][:].rearrange("p a b -> p (a b)"), x[:, t, :], ACT.Square,
                                   bias=stat[:, 1, 2 + t:3 + t], accum_out=stat[:, 1, 4 + t:5 + t])\
                        .then_inc(ev(f"{name}_sum"), 1)
                sqrt(name, stat[:, 1, 4:6])

            variance("ln1")
            lt_act("x3", ltb)

            def conv_of(c, i=None):
                d, cv = i if i is not None else 0, conv[c % 2]
                act.wait_ge(ev("tap_ready"), c + 1 + 2 * d)
                act.wait_ge(conv_free, c + 1 + 2 * d)
                for j in range(4):
                    b, k = T_USE[f"UP{c}.{j // 2}"]
                    act.wait_ge(t_full[b], k + 1 + 2 * d)
                    act.activation(cv[:, j], tb[b][:, 256 * (j % 2):256 * (j % 2) + 256], ACT.Identity,
                                   bias=tap[:, 3, j:j + 1], scale=tap[:, 1, j:j + 1]).then_inc(conv_lin, 1)
                b, k = T_USE[f"UP{c}.0"]
                act.wait_ge(t_free[b], k + 2 + 2 * d)
                act.activation(sig[:], cv[:, 0:2], ACT.Sigmoid).then_inc(conv_sig, 1)

            def conv_hi(c, i=None):
                d = i if i is not None else 0
                act.wait_ge(ev("conv_prod"), c + 1 + 2 * d)
                dst = actT[0][:, 2 * c:2 * c + 2, :] if i is None else actT[0][:, bass.ds(4 * i + 2 * c, 2), :]
                act.copy(dst, conv[c % 2][:, 2:4]).then_inc(ev("conv_hi"), 1)

            def upv_out(c, i=None):
                s, _ = PLAN.bank(f"UP{c}")
                panel_wait(f"UP{c}", 8 * i if i is not None else 0)
                act.copy(upv[c % 2][:], acc[s][:]).then_inc(panel_out[s], 1)

            evac("UP0", upv[0][:])
            u0 = PLAN.unit["UP1"]
            assert cursor[0] == u0 + AHEAD
            with act.Fori(0, 5) as i:
                for c in (1, 2):
                    for k in range(4):
                        split(u0 + 4 * (c - 1) + k + AHEAD, i, 8, 64)
                        if k == 1:
                            conv_of(c - 1, i)
                    upv_out(c, i)
                    conv_hi(c - 1, i)
            cursor[0] += 40
            ahead(PLAN.unit["DN0"] + 2)
            conv_of(10)
            ahead(PLAN.unit["DN0"] + 6)
            conv_hi(10)
            ahead(PLAN.units)
            variance("ln2")

        @block.vector
        def _(dve):
            order = Order(dve, dve_order)
            done = order.done
            for s in panel_out + t_free + s_free:
                dve.sem_inc(s, 1)
            dve.sem_inc(split_ready, RING)
            dve.sem_inc(mod_free, KT // UNIT)
            dve.sem_inc(bias_used, 2)

            def split(u, i=None, per=0):
                s = u % RING
                dve.wait_ge(hi_ready, u + 1 + (per * i if i is not None else 0))
                n = PLAN.cols[u]
                dve.tensor_tensor(wlo[:, s, :, 0:n], raw[:, s, :, 0:n], whi[:, s, :, 0:n].bitcast(F32), ALU.subtract)\
                   .then_inc(split_ready, 1)

            cursor = [0]

            def ahead(pos):
                while cursor[0] < min(pos + AHEAD, PLAN.units):
                    split(cursor[0])
                    cursor[0] += 1

            def panel_wait(name):
                ahead(last_unit(name) + 1)
                dve.wait_ge(unit_used, RING + last_unit(name) + 1)
                return acc[PLAN.bank(name)[0]]

            def evacuated(name):
                s, k = PLAN.bank(name)
                dve.wait_ge(panel_out[s], k + 2)

            def frees(name, ins):
                s, k = PLAN.bank(name)
                ins.then_inc(panel_out[s], 1)
                dve.wait_ge(panel_out[s], k + 2)

            def biased(name, dst):
                p, n = panel_wait(name), n_gate[name]
                twice = (n // 2 + 1) + (1 if n % 2 == 0 and n >= n_gate["CX"] else 0)
                dve.wait_ge(bias_landed[n % 2], 16 * twice)
                frees(name, dve.tensor_tensor(dst, p[:], bias[:, n % 2].unsqueeze(1).broadcast_to([P, T, COLS]),
                                              ALU.add))
                dve.sem_inc(bias_used, 1)

            def lt_dve(name, lt, scale=None, shift=None, groups=range(4), between=None):
                def low(g):
                    dve.wait_ge(lt_hi, lt_done(name, g))
                    dve.tensor_tensor(lt[1][:, 2 * g:2 * g + 2, :].rearrange("p a b -> p (a b)"), turn[:, g % 2],
                                      lt[0][:, 2 * g:2 * g + 2, :].bitcast(F32).rearrange("p a b -> p (a b)"),
                                      ALU.subtract).then_inc(lt_ready, 1)

                for g in groups:
                    b, k = T_USE[f"{name}.{g}"]
                    if lt_done(name, g) > 2:
                        dve.wait_ge(lt_ready, lt_done(name, g) - 2)
                    dve.wait_ge(t_full[b], k + 1)
                    if scale is None:
                        ins = dve.tensor_copy(turn[:, g % 2], tb[b][:])
                    else:
                        for kk in range(2):
                            half, c = slice(256 * kk, 256 * kk + 256), 2 * g + kk
                            if shift is None:
                                ins = dve.tensor_scalar(turn[:, g % 2, half], tb[b][:, half], scale[:, c:c + 1], None,
                                                        ALU.mult)
                            else:
                                ins = dve.tensor_scalar(turn[:, g % 2, half], tb[b][:, half], scale[:, c:c + 1],
                                                        shift[:, c:c + 1], ALU.mult, ALU.add)
                    ins.then_inc(t_free[b], 1)
                    if between:
                        between(g)
                    if g > groups[0]:
                        low(g - 1)
                low(groups[-1])

            def spread(v, n):
                return v.unsqueeze(2).broadcast_to([P, v.shape[1], n])

            def squares(src, scratch, dst):
                done(dve.tensor_tensor(scratch, src, src, ALU.mult))
                done(dve.tensor_reduce(dst, scratch, AX.X, ALU.add))

            def var(view, n, eps=EPS):
                return dve.tensor_scalar(view, view, 1.0 / n, eps, ALU.mult, ALU.add)

            def inverse(name, view):
                dve.wait_ge(ev(f"{name}_std"), 1)
                done(dve.reciprocal(view, view))

            def mod_row(c):
                b, k = T_USE[f"mod.{c}"]
                dve.wait_ge(t_full[b], k + 1)
                dve.tensor_copy(modrow[:], tb[b][0:2, :]).then_inc(t_free[b], 1)
                dve.sem_inc(mod_free, 1)

            def mod_sum_tile(total, kt, c):
                w, factor = wm[:, kt // UNIT, kt % UNIT], sic[:, kt:kt + 1]
                if kt % UNIT == 0:
                    dve.wait_ge(mod_landed[kt // UNIT], 16 * (c + 1))
                if kt == 0:
                    done(dve.tensor_scalar(total, w, factor, None, ALU.mult))
                else:
                    done(dve.scalar_tensor_tensor(total, w, factor, total, ALU.mult, ALU.add))
                if kt % UNIT == UNIT - 1:
                    dve.sem_inc(mod_free, 1)
                if kt == KT - 1:
                    dve.sem_inc(mod_sum, 1)

            def mod_sums(c, pos):
                n = c - MOD_CTX
                if n >= MOD_LOOP + 2:
                    b, k = T_USE[f"mod.{c - 2}"]
                    dve.wait_ge(t_full[b], k + 1)
                for kt in range(KT):
                    if kt % UNIT == 0:
                        ahead(pos + kt // UNIT)
                    mod_sum_tile(msum[1][:, n % 2], kt, c)

            def mod_out(c):
                b, k = T_USE[f"mod.{c}" if c >= MOD_CTX else f"modt.{c}"]
                dve.wait_ge(t_full[b], k + 1)
                m = tb[b][:, 0:8].rearrange("p (j e) -> p j e", e=2)
                if c < 4:
                    done(dve.tensor_tensor(modx[:, 4 * c:4 * c + 4], m[:, :, 1], col("b_mod_2", 4 * c, 4), ALU.add))
                dve.tensor_tensor(modc[:, 4 * c:4 * c + 4], m[:, :, 0], col("b_mod_2", 4 * c, 4), ALU.add)\
                    .then_inc(t_free[b], 1)
                dve.wait_ge(t_free[b], k + 2)

            def attend(name, n, maxima, sums, weigh, at_scores, at_turn, after=None):
                def softmax(i):
                    ahead(at_scores(i))
                    g = STEPS[name][0] + i
                    b, k = S_USE[f"{name}.{i}"]
                    dve.wait_ge(s_full[b], k + 1)
                    maxima(i, soft[:, g % 4], sc[b]).then_inc(soft_ready, 1)

                softmax(0)
                for i in range(n + 1):
                    if i + 1 < n:
                        softmax(i + 1)
                    if i >= 1:
                        b, k = S_USE[f"{name}.{i - 1}"]
                        dve.wait_ge(s_free[b], k + 2)
                        sums(i - 1, soft[:, (STEPS[name][0] + i - 1) % 4])
                    ahead(at_turn(i))
                    if i >= 1:
                        b, k = T_USE[f"{name}.O{i - 1}"]
                        dve.wait_ge(t_full[b], k + 1)
                        weigh(i - 1, soft[:, (STEPS[name][0] + i - 1) % 4, 8:10], tb[b]).then_inc(t_free[b], 1)
                    if after:
                        after(i)

            def vectors(g):
                b, k = T_USE[f"vec.{g}"]
                dve.wait_ge(t_full[b], k + 1)
                if g < 2:
                    first, n = ((0, 8), (8, 88))[g]
                    done(dve.tensor_copy(vcol[:, first:first + n], tb[b][:, first:first + n]))
                else:
                    if g == 2:
                        done(dve.tensor_copy(ln1c[:], tb[b][:, 4 * FT2:4 * FT2 + 16]))
                    done(dve.tensor_copy(ccol[:, 2 * (g - 2):2 * (g - 2) + 2],
                                         tb[b][:, 0:4 * FT2].rearrange("p (a c) -> p a c", a=2)))
                dve.sem_inc(t_free[b], 1)

            vectors(0)
            lt_dve("me", ltb, col("g_mem", 0, 8), between=lambda g: ahead(g - 2))
            for name, s in (("me", 0), ("h", 1)):
                ahead(2 + s)
                dve.wait_ge(ev(f"{name}_sum"), T)
                dve.tensor_scalar(stat[:, s, 2:4], stat[:, s, 0:2], 1.0 / D, EPS, ALU.mult, ALU.add)\
                    .then_inc(ev(f"{name}_var"), 1)
            for name, s in (("me", 0), ("h", 1)):
                inverse(name, stat[:, s, 2:4])
                if name == "me":
                    dve.sem_inc(ev("me_inverse"), 1)
            for t in range(T):
                dve.tensor_scalar(work[:, t], x[:, t], stat[:, 1, 2 + t:3 + t], None, ALU.mult)\
                   .then_inc(ev("h_scaled"), 1)
            ahead(PLAN.unit["MK1"])
            vectors(1)
            dve.sem_inc(ev("vec_ready"), 1)
            ahead(PLAN.unit["MK1"] + 2)

            dve.wait_ge(ev("grid_ready"), 1)
            dve.wait_ge(ev("pos_landed"), 16)
            done(dve.tensor_copy(stat[:, 7, 6:8], stat[:, 7, 4:6].bitcast(I32)))
            done(dve.tensor_copy(stat[:, 7, 8:9], stat[:, 7, 2:3].bitcast(I32)))
            freq = ar(13568, 64)
            for t in range(T):
                for first, n, p in ((0, 32, stat[:, 7, 6 + t:7 + t]), (32, 16, stat[:, 7, t:t + 1]),
                                    (48, 16, stat[:, 7, 8:9])):
                    done(dve.tensor_scalar(angle[:, t, first:first + n], freq[:, first:first + n], p, None, ALU.mult))
            magic = 1.5 * 2.0 ** 23
            done(dve.tensor_scalar(turns, angle, float(1 / (2 * np.pi)), magic, ALU.mult, ALU.add))
            done(dve.tensor_scalar(turns, turns, magic, None, ALU.subtract))
            rest = 2 * np.pi
            for bits in (5, 14, 23, 60):
                part = float(np.float32(np.floor(rest * 2.0 ** bits) / 2.0 ** bits)) if bits < 60 else \
                    float(np.float32(rest))
                rest -= part
                done(dve.scalar_tensor_tensor(angle, turns, -part, angle, ALU.mult, ALU.add))
            pi = float(np.nextafter(np.float32(np.pi), np.float32(0)))
            done(dve.tensor_scalar(rot[:, 0], angle, pi, -pi, ALU.min, ALU.max))
            done(dve.scalar_tensor_tensor(turns, rot[:, 0], -1.0, rot[:, 0], ALU.mult, ALU.max))
            dve.tensor_scalar(rot[:, 1], turns, -1.0, float(np.pi / 2), ALU.mult, ALU.add)\
                .then_inc(ev("rot_arg"), 1)

            ahead(PLAN.unit["MK2"])
            for g in (2, 3):
                vectors(g)
            ahead(PLAN.unit["MK2"] + 2)
            lt_dve("h", lta, col("g_mix", 0, 8), groups=(0, 1))
            ahead(PLAN.unit["MK2"] + 3)
            lt_dve("h", lta, col("g_mix", 0, 8), groups=(2, 3))

            ahead(PLAN.unit["CK"])
            evacuated("AQ")
            evacuated("MK0")
            views = []
            for t in range(T):
                views.append((aq[:, t, GATE_RANK:272].rearrange("p (h c) -> p h c", c=DQ_MEM), stat[:, 2, 4 * t:4 * t + 4],
                              "g_q_mem"))
            for t in range(T):
                views.append((kvm[:, t, 0:256].rearrange("p (h c) -> p h c", c=DQ_MEM),
                              stat[:, 2, 8 + 4 * t:12 + 4 * t], "g_k_mem"))
            b, k = T_USE["h.3"]
            dve.wait_ge(t_full[b], k + 1)
            scratch = work[:, 0, 0:256].rearrange("p (h c) -> p h c", c=DQ_MEM)
            for v, s, _ in views:
                squares(v, scratch, s)
            var(stat[:, 2, :], DQ_MEM).then_inc(ev("mm_var"), 1)
            ahead(PLAN.unit["GQ"])
            evacuated("CK")
            for t in range(T):
                squares(ck[:, t:t + 1, 0:256], work[:, t:t + 1, 0:256], stat[:, 3, t:t + 1])
                squares(ck[:, t:t + 1, 256:320], work[:, t:t + 1, 0:64], stat[:, 3, 2 + t:3 + t])
            done(var(stat[:, 3, 0:2], KV_RANK))
            var(stat[:, 3, 2:4], ROPE).then_inc(ev("ck_var"), 1)

            done(dve.memset(zflag, 1.0))
            done(dve.memset(zflag[:, :, 0:1], 0.0))
            ahead(PLAN.unit["GK"])
            for g in range(2):
                b, k = T_USE[f"z.{g}"]
                dve.wait_ge(t_full[b], k + 1)
                for j in range(2):
                    ins = dve.tensor_scalar(zb[:, 2 * g + j, :], tb[b][:, 256 * j:256 * j + 256],
                                            col("b_gla_gate", 2 * g + j), None, ALU.add)
                ins.then_inc(t_free[b], 1)
                dve.wait_ge(t_free[b], k + 2)
            dve.sem_inc(ev("zb_ready"), 1)
            ahead(PLAN.unit["GK"] + 1)
            inverse("mm", stat[:, 2, :])
            dve.wait_ge(ev("gains_landed"), 16 * len(GAIN))
            for i, (v, s, gain) in enumerate(views):
                done(dve.tensor_tensor(v, v, spread(s, DQ_MEM), ALU.mult))
                done(dve.tensor_tensor(v, v, GAIN[gain].unsqueeze(1).broadcast_to([P, H_MEM, DQ_MEM]), ALU.mult))
                if i % 2 == 1:
                    ahead(PLAN.unit["GK"] + 2 + i // 2)
                    dve.sem_inc(ev(("mqT_normed", "mkT_normed")[i // 2]), 1)
            ahead(PLAN.unit["V0"])
            dve.wait_ge(ev("zln_ready"), 1)
            done(dve.scalar_tensor_tensor(zb, zb, 0.0, ze, ALU.min, ALU.subtract))
            done(dve.tensor_scalar(zb, zb, 1.0 / 16.0, None, ALU.mult))
            done(dve.tensor_tensor_scan(arena[:, 6144:7168], arena[:, 13312:14336], arena[:, 11264:12288], 0.0,
                                        ALU.mult, ALU.add))
            ahead(PLAN.unit["V0"] + 1)
            inverse("ck", stat[:, 3, 0:4])
            for t in range(T):
                done(dve.tensor_scalar(ck[:, t, 0:256], ck[:, t, 0:256], stat[:, 3, t:t + 1], None, ALU.mult))
            dve.sem_inc(ev("ck_normed"), 1)
            ahead(PLAN.unit["V1"])
            b, k = T_USE["ck"]
            dve.wait_ge(t_full[b], k + 1)
            for kk in range(2):
                ins = dve.tensor_scalar(turn[:, 0, 256 * kk:256 * kk + 256], tb[b][:, 256 * kk:256 * kk + 256],
                                        col("g_ckv", kk), None, ALU.mult)
            ins.then_inc(t_free[b], 1)
            dve.wait_ge(t_free[b], k + 2)
            dve.sem_inc(ev("ck_turned"), 1)
            dve.wait_ge(ev("ckT_hi"), 1)
            dve.tensor_tensor(ckT[1][:].rearrange("p a b -> p (a b)"), turn[:, 0],
                              ckT[0][:].bitcast(F32).rearrange("p a b -> p (a b)"), ALU.subtract)\
                .then_inc(ev("ckT_ready"), 1)
            dve.wait_ge(ev("ckT_ready"), 1)

            def neg(s, n, scale):
                return dve.tensor_scalar(s[:, 2:2 + n], s[:, 0:n], -scale, None, ALU.mult)

            def mem_maxima(i, s, bank):
                done(dve.tensor_reduce(s[:, 0:2], bank[:].rearrange("p (t k) -> p t k", t=T), AX.X, ALU.max))
                return neg(s, 2, DQ_MEM ** -0.5)

            def sums2(i, s):
                done(dve.reciprocal(s[:, 8:10], s[:, 4:6]))

            def weigh2(dst, bank, r, n):
                return dve.tensor_tensor(dst, bank[:, 0:T * n].rearrange("p (t c) -> p t c", t=T), spread(r, n), ALU.mult)

            def mem_after(i):
                if 1 <= i < 3:
                    name, c = f"R{i - 1}", COLS * (i - 1)
                    p = panel_wait(name)
                    dve.wait_ge(ev("r_sig"), i)
                    v = r_gla[:, :, c:c + COLS]
                    frees(name, dve.tensor_tensor(v, p[:], rsig, ALU.mult))
                    for t in range(T):
                        g = v[:, t].rearrange("p (h c) -> p h c", c=DV_GLA)
                        done(dve.tensor_tensor(g, g, GAIN["g_gla_out"].unsqueeze(1).broadcast_to([P, 2, DV_GLA]), ALU.mult))
                    if i == 1:
                        dve.wait_ge(ev("c_sig"), 1)
                        done(dve.tensor_tensor(sic[:], sic[:], vcol[:, ROWS["c_2"][0]:ROWS["c_2"][0] + 16], ALU.mult))
                        dve.sem_inc(ev("sic_ready"), 1)

            def gate_in_psum(name):
                p, n = panel_wait(name), n_gate[name]
                dve.wait_ge(bias_landed[n % 2], 16 * (n // 2 + 1))
                dve.tensor_tensor(p[:], p[:], bias[:, n % 2].unsqueeze(1).broadcast_to([P, T, COLS]), ALU.add)\
                   .then_inc(gate_in, 1)
                dve.wait_ge(gate_in, n + 1)
                dve.sem_inc(bias_used, 1)

            def gate_on(name, branch):
                dve.wait_ge(gate_sig, n_gate[name] + 1)
                part = slice(COLS * int(name[2]), COLS * int(name[2]) + COLS)
                frees(name, dve.tensor_tensor(branch[:, :, part], branch[:, :, part], acc[PLAN.bank(name)[0]][:], ALU.mult))

            u0 = PLAN.unit["V1"]
            attend("MEM", H_MEM, mem_maxima, sums2,
                   lambda i, r, bank: weigh2(o_mem[:, :, DV_MEM * i:DV_MEM * i + DV_MEM], bank, r, DV_MEM),
                   lambda i: u0 + 4 * max(i - 1, 0), lambda i: u0 + min(4 * i + 2, 14), mem_after)

            u0 = PLAN.unit["Q1"]
            done(dve.memset(attn, 0.0))
            dve.wait_ge(ev("gmask_ready"), 1)

            def halves(v, w):
                return v.rearrange("p h (m e w) -> p (h m) e w", e=2, w=w)

            def exponents(s):
                if s == 1:
                    e = eq.rearrange("p (h c) -> p h c", h=H_GLA), ek.rearrange("p (h c) -> p h c", h=H_GLA)
                    done(dve.tensor_copy(e[0], decay[:, :, P:2 * P]))
                    ins = dve.tensor_tensor(e[1], decay[:, :, P - 1:P].broadcast_to([P, H_GLA, P]), decay[:, :, 0:P],
                                            ALU.subtract)
                else:
                    w = P >> (s - 1)
                    d = halves(decay, w)
                    ref = d[:, :, 0, w - 1:w].broadcast_to([P, d.shape[1], w])
                    done(dve.tensor_tensor(eq.rearrange("p (m w) -> p m w", w=w), d[:, :, 1, :], ref, ALU.subtract))
                    ins = dve.tensor_tensor(ek.rearrange("p (m w) -> p m w", w=w), ref, d[:, :, 0, :], ALU.subtract)
                ins.then_inc(gla_exp, 1)

            def decayed(s):
                if s >= 2:
                    b, k = S_USE["gla.off" if s == 2 else f"gla.{s - 2}.1"]
                    dve.wait_ge(s_full[b], k + 1)
                dve.wait_ge(ev("gla_expd"), s)
                if s == 1:
                    done(dve.tensor_tensor(gqd[:, :, P:2 * P], gqT[:, :, P:2 * P],
                                           eq.rearrange("p (h c) -> p h c", h=H_GLA), ALU.mult))
                    ins = dve.tensor_tensor(gkd[:, :, 0:P], gkT[:, :, 0:P],
                                            ek.rearrange("p (h c) -> p h c", h=H_GLA), ALU.mult)
                else:
                    w = P >> (s - 1)
                    done(dve.tensor_tensor(halves(gqd, w)[:, :, 1, :], halves(gqT, w)[:, :, 1, :],
                                           eq.rearrange("p (m w) -> p m w", w=w), ALU.mult))
                    ins = dve.tensor_tensor(halves(gkd, w)[:, :, 0, :], halves(gkT, w)[:, :, 0, :],
                                            ek.rearrange("p (m w) -> p m w", w=w), ALU.mult)
                ins.then_inc(gla_in, 1)
                dve.wait_ge(gla_in, s)

            def weights(s):
                if s == 1:
                    b, k = S_USE["gla.off"]
                    dve.wait_ge(s_full[b], k + 1)
                    dve.tensor_copy(attn[:, 2], sc[b][:].rearrange("p (h c) -> p h c", h=H_GLA)).then_inc(s_free[b], 1)
                    return
                mask = ident[:].bitcast(I32) if s == 0 else gmask[:, s - 2, :]
                for t in range(T):
                    b, k = S_USE[f"gla.{max(s - 1, 0)}.{t}"]
                    dve.wait_ge(s_full[b], k + 1)
                    dve.copy_predicated(attn[:, t], mask.unsqueeze(1).broadcast_to([P, H_GLA, P]),
                                        sc[b][:].rearrange("p (h c) -> p h c", h=H_GLA)).then_inc(s_free[b], 1)
                    dve.wait_ge(s_free[b], k + 2)

            exponents(1)
            for g in ("gqT.0", "gqT.1", "gkT.0", "gkT.1"):
                b, k = T_USE[g]
                dve.wait_ge(t_free[b], k + 2)
            for s in range(1, 9):
                ahead(u0 + 2 * s - 1)
                decayed(s)
                weights(s - 1)
                if s < 8:
                    exponents(s + 1)
                ahead(u0 + 2 * s)
                if s in (6, 8):
                    gate_in_psum(f"G2{s // 2 - 3}")
                if s == 7:
                    gate_on("G20", o_mem)
                if s % 2 == 0:
                    mod_row(s // 2 - 1)
                elif s >= 3:
                    mod_out(s // 2 - 1)
            mod_out(3)
            weights(8)
            dve.wait_ge(ev("qq_sq"), 2 * T * H_MLA)
            done(var(stat[:, 4, :], NOPE))
            var(stat[:, 5, :], ROPE).then_inc(ev("qq_var"), 1)
            gate_on("G21", o_mem)
            for v in (modc[:, 8:16], modx[:, 8:16]):
                done(dve.tensor_scalar(v, v, 1.0, None, ALU.add))

            inverse("qq", stat[:, 4:6, :])
            dve.sem_inc(ev("qq_inverse"), 1)
            done(dve.tensor_tensor(qh[:, :, 0:NOPE], qh[:, :, 0:NOPE], spread(stat[:, 4, :], NOPE), ALU.mult))
            dve.sem_inc(ev("qn_normed"), 1)
            ahead(PLAN.unit["G10"] + 3)
            dve.wait_ge(ev("kk_sq"), 1)
            done(dve.tensor_reduce(stat[:, 2, :], room, AX.X, ALU.add))
            var(stat[:, 2, :], NOPE).then_inc(ev("kk_var"), 1)
            dve.wait_ge(ev("og_sum"), T * H_GLA)
            var(stat[:, 6, 0:8], DV_GLA).then_inc(ev("og_var"), 1)
            ahead(PLAN.unit["G11"])
            inverse("kk", stat[:, 2, :])
            done(dve.tensor_tensor(kh, kh, spread(stat[:, 2, :], NOPE), ALU.mult))
            dve.sem_inc(ev("k_normed"), 1)
            gate_in_psum("G10")
            ahead(PLAN.unit["G11"] + 1)
            inverse("og", stat[:, 6, 0:8])
            for t in range(T):
                for h in range(H_GLA):
                    v = r_gla[:, t, DV_GLA * h:DV_GLA * h + DV_GLA]
                    ins = dve.scalar_tensor_tensor(v, og[:, t, h], stat[:, 6, 4 * t + h:4 * t + h + 1], v, ALU.mult, ALU.mult)
            done(ins)
            gate_on("G10", r_gla)

            dve.wait_ge(ev("keeps_ready"), 1)

            def mla_maxima(i, s, bank):
                diagonal = bank[:].rearrange("p (a b) -> p a b", b=256)[:, :, 0:P]
                done(dve.tensor_tensor(diagonal, diagonal, keep_past[:].unsqueeze(1).broadcast_to([P, 2, P]), ALU.add))
                done(dve.tensor_reduce(s[:, 0:1], bank[:, 0:P], AX.X, ALU.max))
                done(dve.tensor_reduce(s[:, 1:2], bank[:, P:3 * P], AX.X, ALU.max))
                return neg(s, 2, (NOPE + ROPE) ** -0.5)

            def mla_after(i):
                if i in (0, 3, 7):
                    gate_in_psum(("G11", "G00", "G01")[(i + 1) // 4])
                if i == 1:
                    gate_on("G11", r_gla)
                    done(dve.tensor_tensor(r_gla, r_gla, o_mem, ALU.add))
                elif i == 5:
                    mix(0)

            def mix(c):
                part, half = slice(COLS * c, COLS * c + COLS), H_MLA // 2
                for h in (half * (c + 1) - 2, half * (c + 1) - 1):
                    b, k = T_USE[f"MLA.O{h}"]
                    dve.wait_ge(t_free[b], k + 2)
                gate_on(f"G0{c}", o_mla)
                done(dve.tensor_tensor(r_gla[:, :, part], r_gla[:, :, part], o_mla[:, :, part], ALU.add))
                dve.sem_inc(ev("branches_mixed"), 1)

            u0 = PLAN.unit["G00"]
            attend("MLA", H_MLA, mla_maxima, sums2,
                   lambda i, r, bank: weigh2(o_mla[:, :, V_MLA * i:V_MLA * i + V_MLA], bank, r, V_MLA),
                   lambda i: u0 + max(i - 1, 0), lambda i: u0 + min(i + 1, 8), mla_after)
            lt_dve("y", lta, groups=(0, 1))
            mix(1)
            lt_dve("y", lta, groups=(2, 3))
            for c in range(2):
                name, part = f"WO{c}", slice(COLS * c, COLS * c + COLS)
                p = panel_wait(name)
                frees(name, dve.tensor_tensor(x[:, :, part], x[:, :, part], p[:], ALU.add))
                dve.sem_inc(ev("x1_ready"), 1)
                if c == 0:
                    lt_dve("hc", ltb, modx[:, 8:16], modx[:, 0:8], (0, 1))
                    ahead(PLAN.unit["WO1"] + 1)
                    lt_dve("hc", ltb, modx[:, 8:16], modx[:, 0:8], (2, 3))
            dve.wait_ge(ev("h2_sum"), T)
            dve.tensor_scalar(stat[:, 1, 2:4], stat[:, 1, 0:2], 1.0 / D, EPS, ALU.mult, ALU.add)\
                .then_inc(ev("h2_var"), 1)
            inverse("h2", stat[:, 1, 2:4])
            for t in range(T):
                dve.tensor_scalar(work[:, t], x[:, t], stat[:, 1, 2 + t:3 + t], None, ALU.mult)\
                   .then_inc(ev("h2_scaled"), 1)
            ahead(PLAN.unit["CX"] + 1)
            lt_dve("h2", lta, col("g_ffn", 0, 8), groups=(0, 1))
            biased("CX", kvx[:])
            lt_dve("h2", lta, col("g_ffn", 0, 8), groups=(2, 3))

            def up_square(c, i=None):
                s, k = PLAN.bank(f"WU{c}")
                dve.wait_ge(panel_out[s], k + 2 + (i if i is not None else 0))
                dve.tensor_tensor(up[c % 2][:], up[c % 2][:], up[c % 2][:], ALU.mult).then_inc(up_done, 1)

            def up_lo(c, i=None):
                for g in range(2):
                    b, _ = T_USE[f"WU{c}.{g}"]
                    ft = 4 * c + 2 * g
                    dve.wait_ge(up_hi, 2 * c + g + 1 + (4 * i if i is not None else 0))
                    hi, lo = (v[:, ft:ft + 2, :] if i is None else v[:, bass.ds(8 * i + ft, 2), :] for v in ff)
                    dve.tensor_tensor(lo.rearrange("p a b -> p (a b)"), tb[b][:],
                                      hi.bitcast(F32).rearrange("p a b -> p (a b)"), ALU.subtract)\
                        .then_inc(t_free[b], 1)

            ahead(PLAN.unit["WU1"])
            up_square(0)
            u0 = PLAN.unit["WU1"]
            assert cursor[0] == u0 + AHEAD
            with dve.Fori(0, MOD_LOOP) as i:
                order.enter(i, KT)
                for c in (1, 2):
                    for k in range(4):
                        split(u0 + 4 * (c - 1) + k + AHEAD, i, 8)
                        mod_sum_tile(msum[0][:, bass.ds(i, 1), :].rearrange("p a c -> p (a c)"), 4 * (c - 1) + k, i + MOD_CTX)
                        if k == 1:
                            up_lo(c - 1, i)
                    up_square(c, i)
                order.leave(MOD_LOOP)
            cursor[0] += 24
            ahead(PLAN.unit["WU7"] + 2)
            up_lo(6)
            ahead(PLAN.unit["WU7"] + 4)
            up_square(7)
            ahead(PLAN.unit["WD0"] + 2)
            up_lo(7)
            for c in range(2):
                if c == 0:
                    for n in range(MOD_LOOP):
                        ahead(PLAN.unit["WD0"] + MOD_UNIT + n)
                        mod_out(MOD_CTX + n)
                for n in (range(2), range(2, 5))[c]:
                    mod_sums(MOD_CTX + MOD_LOOP + n, PLAN.unit["WD0"] + MOD_DOWN[n])
                    if n > 0:
                        ahead(PLAN.unit["WD0"] + MOD_TURN[n - 1])
                        mod_out(MOD_CTX + MOD_LOOP + n - 1)
                if c == 1:
                    ahead(PLAN.unit["IN0"] - 1)
                    mod_out(6 * D // COLS - 1)
                    lt_dve("x2", lta, modc[:, 8:16], modc[:, 0:8], (0, 1))
                name, part = f"WD{c}", slice(COLS * c, COLS * c + COLS)
                p = panel_wait(name)
                frees(name, dve.tensor_tensor(x[:, :, part], x[:, :, part], p[:], ALU.add))

            ahead(PLAN.unit["IN0"] + 1)
            lt_dve("x2", lta, modc[:, 8:16], modc[:, 0:8], (2, 3))
            for c in range(3):
                biased(f"IN{c}", qkv[:, :, COLS * c:COLS * c + COLS])
                if c == 0:
                    for t in range(T):
                        ahead(PLAN.unit["IN1"] + t)
                        queries(dve, done, 0, t)
                    dve.sem_inc(ev("qA_normed"), 1)
                elif c == 1:
                    keys(dve, done, 0)

            def norm_sums(t):
                for v, s, _, square in normed(t):
                    done(dve.tensor_reduce(s, square, AX.X, ALU.add))

            biased("IN3", gate2[:, :, 0:COLS])

            def diagonals(name, first):
                for j in range(KT):
                    ins = dve.tensor_scalar(diag[:, j, :], ident[:], modc[:, first + j:first + j + 1], None, ALU.mult)
                done(ins)
                dve.sem_inc(ev(f"{name}_diag"), 1)

            diagonals("gate1", 16)
            done(dve.memset(stat[:, 3, :], 1.0))
            done(dve.scalar_tensor_tensor(x3c[:, 0:8], modc[:, 32:40], 1.0, ln1c[:, 0:8], ALU.add, ALU.mult))
            done(dve.scalar_tensor_tensor(x3c[:, 8:16], modc[:, 32:40], 1.0, ln1c[:, 8:16], ALU.add, ALU.mult))
            done(dve.tensor_tensor(x3c[:, 8:16], x3c[:, 8:16], modc[:, 24:32], ALU.add))
            done(dve.tensor_scalar(GAIN["attn_sink_2"], GAIN["attn_sink_2"], -1.0, None, ALU.mult))

            def ab_step(i):
                return i // (HEADS * T), i % (HEADS * T) // T, i % T

            def ab_maxima(i, s, bank):
                br, h, t = ab_step(i)
                if br == 0:
                    far = bank[:, P * (1 - t):P * (1 - t) + P]
                    done(dve.tensor_tensor(far, far, (keep_past if t == 0 else keep_next)[:], ALU.add))
                done(dve.tensor_reduce(s[:, 0:1], bank[:], AX.X, ALU.max))
                if br == 0:
                    return dve.tensor_scalar(s[:, 2:3], s[:, 0:1], -HD ** -0.5, GAIN["attn_sink_2"][:, h:h + 1],
                                             ALU.mult, ALU.min)
                return neg(s, 1, HD ** -0.5)

            def ab_sums(i, s):
                if ab_step(i)[0] == 0:
                    done(dve.tensor_tensor(s[:, 4:5], s[:, 4:5], s[:, 6:7], ALU.add))
                done(dve.reciprocal(s[:, 8:9], s[:, 4:5]))

            def ab_weigh(i, r, bank):
                br, h, t = ab_step(i)
                c = 512 * br + HD * h
                return dve.tensor_scalar(oab[:, t, c:c + HD], bank[:, 0:HD], r[:, 0:1], None, ALU.mult)

            def ab_after(i):
                if i < T:
                    dve.wait_ge(ev("ab_sq"), i + 1)
                    norm_sums(i)
                    if i == T - 1:
                        var(stat[:, 2:4, :], HD).then_inc(ev("ab_var"), 1)
                elif i == 4:
                    inverse("ab", stat[:, 2:4, :])
                    dve.sem_inc(ev("ab_inverse"), 1)
                elif i == 15:
                    dve.wait_ge(ev("qB_normed"), 1)
                elif i == AB_OUT:
                    lt_dve("oab", ltb, groups=(0, 1))
                if i == AB_QUERIES + 2:
                    diagonals("gate2", 40)
                if i in IN_DONE:
                    c = IN_DONE.index(i) + 1
                    biased(f"IN{3 + c}", gate2[:, :, COLS * c:COLS * c + COLS])
                if i == BA_DONE:
                    merge(0, 0)

            def merge(br, c):
                name, part = f"B{'AB'[br]}{c}", slice(COLS * c, COLS * c + COLS)
                p = panel_wait(name)
                dve.wait_ge(gate_sig, 6 + 2 * br + 2)
                g = gate2[:, :, D * br + COLS * c:D * br + COLS * c + COLS]
                if br == 0:
                    frees(name, dve.tensor_tensor(ym[:, :, part], p[:], g, ALU.mult))
                else:
                    for e in range(2):
                        half = slice(256 * e, 256 * e + 256)
                        ins = dve.tensor_tensor(g[:, :, half], p[:, :, half], g[:, :, half], ALU.mult)
                        done(ins) if e == 0 else frees(name, ins)
                        y = ym[:, :, part][:, :, half]
                        done(dve.tensor_tensor(y, y, g[:, :, half], ALU.add))
                        dve.sem_inc(ev("ym_ready"), 1)

            u0 = PLAN.unit["IN4"]
            attend("AB", 2 * HEADS * T, ab_maxima, ab_sums, ab_weigh, lambda i: u0 + ab_units(max(i - 1, 0)),
                   lambda i: u0 + ab_units(i + 1), ab_after)
            lt_dve("oab", ltb, groups=(2, 3))
            merge(0, 1)
            for c in range(2):
                merge(1, c)
                lt_dve("ym", lta, groups=(2 * c, 2 * c + 1))

            def layer_norm_sums(name, src):
                for g in range(2):
                    part = slice(COLS * g, COLS * g + COLS)
                    p = panel_wait(f"{src}{g}")
                    b, k = T_USE[f"{name[0]}.{g}"]
                    dve.wait_ge(t_free[b], k + 2)
                    for t in range(T):
                        ins = dve.tensor_tensor(work[:, t, part], p[:, t], gate_row[:, part], ALU.mult)
                        if t == T - 1:
                            frees(f"{src}{g}", ins)
                        else:
                            done(ins)
                        done(dve.scalar_tensor_tensor(x[:, t, part], x[:, t, part], ALPHA, work[:, t, part], ALU.mult,
                                                      ALU.add, accum_out=stat[:, 1, 8 + 2 * g + t:9 + 2 * g + t]))
                        if g == 1:
                            dve.tensor_scalar(stat[:, 1, 2 + t:3 + t], stat[:, 1, 8 + t:9 + t], stat[:, 1, 10 + t:11 + t],
                                              -1.0 / D, ALU.add, ALU.mult).then_inc(ev(f"{name[1]}_mean"), 1)
                dve.wait_ge(ev(f"{name[1]}_mean"), T)

            def layer_norm_var(name):
                dve.wait_ge(ev(f"{name}_sum"), T)
                var(stat[:, 1, 4:6], D, LN_EPS).then_inc(ev(f"{name}_var"), 1)

            layer_norm_sums(("gate1", "ln1"), "OUT")
            for g in range(2):
                b, k = T_USE[f"gate2.{g}"]
                dve.wait_ge(t_full[b], k + 1)
                dve.tensor_copy(gate_row[:, COLS * g:COLS * g + COLS], tb[b][:]).then_inc(t_free[b], 1)
            layer_norm_var("ln1")
            inverse("ln1", stat[:, 1, 4:6])
            for half in (slice(0, COLS), slice(COLS, D)):
                for t in range(T):
                    ins = dve.tensor_scalar(x[:, t, half], x[:, t, half], stat[:, 1, 2 + t:3 + t], stat[:, 1, 4 + t:5 + t],
                                            ALU.add, ALU.mult)
                ins.then_inc(ev("x3_ready"), 1)
            lt_dve("x3", ltb, x3c[:, 0:8], x3c[:, 8:16])

            def taps(c, i=None):
                v = ccol[:].rearrange("p v (g f) -> p v g f", g=2)
                v = v[:, :, :, 2 * c:2 * c + 2] if i is None else v[:, :, :, bass.ds(4 * i + 2 * c, 2)]
                dve.tensor_copy(tap[:].rearrange("p v (g f) -> p v g f", g=2), v).then_inc(ev("tap_ready"), 1)

            def conv_taps(c, i=None):
                d, cv = i if i is not None else 0, conv[c % 2]
                for pair in range(2):
                    b, _ = T_USE[f"UP{c}.{pair}"]
                    dve.wait_ge(conv_lin, 4 * c + 2 * pair + 2 + 8 * d)
                    for v, to, of in ((0, slice(1, SEQ), slice(0, SEQ - 1)), (2, slice(0, SEQ - 1), slice(1, SEQ))):
                        for e in range(2):
                            j = 2 * pair + e
                            ins = dve.scalar_tensor_tensor(cv[:, j, to], tb[b][:, 256 * e:256 * e + 256][:, of],
                                                           tap[:, v, j:j + 1], cv[:, j, to], ALU.mult, ALU.add)
                        done(ins)
                    dve.sem_inc(t_free[b], 1)
                dve.sem_inc(ev("conv_sums"), 1)

            ahead(PLAN.unit["UP1"])
            u0 = PLAN.unit["UP1"]
            assert cursor[0] == u0 + AHEAD
            with dve.Fori(0, 5) as i:
                order.enter(i, 8)
                for c in (1, 2):
                    taps(c - 1, i)
                    for k in range(4):
                        split(u0 + 4 * (c - 1) + k + AHEAD, i, 8)
                        if k == 1:
                            conv_taps(c - 1, i)
                order.leave(5)
            cursor[0] += 40
            taps(10)
            ahead(PLAN.unit["DN0"] + 2)
            conv_taps(10)
            ahead(PLAN.units)
            dve.wait_ge(ev("x3_residual"), 1)
            layer_norm_sums(("gate2", "ln2"), "DN")
            dve.wait_ge(ev("ln2_landed"), 32)
            for t in range(T):
                done(dve.scalar_tensor_tensor(work[:, t, :], x[:, t, :], stat[:, 1, 2 + t:3 + t], lnrow[:, 0], ALU.add,
                                              ALU.mult))
                if t == 0:
                    layer_norm_var("ln2")
            inverse("ln2", stat[:, 1, 4:6])
            for t in range(T):
                dve.scalar_tensor_tensor(x[:, t, :], work[:, t, :], stat[:, 1, 4 + t:5 + t], lnrow[:, 1], ALU.mult, ALU.add)\
                   .then_inc(ev("y_ready"), 1)


_INS = ["x", "mem", "positions", "g_mix", "w_in", "b_gate", "g_ckv", "w_ukv", "g_q_nope", "g_k_nope", "g_q_rope",
        "g_k_rope", "w_gla_gate", "b_gla_gate", "g_gla_out", "g_mem", "w_mem_kv", "g_q_mem", "g_k_mem", "w_o", "g_ffn",
        "w_up", "w_down", "c_2", "ctx_2", "c_ctx_2", "w_mod_2", "b_mod_2", "w_in_2", "b_in_2", "attn_sink_2",
        "q_norm_g_2", "k_norm_g_2", "w_branch_a_2", "w_branch_b_2", "w_out_2", "ln1_g_2", "ln1_b_2", "w_up_2",
        "conv_w_2", "conv_b_2", "w_down_2", "ln2_g_2", "ln2_b_2"]


def build(nc, shapes):
    views = {}
    for name in _INS:
        shape, dt = shapes[name]
        v = nc.dram_tensor(f"in_{name}", shape, dt, kind="ExternalInput").ap()
        views[name] = v[0] if len(shape) > 1 and shape[0] == 1 else v
    out = nc.dram_tensor("out", (1, SEQ, D), F32, kind="ExternalOutput").ap()
    hybrid_kernel(nc, views, out[0])


def kernel(**inputs):
    import concourse.bacc as bacc
    from concourse.bass_utils import run_bass_kernel_spmd

    nc = bacc.Bacc("TRN2", target_bir_lowering=False, num_devices=1)
    arrays = {f"in_{name}": np.ascontiguousarray(inputs[name]) for name in _INS}
    build(nc, {name: (arrays[f"in_{name}"].shape, mybir.dt.from_np(arrays[f"in_{name}"].dtype)) for name in _INS})
    r = run_bass_kernel_spmd(nc, [arrays], core_ids=[0])
    return r.results[0]["out"]
```
